# Optimizing a Trainium2 kernel written in Bass

```python
import jax, jax.numpy as jnp
from jax import lax
import numpy as np

D_MODEL = 1024
BATCH = 1
SEQ = 256
DEPTH = 2

N_MIXERS = 2
N_POOL_GROUPS = 4
POOL_GROUP = D_MODEL // N_POOL_GROUPS
POOL_WINDOWS = (2, 4, 8, 16)
N_HEADS = 16
QK_NOPE = 64
QK_ROPE = 32
V_HEAD = 64
Q_LORA = D_MODEL // 4
KV_LORA = D_MODEL // 8
ROPE_THETA = 10000.0
D_FF = 11 * D_MODEL // 4
Q_BLOCK = 128
EPS = 1e-6
N_MOD = 9
N_POOL_LAYERS = (DEPTH + 1) // 2
N_MLA_LAYERS = DEPTH // 2
ATTN_SCALE = (QK_NOPE + QK_ROPE) ** -0.5


def rmsnorm(x, g):
    xf = x.astype(jnp.float32)
    y = xf * lax.rsqrt(jnp.mean(xf * xf, axis=-1, keepdims=True) + EPS)
    return (y * g.astype(jnp.float32)).astype(x.dtype)

def swiglu(h, w_in, w_out):
    gate, up = jnp.split(h @ w_in, 2, axis=-1)
    return (jax.nn.silu(gate) * up) @ w_out

def centred_mean(x, window):
    s = x.shape[1]
    cs = lax.cumsum(x.astype(jnp.float32), axis=1)
    cs = jnp.pad(cs, ((0, 0), (1, 0), (0, 0)))
    t = jnp.arange(s)
    hi = jnp.clip(t + window // 2, 0, s)
    lo = jnp.clip(t - window // 2, 0, s)
    tot = jnp.take(cs, hi, axis=1) - jnp.take(cs, lo, axis=1)
    cnt = (hi - lo).astype(jnp.float32)[None, :, None]
    return (tot / cnt).astype(x.dtype)

def pool_mixer(h, w, b, scale):
    B, S, _ = h.shape
    hg = h.reshape(B, S, N_POOL_GROUPS, POOL_GROUP)
    pooled = jnp.stack([centred_mean(hg[:, :, g], POOL_WINDOWS[g]) for g in range(N_POOL_GROUPS)], axis=2)
    y = jnp.einsum('bsgc,gcd->bsgd', pooled - hg, w) + b
    return y.reshape(B, S, D_MODEL) * scale

def rope_tables(s, dtype):
    inv = 1.0 / (ROPE_THETA ** (jnp.arange(0, QK_ROPE, 2, dtype=jnp.float32) / QK_ROPE))
    ang = jnp.arange(s, dtype=jnp.float32)[:, None] * inv[None, :]
    return jnp.cos(ang).astype(dtype), jnp.sin(ang).astype(dtype)

def apply_rope(x, cos, sin):
    x1, x2 = jnp.split(x, 2, axis=-1)
    return jnp.concatenate([x1 * cos - x2 * sin, x2 * cos + x1 * sin], axis=-1)

def mla_mixer(h, w_in, q_norm, kv_norm, w_uq, w_uk, w_uv, w_o, cos, sin):
    B, S, _ = h.shape
    lat = h @ w_in
    c_q, c_kv, k_r = jnp.split(lat, [Q_LORA, Q_LORA + KV_LORA], axis=-1)
    c_q = rmsnorm(c_q, q_norm)
    c_kv = rmsnorm(c_kv, kv_norm)
    q = jnp.einsum('bsc,chd->bshd', c_q, w_uq)
    q_nope, q_rope = q[..., :QK_NOPE], q[..., QK_NOPE:]
    q_rope = apply_rope(q_rope, cos[:, None, :], sin[:, None, :]) * ATTN_SCALE
    k_rope = apply_rope(k_r, cos, sin)
    q_lat = jnp.einsum('bshn,chn->bshc', q_nope, w_uk) * ATTN_SCALE
    nb = S // Q_BLOCK
    qlb = q_lat.reshape(B, nb, Q_BLOCK, N_HEADS, KV_LORA).transpose(1, 0, 2, 3, 4)
    qrb = q_rope.reshape(B, nb, Q_BLOCK, N_HEADS, QK_ROPE).transpose(1, 0, 2, 3, 4)

    def block(args):
        ql, qr = args
        s = (jnp.einsum('bqhc,bkc->bhqk', ql, c_kv)
             + jnp.einsum('bqhr,bkr->bhqk', qr, k_rope))
        p = jax.nn.softmax(s.astype(jnp.float32), axis=-1).astype(c_kv.dtype)
        return jnp.einsum('bhqk,bkc->bqhc', p, c_kv)

    o_lat = lax.map(block, (qlb, qrb))
    o_lat = o_lat.transpose(1, 0, 2, 3, 4).reshape(B, S, N_HEADS, KV_LORA)
    o = jnp.einsum('bshc,chv->bshv', o_lat, w_uv)
    return o.reshape(B, S, N_HEADS * V_HEAD) @ w_o

def modulated_sublayer(x, mod, g_pre, g_post, fn, weight):
    shift, scale, gate = mod[:, 0], mod[:, 1], mod[:, 2]
    h = rmsnorm(x, g_pre) * (1.0 + scale) + shift
    y = rmsnorm(fn(h), g_post)
    return x + weight * (1.0 + gate) * y

def first_inputs(seed: int = 0) -> dict:
    key = jax.random.key(seed)
    ks = jax.random.split(key, 20)
    n = jax.random.normal
    f32 = jnp.float32
    return {
        "x": n(ks[0], (BATCH, SEQ, D_MODEL), f32),
        "c": n(ks[1], (BATCH, D_MODEL), f32),
        "ada_w": n(ks[2], (DEPTH, D_MODEL, N_MOD * D_MODEL), f32) * (0.5 * D_MODEL ** -0.5),
        "ada_b": n(ks[3], (DEPTH, N_MOD * D_MODEL), f32) * 0.01,
        "norm_g": 1.0 + 0.05 * n(ks[4], (DEPTH, 6, D_MODEL), f32),
        "ffn_w_in": n(ks[5], (DEPTH, 2, D_MODEL, 2 * D_FF), f32) * D_MODEL ** -0.5,
        "ffn_w_out": n(ks[6], (DEPTH, 2, D_FF, D_MODEL), f32) * D_FF ** -0.5,
        "pool_w": n(ks[7], (N_POOL_LAYERS, N_POOL_GROUPS, POOL_GROUP, POOL_GROUP), f32) * POOL_GROUP ** -0.5,
        "pool_b": n(ks[8], (N_POOL_LAYERS, N_POOL_GROUPS, POOL_GROUP), f32) * 0.01,
        "pool_scale": 1.0 + 0.05 * n(ks[9], (N_POOL_LAYERS, D_MODEL), f32),
        "mla_w_in": n(ks[10], (N_MLA_LAYERS, D_MODEL, Q_LORA + KV_LORA + QK_ROPE), f32) * D_MODEL ** -0.5,
        "mla_q_norm": 1.0 + 0.05 * n(ks[11], (N_MLA_LAYERS, Q_LORA), f32),
        "mla_kv_norm": 1.0 + 0.05 * n(ks[12], (N_MLA_LAYERS, KV_LORA), f32),
        "mla_w_uq": n(ks[13], (N_MLA_LAYERS, Q_LORA, N_HEADS, QK_NOPE + QK_ROPE), f32) * Q_LORA ** -0.5,
        "mla_w_uk": n(ks[14], (N_MLA_LAYERS, KV_LORA, N_HEADS, QK_NOPE), f32) * KV_LORA ** -0.5,
        "mla_w_uv": n(ks[15], (N_MLA_LAYERS, KV_LORA, N_HEADS, V_HEAD), f32) * KV_LORA ** -0.5,
        "mla_w_o": n(ks[16], (N_MLA_LAYERS, N_HEADS * V_HEAD, D_MODEL), f32) * (N_HEADS * V_HEAD) ** -0.5,
    }

def first_block(x, c, ada_w, ada_b, norm_g, ffn_w_in, ffn_w_out, pool_w, pool_b, pool_scale,
              mla_w_in, mla_q_norm, mla_kv_norm, mla_w_uq, mla_w_uk, mla_w_uv, mla_w_o):
    B = x.shape[0]
    cos, sin = rope_tables(x.shape[1], x.dtype)
    sc = jax.nn.silu(c)
    for i in range(DEPTH):
        mod = (sc @ ada_w[i] + ada_b[i]).reshape(B, N_MOD, D_MODEL)[:, :, None, :]
        g = norm_g[i]
        x = modulated_sublayer(x, mod[:, 0:3], g[0], g[1],
                               lambda h: swiglu(h, ffn_w_in[i, 0], ffn_w_out[i, 0]), 0.5)
        if i % N_MIXERS == 0:
            li = i // N_MIXERS
            mixer = lambda h: pool_mixer(h, pool_w[li], pool_b[li], pool_scale[li])
        else:
            li = i // N_MIXERS
            mixer = lambda h: mla_mixer(h, mla_w_in[li], mla_q_norm[li], mla_kv_norm[li],
                                        mla_w_uq[li], mla_w_uk[li], mla_w_uv[li], mla_w_o[li],
                                        cos, sin)
        x = modulated_sublayer(x, mod[:, 3:6], g[2], g[3], mixer, 1.0)
        x = modulated_sublayer(x, mod[:, 6:9], g[4], g[5],
                               lambda h: swiglu(h, ffn_w_in[i, 1], ffn_w_out[i, 1]), 0.5)
    return x


DEPTH_2 = 1

N_HEADS_A = 8
N_KV_HEADS_A = 2
HEAD_DIM_A = 64
IDX_HEADS = 8
IDX_DIM = 64
TOPK_MAX = 256
CONV_CH = 512
CONV_WIDTH = 31
N_MEM = 256
MEM_HEADS = 4
MEM_HEAD_DIM = 128
N_BRANCHES = 3
N_GROUPS = 4
EXPERTS_PER_GROUP = 8
N_EXPERTS = N_GROUPS * EXPERTS_PER_GROUP
TOP_K_INNER = 2
D_FF_EXPERT = 256


SPLIT_SIZES = (
    N_HEADS_A * HEAD_DIM_A,
    N_KV_HEADS_A * HEAD_DIM_A,
    N_KV_HEADS_A * HEAD_DIM_A,
    IDX_HEADS * IDX_DIM,
    IDX_DIM,
    IDX_HEADS,
    2 * CONV_CH,
    MEM_HEADS * MEM_HEAD_DIM,
    N_BRANCHES * D_MODEL,
)
IN_COLS = sum(SPLIT_SIZES)


def rmsnorm_2(x, g):
    xf = x.astype(jnp.float32)
    y = xf * lax.rsqrt(jnp.mean(xf * xf, axis=-1, keepdims=True) + EPS)
    return (y * g.astype(jnp.float32)).astype(x.dtype)

def layernorm(x, g, b):
    xf = x.astype(jnp.float32)
    mu = jnp.mean(xf, axis=-1, keepdims=True)
    var = jnp.mean(jnp.square(xf - mu), axis=-1, keepdims=True)
    y = (xf - mu) * lax.rsqrt(var + EPS)
    return (y * g.astype(jnp.float32) + b.astype(jnp.float32)).astype(x.dtype)

def rope(x, pos):
    d = x.shape[-1]
    half = d // 2
    inv = ROPE_THETA ** (-jnp.arange(half, dtype=jnp.float32) / half)
    ang = pos.astype(jnp.float32)[:, None] * inv[None, :]
    cos = jnp.cos(ang)[None, :, None, :]
    sin = jnp.sin(ang)[None, :, None, :]
    xf = x.astype(jnp.float32)
    x1, x2 = xf[..., :half], xf[..., half:]
    out = jnp.concatenate([x1 * cos - x2 * sin, x2 * cos + x1 * sin], axis=-1)
    return out.astype(x.dtype)

def dsa_attention(q, k, v, q_idx, k_idx, w_idx, topk):
    B, S = q.shape[0], q.shape[1]
    G = N_HEADS_A // N_KV_HEADS_A
    n_blocks = S // Q_BLOCK
    key_pos = jnp.arange(S)
    w_idx = w_idx.astype(jnp.float32) * (IDX_HEADS ** -0.5)
    scale = HEAD_DIM_A ** -0.5

    def block(i):
        start = i * Q_BLOCK
        qb = lax.dynamic_slice_in_dim(q, start, Q_BLOCK, axis=1)
        qib = lax.dynamic_slice_in_dim(q_idx, start, Q_BLOCK, axis=1)
        wib = lax.dynamic_slice_in_dim(w_idx, start, Q_BLOCK, axis=1)
        tpos = start + jnp.arange(Q_BLOCK)
        logits = jnp.einsum('bqhd,bsd->bqhs', qib, k_idx,
                            preferred_element_type=jnp.float32) * (IDX_DIM ** -0.5)
        score = jnp.einsum('bqh,bqhs->bqs', wib, jax.nn.relu(logits))
        causal = key_pos[None, :] <= tpos[:, None]
        score = jnp.where(causal[None], score, -jnp.inf)
        _, sel = lax.top_k(score, topk)
        valid = sel <= tpos[None, :, None]
        kg = jax.vmap(lambda kk, ii: kk[ii])(k, sel)
        vg = jax.vmap(lambda vv, ii: vv[ii])(v, sel)
        qg = qb.reshape(B, Q_BLOCK, N_KV_HEADS_A, G, HEAD_DIM_A)
        s = jnp.einsum('bqhgd,bqkhd->bqhgk', qg, kg,
                       preferred_element_type=jnp.float32) * scale
        s = jnp.where(valid[:, :, None, None, :], s, -jnp.inf)
        p = jax.nn.softmax(s, axis=-1)
        o = jnp.einsum('bqhgk,bqkhd->bqhgd', p.astype(vg.dtype), vg)
        return o.reshape(B, Q_BLOCK, N_HEADS_A * HEAD_DIM_A)

    out = lax.map(block, jnp.arange(n_blocks))
    return jnp.moveaxis(out, 0, 1).reshape(B, S, N_HEADS_A * HEAD_DIM_A)

def conformer_conv(conv_in, conv_w, conv_b, ln_g, ln_b):
    a, gte = jnp.split(conv_in, 2, axis=-1)
    u = a * jax.nn.sigmoid(gte)
    y = lax.conv_general_dilated(
        u, conv_w, window_strides=(1,), padding=[(CONV_WIDTH - 1, 0)],
        dimension_numbers=('NWC', 'WIO', 'NWC'), feature_group_count=CONV_CH)
    y = y + conv_b
    return jax.nn.silu(layernorm(y, ln_g, ln_b))

def memory_attention(q_m, mem, g_mem, w_mem_kv, g_qm, g_km):
    B, S = q_m.shape[0], q_m.shape[1]
    M = mem.shape[1]
    kv = jnp.einsum('bmd,dc->bmc', rmsnorm_2(mem, g_mem), w_mem_kv)
    k_m, v_m = jnp.split(kv, 2, axis=-1)
    k_m = rmsnorm_2(k_m.reshape(B, M, MEM_HEADS, MEM_HEAD_DIM), g_km)
    v_m = v_m.reshape(B, M, MEM_HEADS, MEM_HEAD_DIM)
    q = rmsnorm_2(q_m.reshape(B, S, MEM_HEADS, MEM_HEAD_DIM), g_qm)
    s = jnp.einsum('bshd,bmhd->bhsm', q, k_m,
                   preferred_element_type=jnp.float32) * (MEM_HEAD_DIM ** -0.5)
    p = jax.nn.softmax(s, axis=-1)
    o = jnp.einsum('bhsm,bmhd->bshd', p.astype(v_m.dtype), v_m)
    return o.reshape(B, S, MEM_HEADS * MEM_HEAD_DIM)

def hier_moe(h, w_rg, b_rg, w_re, b_re, w_up, w_down):
    T = h.shape[0]
    g_logits = (h @ w_rg + b_rg).astype(jnp.float32)
    p_g = jax.nn.softmax(g_logits, axis=-1)
    g_sel = jnp.argmax(g_logits, axis=-1)
    p_sel = jnp.take_along_axis(p_g, g_sel[:, None], axis=1)
    e_logits = (h @ w_re + b_re).astype(jnp.float32).reshape(T, N_GROUPS, EXPERTS_PER_GROUP)
    e_in = jnp.take_along_axis(e_logits, g_sel[:, None, None], axis=1)[:, 0]
    top_v, top_i = lax.top_k(e_in, TOP_K_INNER)
    w2 = jax.nn.softmax(top_v, axis=-1) * p_sel
    expert_id = g_sel[:, None] * EXPERTS_PER_GROUP + top_i
    combine = jnp.sum(jax.nn.one_hot(expert_id, N_EXPERTS, dtype=jnp.float32)
                      * w2[..., None], axis=1).astype(h.dtype)
    out = jnp.zeros_like(h)
    for n in range(N_EXPERTS):
        a, b = jnp.split(h @ w_up[n], 2, axis=-1)
        out = out + combine[:, n:n + 1] * ((jax.nn.silu(a) * b) @ w_down[n])
    return out

def second_inputs(seed: int = 0) -> dict:
    key = jax.random.key(seed)
    ks = jax.random.split(key, 28)
    f32 = jnp.float32
    L = DEPTH_2

    def nrm(k, shape, fan_in):
        return jax.random.normal(k, shape, f32) * (fan_in ** -0.5)

    def gain(k, shape):
        return 1.0 + 0.05 * jax.random.normal(k, shape, f32)

    def small(k, shape, s):
        return s * jax.random.normal(k, shape, f32)

    return {
        "x": jax.random.normal(ks[0], (BATCH, SEQ, D_MODEL), f32),
        "mem": jax.random.normal(ks[1], (BATCH, N_MEM, D_MODEL), f32),
        "g_mix": gain(ks[2], (L, D_MODEL)),
        "w_in": nrm(ks[3], (L, D_MODEL, IN_COLS), D_MODEL),
        "b_gate": small(ks[4], (L, N_BRANCHES * D_MODEL), 0.02),
        "g_qa": gain(ks[5], (L, HEAD_DIM_A)),
        "g_ka": gain(ks[6], (L, HEAD_DIM_A)),
        "g_idx_k": gain(ks[7], (L, IDX_DIM)),
        "conv_w": nrm(ks[8], (L, CONV_WIDTH, 1, CONV_CH), CONV_WIDTH),
        "conv_b": small(ks[9], (L, CONV_CH), 0.02),
        "ln_g": gain(ks[10], (L, CONV_CH)),
        "ln_b": small(ks[11], (L, CONV_CH), 0.02),
        "g_mem": gain(ks[12], (L, D_MODEL)),
        "w_mem_kv": nrm(ks[13], (L, D_MODEL, 2 * MEM_HEADS * MEM_HEAD_DIM), D_MODEL),
        "g_qm": gain(ks[14], (L, MEM_HEAD_DIM)),
        "g_km": gain(ks[15], (L, MEM_HEAD_DIM)),
        "w_br_a": nrm(ks[16], (L, N_HEADS_A * HEAD_DIM_A, D_MODEL), N_HEADS_A * HEAD_DIM_A),
        "w_br_b": nrm(ks[17], (L, CONV_CH, D_MODEL), CONV_CH),
        "w_br_m": nrm(ks[18], (L, MEM_HEADS * MEM_HEAD_DIM, D_MODEL), MEM_HEADS * MEM_HEAD_DIM),
        "w_o": nrm(ks[19], (L, D_MODEL, D_MODEL), D_MODEL),
        "g_ffn": gain(ks[20], (L, D_MODEL)),
        "w_rg": nrm(ks[21], (L, D_MODEL, N_GROUPS), D_MODEL),
        "b_rg": small(ks[22], (L, N_GROUPS), 0.01),
        "w_re": nrm(ks[23], (L, D_MODEL, N_EXPERTS), D_MODEL),
        "b_re": small(ks[24], (L, N_EXPERTS), 0.01),
        "w_up": nrm(ks[25], (L, N_EXPERTS, D_MODEL, 2 * D_FF_EXPERT), D_MODEL),
        "w_down": nrm(ks[26], (L, N_EXPERTS, D_FF_EXPERT, D_MODEL), D_FF_EXPERT),
    }

def second_block(x, mem, g_mix, w_in, b_gate, g_qa, g_ka, g_idx_k, conv_w, conv_b, ln_g, ln_b,
              g_mem, w_mem_kv, g_qm, g_km, w_br_a, w_br_b, w_br_m, w_o, g_ffn,
              w_rg, b_rg, w_re, b_re, w_up, w_down):
    B, S, D = x.shape
    topk = min(TOPK_MAX, S // 4)
    pos = jnp.arange(S, dtype=jnp.int32)
    split_points = []
    acc = 0
    for sz in SPLIT_SIZES[:-1]:
        acc += sz
        split_points.append(acc)

    for l in range(DEPTH_2):
        h = rmsnorm_2(x, g_mix[l])
        proj = jnp.einsum('bsd,dc->bsc', h, w_in[l])
        q_a, k_a, v_a, q_i, k_i, w_i, conv_in, q_m, gate_logits = jnp.split(
            proj, split_points, axis=-1)

        q_a = rope(rmsnorm_2(q_a.reshape(B, S, N_HEADS_A, HEAD_DIM_A), g_qa[l]), pos)
        k_a = rope(rmsnorm_2(k_a.reshape(B, S, N_KV_HEADS_A, HEAD_DIM_A), g_ka[l]), pos)
        v_a = v_a.reshape(B, S, N_KV_HEADS_A, HEAD_DIM_A)
        q_i = rope(q_i.reshape(B, S, IDX_HEADS, IDX_DIM), pos)
        k_i = rope(rmsnorm_2(k_i, g_idx_k[l])[:, :, None, :], pos)[:, :, 0, :]
        o_a = dsa_attention(q_a, k_a, v_a, q_i, k_i, w_i, topk)

        o_b = conformer_conv(conv_in, conv_w[l], conv_b[l], ln_g[l], ln_b[l])

        o_m = memory_attention(q_m, mem, g_mem[l], w_mem_kv[l], g_qm[l], g_km[l])

        gates = jax.nn.sigmoid((gate_logits + b_gate[l]).astype(jnp.float32)).astype(x.dtype)
        gates = gates.reshape(B, S, N_BRANCHES, D)
        merged = (gates[:, :, 0] * (o_a @ w_br_a[l])
                  + gates[:, :, 1] * (o_b @ w_br_b[l])
                  + gates[:, :, 2] * (o_m @ w_br_m[l]))
        x = x + merged @ w_o[l]

        h2 = rmsnorm_2(x, g_ffn[l]).reshape(B * S, D)
        moe = hier_moe(h2, w_rg[l], b_rg[l], w_re[l], b_re[l], w_up[l], w_down[l])
        x = x + moe.reshape(B, S, D)
    return x


def setup_inputs(seed=0):
    out = dict(first_inputs(seed))
    for name, value in second_inputs(seed + 1).items():
        if name != "x":
            out[name + "_2"] = value
    return out


def reference(
    x, c, ada_w, ada_b, norm_g, ffn_w_in, ffn_w_out, pool_w, pool_b, pool_scale, mla_w_in,
    mla_q_norm, mla_kv_norm, mla_w_uq, mla_w_uk, mla_w_uv, mla_w_o, mem_2, g_mix_2, w_in_2,
    b_gate_2, g_qa_2, g_ka_2, g_idx_k_2, conv_w_2, conv_b_2, ln_g_2, ln_b_2, g_mem_2,
    w_mem_kv_2, g_qm_2, g_km_2, w_br_a_2, w_br_b_2, w_br_m_2, w_o_2, g_ffn_2, w_rg_2, b_rg_2,
    w_re_2, b_re_2, w_up_2, w_down_2,
):
    x = first_block(
        x, c, ada_w, ada_b, norm_g, ffn_w_in, ffn_w_out, pool_w, pool_b, pool_scale, mla_w_in,
        mla_q_norm, mla_kv_norm, mla_w_uq, mla_w_uk, mla_w_uv, mla_w_o,
    )
    return second_block(
        x, mem_2, g_mix_2, w_in_2, b_gate_2, g_qa_2, g_ka_2, g_idx_k_2, conv_w_2, conv_b_2,
        ln_g_2, ln_b_2, g_mem_2, w_mem_kv_2, g_qm_2, g_km_2, w_br_a_2, w_br_b_2, w_br_m_2,
        w_o_2, g_ffn_2, w_rg_2, b_rg_2, w_re_2, b_re_2, w_up_2, w_down_2,
    )


_drawn_inputs = setup_inputs


def setup_inputs(seed=0):
    import zlib

    import numpy as np

    out = dict(_drawn_inputs(seed))
    spreads = {}
    factors = {'pool_b': 2.883,
     'mla_q_norm': 4.269,
     'g_mix_2': 3.305,
     'b_gate_2': 8.0,
     'g_qa_2': 8.0,
     'g_ka_2': 8.0,
     'g_idx_k_2': 5.437,
     'conv_b_2': 8.0,
     'ln_g_2': 15.05,
     'ln_b_2': 37.712,
     'g_mem_2': 8.0,
     'g_qm_2': 8.0,
     'g_km_2': 8.0,
     'b_rg_2': 64.0,
     'b_re_2': 58.167,
     'g_ffn_2': 7.681}
    for name, (base, spread) in spreads.items():
        noise = np.random.default_rng([zlib.crc32(name.encode()), seed]).standard_normal(out[name].shape)
        drawn = base * np.exp(spread * noise) if base else spread * noise
        out[name] = __import__('jax').numpy.asarray(drawn.astype(out[name].dtype))
    for name, factor in factors.items():
        out[name] = (out[name] * factor).astype(out[name].dtype)
    return out
```

```python
from contextlib import ExitStack

import numpy as np

import concourse.bass as bass
from concourse import mybir

F32 = mybir.dt.float32
F32R = mybir.dt.float32r
ACT = mybir.ActivationFunctionType
ALU = mybir.AluOpType
AX_X = mybir.AxisListType.X

P = 128
T = 2
S = 256
D = 1024
KD = D // P
EPS = 1e-6
F2 = 2816
CHUNK = 2048
UNIT = 1024
NRAW = 6
NUNIT = 6
NFF = 11
ARENA = 11460
NEG = -1e30
MARK = -3e38
PROJ = [(1352, 512), (1864, 512), (1280, 72), (768, 512), (0, 512), (512, 256), (2376, 512)]
GATE0 = 2888
CONVW = 31


class Tok:

    def __init__(self, queue, index, sem, value):
        self.queue, self.index, self.sem, self.value = queue, index, sem, value


class Queues:

    NAMES = ("tensor", "vector", "scalar", "gpsimd", "sync")

    def __init__(self, sems):
        self.sems = sems
        self.wanted = {n: set() for n in self.NAMES}
        self.values = {}
        self.begin(None, None)

    def begin(self, name, eng):
        self.active, self.eng = name, eng
        self.at = {n: 0 for n in self.NAMES}
        self.last, self.seen = {}, {}

    def counted(self):
        for n in self.NAMES:
            self.values[n] = {index: k + 1 for k, index in enumerate(sorted(self.wanted[n]))}

    def wait(self, waits):
        if self.active is None:
            for w in waits:
                if w.queue is not None:
                    self.wanted[w.queue].add(w.index)
            return
        need = {}
        for w in waits:
            if w.value > self.seen.get(w.sem.name, 0):
                if w.sem.name not in need or w.value > need[w.sem.name].value:
                    need[w.sem.name] = w
        for key, w in need.items():
            self.eng.wait_ge(w.sem, w.value)
            self.seen[key] = w.value

    def put(self, name, fn, waits, own=True):
        index = self.at[name]
        self.at[name] += 1
        waits = flat(waits)
        if own and name in self.last and name != "tensor":
            waits.append(self.last[name])
        value = self.values[name].get(index) if self.values else None
        tok = Tok(name, index, self.sems[name], value)
        self.last[name] = tok
        if self.active in (None, name):
            self.wait(waits)
        if self.active == name:
            ins = fn(self.eng)
            if value is not None:
                ins.then_inc(tok.sem, 1)
        return tok

    def dma(self, name, fn, waits, sem, value):
        if self.active in (None, name):
            self.wait(flat(waits))
        if self.active == name:
            fn(self.eng).then_inc(sem, 16)
        return Tok(None, None, sem, value)


def flat(x):
    if x is None:
        return []
    if isinstance(x, Tok):
        return [x]
    return [t for y in x for t in flat(y)]


def build(nc, I, out_ap):
    ctx = ExitStack()
    with ctx:
        def sb(name, shape, dt=F32):
            return ctx.enter_context(nc.sbuf_tensor(name, shape, dt))

        named = {}

        def sem(name):
            if name not in named:
                named[name] = ctx.enter_context(nc.semaphore(name))
            return named[name]

        Q = Queues({n: sem(f"done_{n}") for n in Queues.NAMES})

        def pe(fn, *w):
            return Q.put("tensor", fn, w)

        def dve(fn, *w, own=True):
            return Q.put("vector", fn, w, own)

        def act(fn, *w, own=True):
            return Q.put("scalar", fn, w, own)

        def pool(fn, *w, own=True):
            return Q.put("gpsimd", fn, w, own)

        PS = ctx.enter_context(nc.psum_tensor("banks", [P, 8, 512], F32))
        PB = [PS[:, i, :] for i in range(8)]
        YB = [[0, 1], [2, 3]]
        AB = [4, 5]

        raw = [sb(f"raw{i}", [P, CHUNK]) for i in range(NRAW)]
        uh = [sb(f"uh{i}", [P, UNIT], F32R) for i in range(NUNIT)]
        ul = [sb(f"ul{i}", [P, UNIT], F32R) for i in range(NUNIT)]
        ident = sb("ident", [P, P])
        x = sb("x", [P, T, D])
        hh = sb("hh", [P, KD, S], F32R)
        hl = sb("hl", [P, KD, S], F32R)
        Gs = sb("Gs", [P, 3, D])
        G = [Gs[:, i, :] for i in range(3)]
        bh = sb("bh", [P, 4, S], F32R)
        bl = sb("bl", [P, 4, S], F32R)
        gT_h = [bh[:, 2 * i:2 * i + 2, :] for i in range(2)]
        gT_l = [bl[:, 2 * i:2 * i + 2, :] for i in range(2)]
        sg = sb("sg", [P, T, 256])
        ug = [sb(f"ug{i}", [P, T, 256]) for i in range(2)]
        full = sb("full", [P, 2, 512])
        ab = sb("ab", [P, 6, 2, KD])
        ngc = sb("ngc", [P, 96])
        cc = sb("cc", [P, 48])
        sc = sb("sc", [P, KD])
        st = sb("st", [P, 280])
        comb = Gs[:, 0, 0:64].rearrange("p (t n) -> p t n", t=T)
        AR = sb("arena", [P, ARENA])
        adab = sb("adab", [P, 512])
        kvm = sb("kvm", [P, 2, T, 512])
        sum4 = sb("sum4", [P, P])

        def flow():
            free = {i: [] for i in range(8)}
            at = [0]

            def arena(*shape):
                n = int(np.prod(shape))
                a = AR[:, at[0]:at[0] + n]
                at[0] += n
                assert at[0] <= ARENA, at[0]
                if len(shape) == 2:
                    a = a.rearrange("p (a b) -> p a b", b=shape[1])
                elif len(shape) == 3:
                    a = a.rearrange("p (a b c) -> p a b c", b=shape[1], c=shape[2])
                return a

            chunks = []

            def plan_rows(key, w, k0, kk, c0, n, conv=True):
                v = w.rearrange("(k p) n -> p k n", p=P)[:, k0:k0 + kk, c0:c0 + n]
                chunks.append((key, [(v, kk, n, 0)], kk, n, conv))

            def plan_block(key, w, c0, n, K=KD):
                for k0 in range(0, K, 4):
                    plan_rows(key, w, k0, 4, c0, n)

            def plan_wide(key, w, r0):
                v = w[r0:r0 + 256, :].rearrange("(k p) n -> p k n", p=P)
                chunks.append((key, [(v, 2, D, 0)], 2, D, True))

            def plan_ffn_block(key, i, s, b):
                w = I["ffn_w_in"][i, s].rearrange("(k p) (g n) -> p k g n", p=P, g=2)
                for k0 in (0, 4):
                    pcs = [(w[:, k0:k0 + 4, g, b * 256:(b + 1) * 256], 4, 512, g * 256) for g in (0, 1)]
                    chunks.append((key, pcs, 4, 512, True))

            def plan_ada(i, j):
                w = I["ada_w"][i]
                for k0 in (0, 4):
                    plan_rows(("ada", i, j), w, k0, 4, j * 512, 512, conv=False)

            ada_order = [(i, j) for i in range(2) for j in range(18)]
            ADA_AT, at_ = {}, 4
            for i_, s_, n_ in ((0, 0, 11), (0, 1, 11), (1, 0, 7)):
                for b_ in range(n_):
                    ADA_AT[(i_, s_, b_)] = ada_order[at_:at_ + 1]
                    at_ += 1
                if at_ == 15:
                    ada_pool = ada_order[15:18]
                    at_ = 18

            def plan_ffn(i, s):
                for b in range(NFF):
                    plan_ffn_block(("fi", i, s, b), i, s, b)
                    if b:
                        plan_wide(("fo", i, s, b - 1), I["ffn_w_out"][i, s], (b - 1) * 256)
                    for a in ADA_AT.get((i, s, b), []):
                        plan_ada(*a)
                plan_wide(("fo", i, s, NFF - 1), I["ffn_w_out"][i, s], (NFF - 1) * 256)

            for a in ada_order[:4]:
                plan_ada(*a)
            plan_ffn(0, 0)
            for b in range(2):
                plan_block(("kv",), I["w_mem_kv_2"][0], b * 512, 512)
            for a in ada_pool:
                plan_ada(*a)
            chunks.append((("pw",), [(I["pool_w"][0].rearrange("g (k p) n -> p (g k) n", p=P), 8, 256, 0)], 8, 256, False))
            plan_ffn(0, 1)
            plan_ffn(1, 0)
            plan_block(("mi",), I["mla_w_in"][0], 0, 416)
            for k in range(2):
                v = I["mla_w_uq"][0].rearrange("(k p) h d -> p k (h d)", p=P)[:, k:k + 1, :]
                chunks.append((("uq",), [(v, 1, 1536, 0)], 1, 1536, False))
            for nm in ("mla_w_uk", "mla_w_uv"):
                v = I[nm].rearrange("a c h d -> c a (h d)")
                chunks.append(((nm,), [(v, 1, 1024, 0)], 1, 1024, False))
            for k in range(4):
                plan_wide(("mo",), I["mla_w_o"][0], k * 256)
            plan_ffn(1, 1)
            for c0, n in PROJ:
                plan_block(("pj",), I["w_in_2"][0], c0, n)
            for g in (0, 2, 1):
                for c in range(2):
                    plan_block(("gt",), I["w_in_2"][0], GATE0 + g * 1024 + c * 512, 512)
            for nm in ("w_br_a_2", "w_br_m_2", "w_br_b_2"):
                for k in range(2):
                    plan_wide(("br",), I[nm][0], k * 256)
            for k in range(4):
                plan_wide(("wo",), I["w_o_2"][0], k * 256)
            for b in range(32):
                plan_block(("mu", b), I["w_up_2"][0, b], 0, 512)
                if b:
                    plan_wide(("md", b - 1), I["w_down_2"][0, b - 1], 0)
            plan_wide(("md", 31), I["w_down_2"][0, 31], 0)

            ring_sem = [sem(f"ring{i}") for i in range(NRAW)]
            dma_tok, chunk_rel = {}, {}
            nxt = [0]

            def pump():
                while nxt[0] < len(chunks) and (nxt[0] < NRAW or nxt[0] - NRAW in chunk_rel):
                    m = nxt[0]
                    key, pcs, kk, n, conv = chunks[m]
                    waits = chunk_rel[m - NRAW] if m >= NRAW else []
                    slot = raw[m % NRAW][:, 0:kk * n].rearrange("p (k n) -> p k n", n=n)
                    base = fills[m % NRAW]
                    for v, k_, n_, c0 in pcs:
                        w = v.shape[-1]
                        base += 16
                        tok = Q.dma("sync", lambda e, d=slot[:, :, c0:c0 + w], v=v: e.dma_start(d, v), waits,
                                    ring_sem[m % NRAW], base)
                    fills[m % NRAW] = base
                    dma_tok[m] = tok
                    nxt[0] += 1

            fills = [0] * NRAW
            units = []
            for m, (key, pcs, kk, n, conv) in enumerate(chunks):
                if conv:
                    for h in range(2):
                        units.append((m, h, kk // 2, n))
            unit_rel, unit_tok = {}, {}
            cpos, upos, conv_pos = [0], [0], [0]
            pump()

            def convert(u):
                m, h, kk, n = units[u]
                w = kk * n
                src = raw[m % NRAW][:, h * w:(h + 1) * w]
                r = u % NUNIT
                th = act(lambda e: e.activation(uh[r][:, 0:w], src, ACT.Copy), dma_tok[m],
                         unit_rel[u - NUNIT] if u >= NUNIT else [], own=False)
                tl = dve(lambda e: e.tensor_tensor(ul[r][:, 0:w], src, uh[r][:, 0:w].bitcast(F32), ALU.subtract),
                         th, own=False)
                unit_tok[u] = tl
                if h == 1:
                    chunk_rel[m] = [tl]
                    pump()

            def ahead(u):
                while conv_pos[0] < len(units) and conv_pos[0] <= u + NUNIT - 1:
                    c = conv_pos[0]
                    if c >= NUNIT and c - NUNIT not in unit_rel:
                        break
                    if units[c][0] not in dma_tok:
                        break
                    convert(c)
                    conv_pos[0] += 1

            later, rate, spent, after_unit = [], [1.5], [0.0], [lambda: None]

            def step(budget):
                spent[0] = min(spent[0] + budget, budget)
                while later and spent[0] > 0:
                    w, fn = later.pop(0)
                    spent[0] -= w
                    fn()

            def flush(mark=None):
                while later and not (mark is not None and mark in done_marks):
                    later.pop(0)[1]()
                spent[0] = 0.0

            done_marks = set()

            def put_off(weight, fn):
                later.append((weight, fn))

            def put_mark(mark):
                later.append((0.0, lambda: done_marks.add(mark)))

            def take_unit(key):
                u = upos[0]
                while u not in unit_tok:
                    ahead(u)
                    if u not in unit_tok:
                        assert later, (u, units[u], chunks[units[u][0]][0])
                        later.pop(0)[1]()
                m, h, kk, n = units[u]
                assert m == cpos[0], (chunks[m][0], chunks[cpos[0]][0], key)
                assert chunks[m][0][:len(key)] == key, (chunks[m][0], key)
                upos[0] += 1
                if h == 1:
                    cpos[0] += 1
                ahead(u)
                r = u % NUNIT
                hi = uh[r][:, 0:kk * n].rearrange("p (k n) -> p k n", n=n)
                lo = ul[r][:, 0:kk * n].rearrange("p (k n) -> p k n", n=n)
                return u, hi, lo, kk, n, unit_tok[u]

            def take_raw(key):
                m = cpos[0]
                k, pcs, kk, n, conv = chunks[m]
                assert k[:len(key)] == key and not conv, (k, key)
                cpos[0] += 1
                return m, raw[m % NRAW][:, 0:kk * n].rearrange("p (k n) -> p k n", n=n), dma_tok[m]

            def give_raw(m, tok):
                chunk_rel[m] = [tok]
                pump()

            def linear(key, K, lhi, llo, lt, banks, first=True, last=True, mid=None):
                k = 0
                tok = None
                while k < K:
                    u, hi, lo, kk, n, ut = take_unit(key)
                    if mid is not None and k >= K // 2:
                        mid()
                        mid = None
                    for t in range(T):
                        for j in range(kk):
                            for c in range((n + 511) // 512):
                                w = min(512, n - c * 512)
                                o = PB[banks[t][c]][:, 0:w]
                                a, b = lhi(k + j, t), llo(k + j, t)
                                wh, wl = hi[:, j, c * 512:c * 512 + w], lo[:, j, c * 512:c * 512 + w]
                                s0 = first and k + j == 0
                                s1 = last and k + j == K - 1
                                pe(lambda e, o=o, a=a, wh=wh, s0=s0: e.matmul(o, a, wh, start=s0, stop=False),
                                   ut, lt[k + j] if isinstance(lt, list) and lt and isinstance(lt[0], list) else lt,
                                   free[banks[t][c]] if s0 else [])
                                pe(lambda e, o=o, a=a, wl=wl: e.matmul(o, a, wl, start=False, stop=False))
                                tok = pe(lambda e, o=o, b=b, wh=wh, s1=s1: e.matmul(o, b, wh, start=False, stop=s1))
                    unit_rel[u] = [tok]
                    k += kk
                    step(rate[0])
                    after_unit[0]()
                ahead(upos[0] - 1)
                return tok

            loads = [0]

            def load(dst, src, *w, q="gpsimd"):
                loads[0] += 1
                s = sem(f"load{loads[0]}")
                return Q.dma(q, lambda e: e.dma_start(dst, src), w, s, 16)

            t_s4 = load(sum4[:, :], I["sum4_c"], q="scalar")
            t_id = load(ident[:, :], I["ident_c"], q="scalar")
            stk1 = G[2][0:96, 0:128]
            stk2 = G[2][0:48, 128:256]
            l2 = []
            r0 = 0
            where = {}
            for nm, rows in (("c", 8), ("mla_q_norm", 2), ("mla_kv_norm", 1), ("g_mix_2", 8), ("conv_b_2", 4),
                             ("ln_g_2", 4), ("ln_b_2", 4), ("g_mem_2", 8), ("g_ffn_2", 8)):
                l2.append(load(stk2[r0:r0 + rows, :], I[nm].rearrange("a (k p) -> (a k) p", p=P), q="scalar"))
                where[nm] = r0
                r0 += rows
            t_n = load(stk1, I["norm_g"].rearrange("i m (k p) -> (i m k) p", p=P), q="scalar")
            t_x = [load(x[:, t, :], I["x"][0, t * P:(t + 1) * P, :], q="scalar") for t in range(T)]

            def col(nm, k):
                return cc[:, where[nm] + k:where[nm] + k + 1]

            tp = pe(lambda e: e.transpose(PB[7][:, 0:r0], stk2[0:r0, :], ident[0:r0, 0:r0]), t_id, l2)
            t_cc = dve(lambda e: e.tensor_copy(cc[:, 0:r0], PB[7][:, 0:r0]), tp)
            t_sc = act(lambda e: e.activation(sc[:, :], cc[:, 0:8], ACT.Silu), t_cc)
            tp = pe(lambda e: e.transpose(PB[6][:, 0:96], stk1, ident[0:96, 0:96]), t_n)
            t_ng = dve(lambda e: e.tensor_copy(ngc[:, :], PB[6][:, 0:96]), tp)
            free[7] = [t_cc]
            free[6] = [t_ng]

            def bcast_row(src, n):
                return src.to_broadcast([P, n])

            g_tok, g_done = {}, {}

            def load_G(s, *w):
                i, m = s // 3, s % 3
                src = I["norm_g"][i, 2 * m + 1:2 * m + 2, :]
                g_tok[s] = load(G[s % 3][:, :], src.to_broadcast([P, D]), *w)

            load_G(0)
            load_G(1)
            load_G(2, t_ng, t_cc)

            t_ab = load(adab[0:36, :], I["ada_b"].rearrange("i (j n) -> (i j) n", n=512), q="scalar")
            ab_tok = {s: [] for s in range(6)}

            xn = arena(T, D)
            XN_END = at[0]
            def ada_end(i, j, tok):
                s, kind, half = i * 3 + j // 6, (j // 2) % 3, j % 2
                if kind == 2:
                    g = G[s % 3][:, half * 512:half * 512 + 512]
                    tk = dve(lambda e: e.scalar_tensor_tensor(g, PB[7], 1.0, g, ALU.add, ALU.mult), tok, g_tok[s])
                    g_done.setdefault(s, []).append(tk)
                else:
                    d = full[:, 1, :].rearrange("p (a b) -> p a b", b=P)
                    dve(lambda e: e.tensor_tensor(d, PB[7].rearrange("p (a b) -> p a b", b=P),
                                                  ident[:, :].unsqueeze(1).to_broadcast([P, 4, P]), ALU.mult),
                        tok, Q.last["scalar"])
                    dst = ab[:, s, 1 - kind, half * 4:half * 4 + 4]
                    tk = dve(lambda e: e.tensor_reduce(dst, d, AX_X, ALU.add))
                    if kind == 1:
                        gc = ngc[:, i * 48 + (s % 3) * 16 + half * 4:i * 48 + (s % 3) * 16 + half * 4 + 4]
                        tk = dve(lambda e: e.scalar_tensor_tensor(dst, dst, 1.0, gc, ALU.add, ALU.mult), t_ng)
                    ab_tok[s].append(tk)
                free[7] = [tk]

            def ada(i, j):
                got = [take_raw(("ada", i, j)) for _ in range(2)]
                r = i * 18 + j

                def parts():
                    pe(lambda e: e.matmul(PB[7][0:32, :], ident[0:36, r:r + 1].to_broadcast([36, 32]),
                                          adab[0:36, :], start=True, stop=False), t_ab, t_id, free[7])
                    for k in range(KD):
                        m, w, dt = got[k // 4]
                        g = (k + 1) % 4
                        tok = pe(lambda e: e.matmul(
                            PB[7][32 * g:32 * g + 32, :], sc[:, k:k + 1].to_broadcast([P, 32]), w[:, k % 4, :],
                            start=(k < 3), stop=(k >= 4)), dt, t_sc)
                        if k % 4 == 3:
                            give_raw(m, tok)
                    ada_s[i, j] = act(lambda e: e.activation(full[:, 0, :], PB[7], ACT.Copy), tok,
                                      Q.last["vector"])

                def total():
                    tok = pe(lambda e: e.matmul(PB[7], sum4[:, :], full[:, 0, :], start=True, stop=True),
                             ada_s[i, j], t_s4)
                    ada_end(i, j, tok)
                    full_pe[:] = [tok, Q.last["vector"]]

                parts()
                put_off(1.3, total)

            ada_s, full_pe = {}, []

            def warm():
                act(lambda e: e.activation(st[:, 258:259], sum4[:, 0:1], ACT.Sqrt), t_s4)

            def rstd(dst, ss, n, *w, weight=1.0):
                c = ss.shape[-1]
                v, r, a = st[:, 128:128 + c], st[:, 160:160 + c], st[:, 192:192 + c]
                tv = dve(lambda e: e.tensor_scalar(v, ss, 1.0 / n, EPS, ALU.mult, ALU.add), w)
                ts = act(lambda e: e.activation(r, v, ACT.Sqrt), tv)
                dve(lambda e: e.reciprocal(r, r), ts)
                dve(lambda e: e.tensor_tensor(a, r, r, ALU.mult))
                dve(lambda e: e.tensor_tensor(a, a, v, ALU.mult))
                dve(lambda e: e.tensor_scalar(a, a, -0.5, 1.5, ALU.mult, ALU.add))
                return dve(lambda e: e.scalar_tensor_tensor(dst, r, weight, a, ALU.mult, ALU.mult))

            def row_squares(dst, src, *w):
                o = full[:, :, :].rearrange("p a b -> p (a b)")
                return act(lambda e: e.activation(o, src, ACT.Square, accum_out=dst), w, full_pe)

            RB = [6, 7, 4, 5]
            rb = [0]

            def to_T(src, K, dst_h, dst_l, scale=None, bias=None, func=None, keep=None, waits=(), wdst=()):
                toks = []
                for k0 in range(0, K, 2):
                    b = RB[rb[0] % 4]
                    rb[0] += 1
                    nk = min(2, K - k0)
                    for k in range(nk):
                        for t in range(T):
                            tp = pe(lambda e, k=k, t=t, b=b: e.transpose(
                                PB[b][:, k * S + t * P:k * S + (t + 1) * P], src(t, k0 + k), ident[:, :]),
                                waits, free[b], t_id)
                    ps = PB[b][:, 0:nk * S].rearrange("p (k n) -> p k n", n=S)
                    H, L = (dst_h[:, k0:k0 + nk, :], dst_l[:, k0:k0 + nk, :]) if dst_h is not None else (None, None)
                    fl = full[:, (k0 // 2) % 2, 0:nk * S].rearrange("p (k n) -> p k n", n=S)
                    if scale is None:
                        th = act(lambda e: e.activation(H, ps, ACT.Copy), tp, wdst)
                        tl = dve(lambda e: e.tensor_tensor(L, ps, H.bitcast(F32), ALU.subtract), th)
                        fr = [th, tl]
                    elif func is None:
                        if keep is not None:
                            fl = keep[:, k0:k0 + nk, :]
                        for k in range(nk):
                            sc_, bi_ = scale(k0 + k), (bias(k0 + k) if bias is not None else 0.0)
                            tf = dve(lambda e: e.tensor_scalar(fl[:, k, :], ps[:, k, :], sc_, bi_, ALU.mult, ALU.add),
                                     tp, wdst, full_pe)
                        fr = [tf]
                        if H is None:
                            toks += [[tf]] * nk
                            free[b] = fr
                            continue
                        th = act(lambda e: e.activation(H, fl, ACT.Copy), tf)
                        tl = dve(lambda e: e.tensor_tensor(L, fl, H.bitcast(F32), ALU.subtract), th)
                    else:
                        for k in range(nk):
                            sc_, bi_ = scale(k0 + k), bias(k0 + k)
                            tf = act(lambda e: e.activation(fl[:, k, :], ps[:, k, :], func, bias=bi_, scale=sc_),
                                     tp, wdst)
                        th = act(lambda e: e.activation(H, fl, ACT.Copy))
                        tl = dve(lambda e: e.tensor_tensor(L, fl, H.bitcast(F32), ALU.subtract), th)
                        fr = [tf]
                    toks += [[th, tl]] * nk
                    free[b] = fr
                return toks


            def prenorm(waits=(), src=None, dst=None):
                src = x if src is None else src
                dst = xn if dst is None else dst
                for t in range(T):
                    ta = row_squares(st[:, 4 + t:5 + t], src[:, t, :], waits[t:t + 1] if len(waits) == T else waits)
                rstd(st[:, 6:8], st[:, 4:6], D, ta)
                for t in range(T):
                    tk = dve(lambda e: e.tensor_scalar(dst[:, t, :], src[:, t, :], st[:, 6 + t:7 + t], None,
                                                       ALU.mult), last_pe_xn)
                return tk

            last_pe_xn = []

            def rows_xn(t, k):
                return xn[:, t, k * P:(k + 1) * P]

            def pre(s, keep=None, split=True):
                wd = [Q.last["tensor"]]
                flush()
                tk = prenorm(x_tok)
                toks = to_T(rows_xn, KD, hh if split else None, hl, scale=lambda k: ab[:, s, 0, k:k + 1],
                            bias=lambda k: ab[:, s, 1, k:k + 1],
                            keep=keep, waits=[tk], wdst=wd + ab_tok[s])
                last_pe_xn[:] = [Q.last["tensor"]]
                return toks

            def post(s, src, weight, waits, psum=True):
                while len(g_done.get(s, [])) < 2:
                    later.pop(0)[1]()
                warm()
                g = G[s % 3]
                if psum:
                    t0 = row_squares(st[:, 4:5], src(0), waits)
                    d1 = dve(lambda e: e.tensor_tensor(xn[:, 1, :], src(1), g, ALU.mult), waits, g_done[s], last_pe_xn)
                    t1 = row_squares(st[:, 5:6], src(1), d1)
                    d0 = dve(lambda e: e.tensor_tensor(xn[:, 0, :], src(0), g, ALU.mult), t0)
                else:
                    for t in range(T):
                        t1 = row_squares(st[:, 4 + t:5 + t], src(t), waits)
                        dve(lambda e: e.tensor_tensor(xn[:, t, :], src(t), g, ALU.mult), t1, g_done[s])
                rstd(st[:, 6:8], st[:, 4:6], D, t1, weight=weight)
                x_tok[:] = [dve(lambda e: e.scalar_tensor_tensor(
                    x[:, t, :], xn[:, t, :], st[:, 6 + t:7 + t], x[:, t, :], ALU.mult, ALU.add)) for t in range(T)]
                if psum:
                    for t in range(T):
                        for b in YB[t]:
                            free[b] = [x_tok[0]]
                if s + 3 < 6:
                    load_G(s + 3, x_tok)

            def ypsum2(t):
                return PS[:, 2 * t:2 * t + 2, :].rearrange("p a b -> p (a b)")

            def ypsum(t, h):
                return PB[YB[t][h]][:, :]

            lh = lambda k, t: hh[:, k, t * P:(t + 1) * P]
            ll = lambda k, t: hl[:, k, t * P:(t + 1) * P]

            ff = {"n": 0, "ug": [[], []], "gt": [[], []], "sg": []}

            def ffn_like(nb, kin, kout, toks, between, combine=None):
                def spread(b):
                    i = b % 2
                    for f in range(2):
                        for t in range(T):
                            tp = pe(lambda e, f=f, t=t: e.transpose(
                                PB[6][:, f * S + t * P:f * S + (t + 1) * P], ug[i][:, t, f * P:(f + 1) * P], ident[:, :]),
                                ff["ug"][i], free[6])
                    th = act(lambda e: e.activation(gT_h[i][:, :, :], PB[6][:, :].rearrange("p (a b) -> p a b", b=S),
                                                    ACT.Copy), tp, ff["gt"][i])
                    tl = dve(lambda e: e.tensor_tensor(
                        gT_l[i][:, :, :], PB[6][:, :].rearrange("p (a b) -> p a b", b=S),
                        gT_h[i][:, :, :].bitcast(F32), ALU.subtract), th)
                    free[6] = [th, tl]
                    ff["ugfree"][i] = [tp]
                    ff["gtt"][i] = [th, tl]

                ff["ugfree"] = [[], []]
                ff["gtt"] = [[], []]

                def outp(b):
                    i = b % 2
                    tok = linear(kout(b), 2, lambda k, t: gT_h[i][:, k, t * P:(t + 1) * P],
                                 lambda k, t: gT_l[i][:, k, t * P:(t + 1) * P], ff["gtt"][i], YB,
                                 first=(b == 0), last=(b == nb - 1))
                    ff["gt"][i] = [tok]
                    return tok

                for b in range(nb):
                    i = b % 2
                    tok = linear(kin(b), KD, lh, ll, toks, [[AB[0]], [AB[1]]], mid=(lambda b=b: spread(b - 1)) if b else None)
                    for t in range(T):
                        ta = act(lambda e, t=t: e.activation(sg[:, t, :], PB[AB[t]][:, 0:256], ACT.Silu), tok, ff["sg"])
                        if combine is None:
                            td = dve(lambda e, t=t: e.tensor_tensor(ug[i][:, t, :], sg[:, t, :], PB[AB[t]][:, 256:512],
                                                                   ALU.mult), ta, ff["ugfree"][i])
                        else:
                            td = dve(lambda e, t=t: e.scalar_tensor_tensor(
                                ug[i][:, t, :], sg[:, t, :], comb[:, t, b:b + 1], PB[AB[t]][:, 256:512],
                                ALU.mult, ALU.mult), ta, ff["ugfree"][i], combine)
                        free[AB[t]] = [ta, td]
                    ff["sg"] = [td]
                    ff["ug"][i] = [td]
                    if b:
                        outp(b - 1)
                    between(b)
                spread(nb - 1)
                return outp(nb - 1)

            x_tok = list(t_x)
            for a in ada_order[:4]:
                ada(*a)
                flush()

            def ffn(i, s):
                sl = i * 3 + 2 * s
                toks = pre(sl)

                def between(b):
                    for a in ADA_AT.get((i, s, b), []):
                        ada(*a)
                tok = ffn_like(NFF, lambda b: ("fi", i, s, b), lambda b: ("fo", i, s, b), toks, between)
                flush()
                post(sl, ypsum2, 0.5, [tok])

            ffn(0, 0)

            at[0] = XN_END
            hp = arena(KD, 272)
            sA, sB = arena(2, 272), arena(2, 272)
            zT = arena(KD, S)
            rc = arena(4, S)
            pbb = arena(D)
            psb = arena(D)
            yp = xn
            t_rc = load(rc, I["rc_c"].rearrange("g n -> (g n)").unsqueeze(0).to_broadcast([P, 4 * S])
                        .rearrange("p (g n) -> p g n", n=S))
            t_pb = load(pbb, I["pool_b"].rearrange("a g n -> a (g n)").to_broadcast([P, D]))
            t_ps = load(psb, I["pool_scale"].to_broadcast([P, D]))
            tz = dve(lambda e: e.memset(hp[:, :, 0:8], 0.0))
            tz = dve(lambda e: e.memset(hp[:, :, 264:272], 0.0))
            KM, VM = kvm[:, 0, :, :], kvm[:, 1, :, :]
            mrow = zT.rearrange("p (a b) c -> p a (b c)", a=T)
            t_mem = load(mrow, I["mem_2"][0].rearrange("(t p) n -> p t n", p=P), x_tok)
            pre(1, keep=hp[:, :, 8:264], split=False)
            tk = prenorm([t_mem], mrow, mrow)
            mtoks = to_T(lambda t, k: mrow[:, t, k * P:(k + 1) * P], KD, hh, hl,
                         scale=lambda k: col("g_mem_2", k), waits=[tk], wdst=[Q.last["tensor"]])
            mtr = [Q.last["tensor"]]
            zt = []
            for g in range(4):
                src = hp[:, 2 * g:2 * g + 2, :]
                n = 272
                for m in range(g + 1):
                    sh = 1 << m
                    n -= sh
                    dst = (sA, sB)[m % 2]
                    dve(lambda e, dst=dst, src=src, n=n, sh=sh: e.tensor_tensor(
                        dst[:, :, 0:n], src[:, :, 0:n], src[:, :, sh:sh + n], ALU.add))
                    src = dst
                o = 8 - (1 << g)
                z = zT[:, 2 * g:2 * g + 2, :]
                dve(lambda e, z=z, src=src, o=o, g=g: e.tensor_tensor(
                    z, src[:, :, o:o + S], rc[:, g:g + 1, :].to_broadcast([P, 2, S]), ALU.mult), t_rc, mtr)
                zt.append(dve(lambda e, z=z, g=g: e.tensor_tensor(z, z, hp[:, 2 * g:2 * g + 2, 8:264], ALU.subtract)))
            tok = linear(("kv",), KD, lh, ll, mtoks, [[4], [5]])
            tok2 = linear(("kv",), KD, lh, ll, mtoks, [[0], [2]])
            for t in range(T):
                tk = act(lambda e: e.activation(KM[:, t, :], PB[4 + t], ACT.Copy), tok)
                free[4 + t] = [tk]
                tk = act(lambda e: e.activation(VM[:, t, :], PB[2 * t], ACT.Copy), tok2)
                free[2 * t] = [tk]
            for a in ada_pool:
                ada(*a)
                flush()
            m, w, dt = take_raw(("pw",))
            for g in range(4):
                for t in range(T):
                    b = YB[t][g // 2]
                    for k in range(2):
                        tp = pe(lambda e, g=g, t=t, k=k, b=b: e.matmul(
                            PB[b][:, (g % 2) * 256:(g % 2) * 256 + 256], zT[:, 2 * g + k, t * P:(t + 1) * P],
                            w[:, 2 * g + k, :], start=(k == 0), stop=(k == 1)), zt[g], dt, free[b])
            give_raw(m, tp)
            for t in range(T):
                for h in range(2):
                    b = YB[t][h]
                    o = yp[:, t, h * 512:(h + 1) * 512]
                    td = dve(lambda e, o=o, b=b, h=h: e.tensor_tensor(o, PB[b][:, :], pbb[:, h * 512:(h + 1) * 512],
                                                                     ALU.add), tp, t_pb)
                    free[b] = [td]
                    tk = dve(lambda e, o=o, h=h: e.tensor_tensor(o, o, psb[:, h * 512:(h + 1) * 512], ALU.mult), t_ps)
            post(1, lambda t: yp[:, t, :], 1.0, [tk], psum=False)

            ffn(0, 1)
            ffn(1, 0)

            def rope(v, n_t, nh, half, cos, sin, tmp, *w, dve=dve):
                x1, x2 = v[:, :, 0:half], v[:, :, half:2 * half]
                c = cos.unsqueeze(1).to_broadcast([P, nh, half])
                s = sin.unsqueeze(1).to_broadcast([P, nh, half])
                a, b = tmp[0], tmp[1]
                a = a[:, 0:nh * half].rearrange("p (h d) -> p h d", d=half)
                b = b[:, 0:nh * half].rearrange("p (h d) -> p h d", d=half)
                dve(lambda e: e.tensor_tensor(a, x2, s, ALU.mult), w)
                dve(lambda e: e.tensor_tensor(b, x1, s, ALU.mult))
                dve(lambda e: e.tensor_tensor(x1, x1, c, ALU.mult))
                dve(lambda e: e.tensor_tensor(x1, x1, a, ALU.subtract))
                dve(lambda e: e.tensor_tensor(x2, x2, c, ALU.mult))
                return dve(lambda e: e.tensor_tensor(x2, x2, b, ALU.add))

            def attention(nh, hd, vd, qrow, krow, kshare, vrow, orow, scale, tq, bufs, mask=None, extra=None):
                qk, pr, pT, sm, mx = bufs
                fq, fp, fpt = [[], []], [[], []], [[], []]
                ex, pt, tS = {}, {}, {}
                kt_of = {}
                sums = st[:, 64:64 + 2 * nh]
                result = []

                cp = {}

                def zero(h):
                    i = h % 2
                    for t in range(T):
                        pe(lambda e, t=t: e.transpose(PB[6][0:hd, t * P:(t + 1) * P], qrow(h, t), ident[:, :]),
                           tq, free[6])
                    for t in range(T):
                        tp = pe(lambda e, t=t: e.transpose(PB[6][0:hd, S + t * P:S + (t + 1) * P], krow(h // kshare, t),
                                                           ident[:, :]))
                    tc = act(lambda e: e.activation(qk[i][0:hd, :], PB[6][0:hd, :], ACT.Copy), tp, fq[i])
                    free[6] = [tc]
                    cp[h] = tc

                def one(h):
                    i = h % 2
                    b = AB[i]
                    tc = cp[h]
                    for t in range(T):
                        ts = pe(lambda e, t=t: e.matmul(PB[b][:, t * S:(t + 1) * S], qk[i][0:hd, t * P:(t + 1) * P],
                                                        qk[i][0:hd, S:2 * S], start=True, stop=True), tc, free[b])
                    fq[i] = [ts]
                    if mask is not None:
                        sv = sm[i].rearrange("p (t n) -> p t n", n=S)
                        tm = dve(lambda e: e.tensor_tensor(sv, PB[b][:, :].rearrange("p (t n) -> p t n", n=S), mask,
                                                           ALU.add), ts)
                        free[b] = [tm]
                    else:
                        sv = PB[b][:, :].rearrange("p (t n) -> p t n", n=S)
                    m2 = mx[:, 2 * i:2 * i + 2]
                    dve(lambda e: e.tensor_reduce(m2, sv, AX_X, ALU.max), ts)
                    tm = dve(lambda e: e.tensor_scalar(m2, m2, -scale, None, ALU.mult))
                    for t in range(T):
                        te = act(lambda e, t=t: e.activation(pr[i][:, t * S:(t + 1) * S], sv[:, t, :], ACT.Exp,
                                                             bias=m2[:, t:t + 1], scale=scale,
                                                             accum_out=sums[:, 2 * h + t:2 * h + t + 1]), tm, fp[i])
                    if mask is None:
                        free[b] = [te]
                    ex[h] = te

                def two(h):
                    i = h % 2
                    for c in range(2):
                        for t in range(T):
                            tp = pe(lambda e, c=c, t=t: e.transpose(
                                PB[7][:, c * S + t * P:c * S + (t + 1) * P], pr[i][:, t * S + c * P:t * S + (c + 1) * P],
                                ident[:, :]), ex[h], free[7])
                    fp[i] = [tp]
                    tc = dve(lambda e: e.tensor_copy(pT[i], PB[7][:, :]), tp, fpt[i])
                    free[7] = [tc]
                    pt[h] = tc

                tlast = [None]

                def three(h):
                    i = h % 2
                    for t in range(T):
                        b = YB[t][h * vd // 512]
                        c0 = h * vd % 512
                        for c in range(2):
                            tlast[0] = pe(lambda e, c=c, t=t, b=b, c0=c0: e.matmul(
                                PB[b][:, c0:c0 + vd], pT[i][:, c * S + t * P:c * S + (t + 1) * P],
                                vrow(c, h // kshare), start=(c == 0), stop=(c == 1)), pt[h], free[b])
                    fpt[i] = [tlast[0]]

                def at_step(h):
                    if extra is not None:
                        extra()
                    if h < nh:
                        zero(h)
                    if 1 <= h <= nh:
                        one(h - 1)
                    if 2 <= h <= nh + 1:
                        two(h - 2)
                    if h >= 3:
                        three(h - 3)

                def finish():
                    rs = st[:, 224:224 + 2 * nh]
                    dve(lambda e: e.reciprocal(rs, sums), ex[nh - 1])
                    rv = rs.rearrange("p (h t) -> p h t", t=2)
                    for t in range(T):
                        for hb in range((nh * vd + 511) // 512):
                            n0 = 512 // vd
                            b = YB[t][hb]
                            tk = dve(lambda e: e.tensor_tensor(
                                orow(t)[:, hb * n0:(hb + 1) * n0, :], PB[b].rearrange("p (h d) -> p h d", d=vd),
                                rv[:, hb * n0:(hb + 1) * n0, t:t + 1].to_broadcast([P, n0, vd]), ALU.mult), tlast[0])
                            free[b] = [tk]
                    result.append(tk)

                for h in range(nh + 3):
                    put_off(2.2 if mask is not None else 1.6, lambda h=h: at_step(h))
                put_off(1.2, finish)
                return result

            at[0] = XN_END
            xf = xn.rearrange("p a b -> p (a b)")
            lat = xf[:, 0:832].rearrange("p (a b) -> p a b", b=416)
            qr = arena(T, 1536)
            kr = arena(T, 1536)
            vr = arena(T, 1024)
            cqT = xf[:, 1024:1536].rearrange("p (a b) -> p a b", b=S)
            ckT = xf[:, 1536:1792]
            ropeC = arena(2, T, 16)
            flat2 = lambda a: a.rearrange("p a b -> p (a b)")
            qk = [flat2(ug[0][:, :, :]), flat2(ug[1][:, :, :])]
            pr = [flat2(sg[:, :, :]), arena(512)]
            pT = [G[0][:, 0:512], G[0][:, 512:1024]]
            orow_a = xn
            tmpA = [qk[0], pr[0]]
            t_rp = load(ropeC, I["rope16_c"].rearrange("p (a t d) -> p a t d", a=2, t=2), x_tok)
            toks = pre(4)
            tok = linear(("mi",), KD, lh, ll, toks, [[AB[0]], [AB[1]]])
            for t in range(T):
                td = dve(lambda e, t=t: e.tensor_copy(lat[:, t, :], PB[AB[t]][:, 0:416]), tok)
                free[AB[t]] = [td]
                for c, (a, n) in enumerate(((0, 256), (256, 128))):
                    ts = act(lambda e, t=t, c=c, a=a, n=n: e.activation(
                        full[:, 1, 0:n], lat[:, t, a:a + n], ACT.Square,
                        accum_out=st[:, 10 + 2 * c + t:11 + 2 * c + t]), td)
            rstd(st[:, 16:18], st[:, 10:12], 256, ts)
            tr = rstd(st[:, 18:20], st[:, 12:14], 128)
            for t in range(T):
                dve(lambda e, t=t: e.tensor_scalar(lat[:, t, 0:256], lat[:, t, 0:256], st[:, 16 + t:17 + t], None, ALU.mult))
                td = dve(lambda e, t=t: e.tensor_scalar(lat[:, t, 256:384], lat[:, t, 256:384], st[:, 18 + t:19 + t], None,
                                                        ALU.mult))
            for k in range(3):
                b = 6 if k < 2 else 7
                for t in range(T):
                    tp = pe(lambda e, k=k, t=t, b=b: e.transpose(
                        PB[b][:, (k % 2) * S + t * P:(k % 2) * S + (t + 1) * P], lat[:, t, k * P:(k + 1) * P],
                        ident[:, :]), td, free[b])
                dst = cqT[:, k, :] if k < 2 else ckT
                g = col("mla_q_norm", k) if k < 2 else col("mla_kv_norm", 0)
                tc = dve(lambda e, dst=dst, g=g, b=b, k=k: e.tensor_scalar(dst, PB[b][:, (k % 2) * S:(k % 2) * S + S], g,
                                                                          None, ALU.mult), tp)
                free[b] = [tc]
            QB = [[0, 1, 4], [2, 3, 5]]
            for k in range(2):
                m, w, dt = take_raw(("uq",))
                for t in range(T):
                    for c in range(3):
                        tp = pe(lambda e, k=k, t=t, c=c, w=w: e.matmul(
                            PB[QB[t][c]][:, :], cqT[:, k, t * P:(t + 1) * P], w[:, 0, c * 512:(c + 1) * 512],
                            start=(k == 0), stop=(k == 1)), dt, tc, free[QB[t][c]])
                give_raw(m, tp)
            for t in range(T):
                for c in range(3):
                    b = QB[t][c]
                    if c % 2:
                        tk = dve(lambda e, t=t, c=c, b=b: e.tensor_copy(qr[:, t, c * 512:(c + 1) * 512], PB[b][:, :]), tp)
                    else:
                        tk = act(lambda e, t=t, c=c, b=b: e.activation(qr[:, t, c * 512:(c + 1) * 512], PB[b][:, :],
                                                                      ACT.Copy), tp)
                    free[b] = [tk]
            ta = Q.last["scalar"]
            krv = kr.rearrange("p t (h d) -> p t h d", d=96)
            qrv = qr.rearrange("p t (h d) -> p t h d", d=96)
            for nm, tgt in (("mla_w_uk", 0), ("mla_w_uv", 1)):
                m, w, dt = take_raw((nm,))
                for t in range(T):
                    for c in range(2):
                        b = YB[t][c]
                        tp = pe(lambda e, t=t, c=c, w=w, b=b: e.matmul(
                            PB[b][:, :], ckT[:, t * P:(t + 1) * P], w[:, 0, c * 512:(c + 1) * 512],
                            start=True, stop=True), dt, tc, free[b])
                        if tgt == 0:
                            tk = act(lambda e, t=t, c=c, b=b: e.activation(
                                krv[:, t, 8 * c:8 * c + 8, 0:64], PB[b][:, :].rearrange("p (h d) -> p h d", d=64),
                                ACT.Copy), tp)
                        else:
                            tk = act(lambda e, t=t, c=c, b=b: e.activation(vr[:, t, c * 512:(c + 1) * 512], PB[b][:, :],
                                                                          ACT.Copy), tp)
                        free[b] = [tk]
                give_raw(m, tp)
            for t in range(T):
                rope(lat[:, t, 384:416].rearrange("p (h d) -> p h d", h=1), T, 1, 16, ropeC[:, 0, t, :], ropeC[:, 1, t, :],
                     tmpA, t_rp)
                dve(lambda e, t=t: e.tensor_copy(krv[:, t, :, 64:96],
                                                 lat[:, t, 384:416].unsqueeze(1).to_broadcast([P, 16, 32])))
                tk2 = rope(qrv[:, t, :, 64:96], T, 16, 16, ropeC[:, 0, t, :], ropeC[:, 1, t, :], tmpA, ta)
            att = attention(16, 96, 64, lambda h, t: qrv[:, t, h, :], lambda h, t: krv[:, t, h, :], 1,
                           lambda c, h: vr[:, c, h * 64:(h + 1) * 64],
                           lambda t: orow_a[:, t, :].rearrange("p (h d) -> p h d", d=64),
                           96 ** -0.5, [tk, tk2], (qk, pr, pT, None, st[:, 96:100]))
            flush()
            wd = [Q.last["tensor"]]
            toks = to_T(lambda t, k: orow_a[:, t, k * P:(k + 1) * P], KD, hh, hl,
                        waits=att, wdst=wd)
            tok = linear(("mo",), KD, lh, ll, toks, YB)
            post(4, ypsum2, 1.0, [tok])

            ffn(1, 1)

            at[0] = XN_END
            QK = arena(T, 19, 64)
            V = arena(T, 128)
            QM = arena(T, 4, 128)
            wi = arena(T, 8)
            gqk = arena(3, 64)
            gqm = arena(2, 128)
            rp32 = arena(2, T, 32)
            cw = arena(4, CONVW)
            uT = arena(4, 286)
            mask = arena(T, S)
            score = arena(T, S)
            pr = [flat2(sg[:, :, :]), arena(512)]
            ga = arena(2, T, 512)
            om = xf[:, 0:1024].rearrange("p (t n) -> p t n", t=T)
            ca = xf[:, 1024:2048].rearrange("p (t n) -> p t n", t=T)
            gm = [G[1].rearrange("p (t n) -> p t n", t=T), ca]
            yc = G[0].rearrange("p (k n) -> p k n", n=S)
            ht = G[2]
            qk = [flat2(ug[0][:, :, :]), flat2(ug[1][:, :, :])]
            pT = [ht[:, 0:512], ht[:, 512:1024]]
            KMv = KM.rearrange("p t (h d) -> p t h d", d=P)
            base = list(x_tok)
            tgn = [load(gqk[:, i:i + 1, :], I[nm].unsqueeze(0).to_broadcast([P, 1, 64]), base)
                   for i, nm in enumerate(("g_qa_2", "g_ka_2", "g_idx_k_2"))]
            tgn += [load(gqm[:, i, :], I[nm].to_broadcast([P, 128]), base) for i, nm in enumerate(("g_qm_2", "g_km_2"))]
            t_rp = load(rp32, I["rope32_c"].rearrange("p (a t d) -> p a t d", a=2, t=2), base)
            t_cm = load(mask, I["cap_c"].rearrange("p (t n) -> p t n", n=S), base)
            cwr = om[0:CONVW, 0, :]
            t_bg = load(adab[0:6, :], I["b_gate_2"].rearrange("a (j n) -> (a j) n", n=512), base)

            tk = prenorm(x_tok)
            toks = to_T(rows_xn, KD, hh, hl, scale=lambda k: col("g_mix_2", k), waits=[tk], wdst=[Q.last["tensor"]])
            t_cw = load(cwr, I["conv_w_2"][0].rearrange("j a n -> j (a n)"), Q.last["tensor"])
            tz = dve(lambda e: e.memset(uT[:, :, 0:30], 0.0), base)

            def norm_steps(v, nh, hd, gains, waits):
                ss, rr = st[:, 20:20 + 2 * nh], st[:, 42:42 + 2 * nh]

                def squares(t):
                    tmp = ht[:, 0:nh * hd].rearrange("p (h d) -> p h d", d=hd)
                    dve(lambda e: e.tensor_tensor(tmp, v(t), v(t), ALU.mult), waits)
                    dve(lambda e: e.tensor_reduce(ss[:, t * nh:(t + 1) * nh], tmp, AX_X, ALU.add))

                def scaled(t):
                    dve(lambda e: e.tensor_tensor(v(t), v(t), rr[:, t * nh:(t + 1) * nh].unsqueeze(2)
                                                  .to_broadcast([P, nh, hd]), ALU.mult))

                def gained(t, a, n, g):
                    dve(lambda e: e.tensor_tensor(v(t)[:, a:a + n, :], v(t)[:, a:a + n, :],
                                                  g.to_broadcast([P, n, hd]), ALU.mult), tgn)

                for t in range(T):
                    put_off(nh * hd * 2.1e-3, lambda t=t: squares(t))
                put_off(1.5, lambda: rstd(rr, ss, hd))
                for t in range(T):
                    put_off(nh * hd * 1.1e-3, lambda t=t: scaled(t))
                    for a, n, g in gains:
                        put_off(n * hd * 1.1e-3, lambda t=t, a=a, n=n, g=g: gained(t, a, n, g))

            rope_tok = {}

            def rope_steps(key, a, n, waits):
                for t in range(T):
                    def go(t=t):
                        rope_tok[key, t] = rope(QK[:, t, a:a + n, :], T, n, 32, rp32[:, 0, t, :], rp32[:, 1, t, :],
                                                [ht[:, 0:512], ht[:, 512:1024]], t_rp, waits)
                    put_off(n * 0.22, go)

            fqk = [[], []]
            ix = {}

            def ix_copy(h):
                i = h % 2
                src = (lambda t: QK[:, t, 10, :]) if h < 0 else (lambda t: QK[:, t, 11 + h, :])
                dst = pr[0][0:64, 0:S] if h < 0 else qk[i][0:64, 0:S]
                for t in range(T):
                    tp = pe(lambda e: e.transpose(PB[6][0:64, t * P:(t + 1) * P], src(t), ident[:, :]),
                            free[6], [rope_tok[k] for k in rope_tok])
                ix[h] = act(lambda e: e.activation(dst, PB[6][0:64, 0:S], ACT.Copy), tp, fqk[i] if h >= 0 else [])
                free[6] = [ix[h]]

            def ix_score(h):
                i, b = h % 2, AB[h % 2]
                for t in range(T):
                    ts = pe(lambda e: e.matmul(PB[b][:, t * S:(t + 1) * S], qk[i][0:64, t * P:(t + 1) * P],
                                               pr[0][0:64, 0:S], start=True, stop=True), ix[h], ix[-1], free[b])
                fqk[i] = [ts]
                rl = pT[h % 2].rearrange("p (t n) -> p t n", n=S)
                ta = act(lambda e: e.activation(pT[h % 2], PB[b], ACT.Relu, scale=0.125), ts, ix.get(("d", h - 2)),
                         Q.last["vector"] if h < 2 else [])
                free[b] = [ta]
                for t in range(T):
                    if h == 0:
                        td = dve(lambda e: e.tensor_scalar(score[:, t, :], rl[:, t, :], wi[:, t, 0:1], None,
                                                           ALU.mult), ta)
                    else:
                        td = dve(lambda e: e.scalar_tensor_tensor(
                            score[:, t, :], rl[:, t, :], wi[:, t, h:h + 1], score[:, t, :], ALU.mult, ALU.add), ta)
                ix["d", h] = td

            def index_steps():
                put_off(0.0, lambda: ix_copy(-1))
                for h in range(9):
                    def go(h=h):
                        if h < 8:
                            ix_copy(h)
                        if h >= 1:
                            ix_score(h - 1)
                    put_off(0.8, go)
                put_off(0.6, lambda: dve(lambda e: e.tensor_tensor(score, score, mask, ALU.min), t_cm))
                for r in range(8):
                    for t in range(T):
                        def mark(t=t):
                            m8 = st[:, 260 + 8 * t:268 + 8 * t]
                            dve(lambda e: e.max(m8, score[:, t, :]))
                            dve(lambda e: e.match_replace(score[:, t, :], m8, score[:, t, :], MARK))
                        put_off(0.8, mark)

                def to_mask():
                    dve(lambda e: e.tensor_scalar(score, score, MARK, None, ALU.is_equal))
                    dve(lambda e: e.scalar_tensor_tensor(mask, mask, 0.0, score, ALU.is_gt, ALU.mult))
                    ix["mask"] = dve(lambda e: e.tensor_scalar(mask, mask, -1.0, -NEG, ALU.add, ALU.mult))
                put_off(1.4, to_mask)

            def conv_taps(k, j):
                y, u, w = yc[:, k, :], uT[:, k, j:j + S], cw[:, k, j:j + 1]
                if j == 0:
                    return dve(lambda e: e.tensor_scalar(y, u, w, col("conv_b_2", k), ALU.mult, ALU.add), t_uT)
                return dve(lambda e: e.scalar_tensor_tensor(y, u, w, y, ALU.mult, ALU.add))

            fill = []

            def filler(n):
                for _ in range(n):
                    if fill:
                        conv_done[0] = conv_taps(*fill.pop(0))

            conv_done = [None]

            lbh = lambda k, t: bh[:, k, t * P:(t + 1) * P]
            lbl = lambda k, t: bl[:, k, t * P:(t + 1) * P]
            pairs = [(1, 3), (0, 2)]
            f64 = lambda a: a.rearrange("p (h d) -> p h d", d=64)
            conv_tr = []

            def conv_transposes():
                for k in range(4):
                    tp = pe(lambda e: e.transpose(PB[7][:, k * 32:k * 32 + CONVW], cwr[:, k * P:(k + 1) * P],
                                                  ident[0:CONVW, 0:CONVW]), t_cw, free[7])
                tc = dve(lambda e: e.tensor_copy(cw, PB[7][:, 0:128].rearrange("p (k j) -> p k j", j=32)[:, :, 0:CONVW]),
                         tp)
                free[7] = [tc]
                tcw = tc
                for k0 in (0, 2):
                    b = 6 if k0 else 5
                    for k in range(2):
                        for t in range(T):
                            tp = pe(lambda e: e.transpose(
                                PB[b][:, k * S + t * P:k * S + (t + 1) * P], ca[:, t, (k0 + k) * P:(k0 + k + 1) * P],
                                ident[:, :]), t_u, free[b])
                    tc = act(lambda e: e.activation(
                        uT[:, k0:k0 + 2, 30:286], PB[b].rearrange("p (k n) -> p k n", n=S), ACT.Copy), tp, tz)
                    free[b] = [tc]
                return [tc, tcw]

            t_uT, fill_rate = [], [0]
            for n_, (c0, n) in enumerate(PROJ):
                b0, b1 = pairs[n_ % 2]
                def go_conv():
                    t_uT.append(conv_transposes())
                    fill[:] = [(k, j) for j in range(CONVW) for k in range(4)]
                mid = go_conv if n_ == 3 else None
                tok = linear(("pj",), KD, lh, ll, toks, [[b0], [b1]], mid=mid)
                for t, b in ((0, b0), (1, b1)):
                    src = PB[b]
                    if n_ == 0:
                        tk = act(lambda e: e.activation(ca[:, t, :], src, ACT.Copy), tok)
                    elif n_ == 1:
                        tk = act(lambda e: e.activation(full[:, t, :], src, ACT.Sigmoid), tok)
                        t_u = dve(lambda e: e.tensor_tensor(ca[:, t, :], ca[:, t, :], full[:, t, :], ALU.mult), tk)
                    elif n_ == 2:
                        act(lambda e: e.activation(QK[:, t, 10, :], src[:, 0:64], ACT.Copy), tok, base)
                        tk = act(lambda e: e.activation(wi[:, t, :], src[:, 64:72], ACT.Copy, scale=8 ** -0.5), tok)
                    elif n_ == 3:
                        tk = act(lambda e: e.activation(QK[:, t, 11:19, :], f64(src), ACT.Copy), tok)
                    elif n_ == 4:
                        tk = act(lambda e: e.activation(QK[:, t, 0:8, :], f64(src), ACT.Copy), tok)
                    elif n_ == 5:
                        act(lambda e: e.activation(QK[:, t, 8:10, :], f64(src[:, 0:128]), ACT.Copy), tok)
                        tk = act(lambda e: e.activation(V[:, t, :], src[:, 128:256], ACT.Copy), tok)
                    else:
                        tk = act(lambda e: e.activation(QM[:, t, :, :], src.rearrange("p (h d) -> p h d", d=128),
                                                        ACT.Copy), tok)
                    free[b] = [tk]
                if n_ == 2:
                    norm_steps(lambda t: QK[:, t, 10:11, :], 1, 64, [(0, 1, gqk[:, 2:3, :])], tk)
                    rope_steps("ki", 10, 1, [])
                elif n_ == 3:
                    rope_steps("qi", 11, 8, tk)
                    index_steps()
                elif n_ == 5:
                    norm_steps(lambda t: QK[:, t, 0:10, :], 10, 64, [(0, 8, gqk[:, 0:1, :]), (8, 2, gqk[:, 1:2, :])], tk)
                    rope_steps("qa", 0, 10, [])

                    def go():
                        ix["att"] = attention(
                            8, 64, 64, lambda h, t: QK[:, t, h, :], lambda h, t: QK[:, t, 8 + h, :], 4,
                            lambda c, h: V[:, c, h * 64:(h + 1) * 64],
                            lambda t: om[:, t, :].rearrange("p (h d) -> p h d", d=64),
                            0.125, [ix["mask"], rope_tok["qa", 1]],
                            (qk, pr, pT, [full[:, 0, :], full[:, 1, :]], st[:, 96:100]), mask=mask, extra=lambda: filler(2))
                        put_mark("att")
                    put_off(0.0, go)
            tqm = tk

            def gates(j, bank, dst, tb=None):
                for b in bank:
                    pe(lambda e: e.matmul(PB[b], ident[0:6, j:j + 1].to_broadcast([6, P]), adab[0:6, :],
                                          start=True, stop=False), free[b], t_bg)
                tok = linear(("gt",), KD, lh, ll, toks, [[b] for b in bank], first=False)
                tks = []
                for t, b in enumerate(bank):
                    ta = act(lambda e: e.activation(dst(t), PB[b], ACT.Sigmoid), tok)
                    free[b] = [ta]
                    tks.append(ta)
                return tks

            tg = {}
            for c in range(2):
                tg[0, c] = gates(c, (1, 3), lambda t: ga[:, c, t, :])
            for c in range(2):
                tg[2, c] = gates(4 + c, (1, 3), lambda t: gm[c][:, t, :])
            flush("att")
            btoks = to_T(lambda t, k: om[:, t, k * P:(k + 1) * P], 4, bh, bl, waits=ix["att"],
                         wdst=[Q.last["tensor"]])
            norm_steps(lambda t: QM[:, t, :, :], 4, 128, [(0, 4, gqm[:, 0:1, :])], tqm)
            norm_steps(lambda t: KMv[:, t, :, :], 4, 128, [(0, 4, gqm[:, 1:2, :])], base)

            def go_m():
                ix["mem"] = attention(
                    4, 128, 128, lambda h, t: QM[:, t, h, :], lambda h, t: KMv[:, t, h, :], 1,
                    lambda c, h: VM[:, c, h * 128:(h + 1) * 128],
                    lambda t: om[:, t, :].rearrange("p (h d) -> p h d", d=128),
                    128 ** -0.5, [Q.last["vector"]], (qk, pr, pT, None, st[:, 96:100]), extra=lambda: filler(3))
                put_mark("mem")
            put_off(0.0, go_m)
            gc = QK.rearrange("p t a b -> p (t a b)")[:, 0:2048].rearrange("p (c t n) -> p c t n", c=2, t=T)
            for c in range(2):
                tg[1, c] = gates(2 + c, (1, 3), lambda t: gc[:, c, t, :])
            flush("mem")

            def branch(btoks, g, gt):
                tb = linear(("br",), 4, lbh, lbl, btoks, YB)
                tks = []
                for c in range(2):
                    for t in range(T):
                        b = YB[t][c]
                        o = gt(c, t)
                        tk = dve(lambda e: e.tensor_tensor(o, o, PB[b], ALU.mult), tg[g, c], tb)
                        free[b] = [tk]
                        if g != 0:
                            tk = dve(lambda e: e.tensor_tensor(ga[:, c, t, :], ga[:, c, t, :], o, ALU.add))
                        filler(1)
                return tk

            fill_rate[0] = 3
            after_unit[0] = lambda: filler(fill_rate[0])
            branch(btoks, 0, lambda c, t: ga[:, c, t, :])
            btoks = to_T(lambda t, k: om[:, t, k * P:(k + 1) * P], 4, bh, bl, waits=ix["mem"],
                         wdst=[Q.last["tensor"]])
            branch(btoks, 2, lambda c, t: gm[c][:, t, :])
            filler(999)
            fill_rate[0] = 0
            tcv = [conv_done[0], Q.last["vector"]]

            for k0 in range(4):
                for t in range(T):
                    tp = pe(lambda e: e.transpose(PB[6 + t][:, k0 * P:(k0 + 1) * P], yc[:, k0, t * P:(t + 1) * P],
                                                  ident[:, :]), tcv, free[6 + t])
            for t in range(T):
                s6, s2 = st[:, 20 + 8 * t:26 + 8 * t], st[:, 40 + 2 * t:42 + 2 * t]
                dve(lambda e: e.bn_stats(s6, PB[6 + t]), tp)
                dve(lambda e: e.bn_aggr(s2, s6))
                dve(lambda e: e.tensor_copy(st[:, 50 + t:51 + t], s2[:, 1:2]))
            rstd(st[:, 52:54], st[:, 50:52], 1)
            for t in range(T):
                tk = dve(lambda e: e.tensor_scalar(om[:, t, :], PB[6 + t], st[:, 40 + 2 * t:41 + 2 * t],
                                                   st[:, 52 + t:53 + t], ALU.subtract, ALU.mult),
                         Q.last["tensor"])
                free[6 + t] = [tk]
            btoks = to_T(lambda t, k: om[:, t, k * P:(k + 1) * P], 4, bh, bl, scale=lambda k: col("ln_g_2", k),
                         bias=lambda k: col("ln_b_2", k), func=ACT.Silu, waits=[tk], wdst=[Q.last["tensor"], tk])
            tk = branch(btoks, 1, lambda c, t: gc[:, c, t, :])
            toks = to_T(lambda t, k: ga[:, k // 4, t, (k % 4) * P:(k % 4 + 1) * P], KD, hh, hl,
                        waits=[tk], wdst=[Q.last["tensor"]])
            tok = linear(("wo",), KD, lh, ll, toks, YB)
            for t in range(T):
                for h in range(2):
                    xs = x[:, t, h * 512:(h + 1) * 512]
                    tk = dve(lambda e, xs=xs, t=t, h=h: e.tensor_tensor(xs, xs, ypsum(t, h), ALU.add), tok)
                    free[YB[t][h]] = [tk]
            x_tok[:] = [tk]

            at[0] = XN_END
            hf = arena(KD, S)
            wr = arena(KD, 36)
            rbias = arena(36)
            tw = [load(wr[:, :, 0:4], I["w_rg_2"][0].rearrange("(k p) n -> p k n", p=P), x_tok),
                  load(wr[:, :, 4:36], I["w_re_2"][0].rearrange("(k p) n -> p k n", p=P), x_tok),
                  load(rbias[:, 0:4], I["b_rg_2"].to_broadcast([P, 4]), x_tok),
                  load(rbias[:, 4:36], I["b_re_2"].to_broadcast([P, 32]), x_tok)]
            tie = arena(8)
            tw.append(load(tie, I["tie_c"].to_broadcast([P, 8]), x_tok))
            lg = arena(T, 36)
            sm_ = arena(T, 128)
            tk = prenorm(x_tok)
            toks = to_T(rows_xn, KD, hh, hl, scale=lambda k: col("g_ffn_2", k),
                        keep=hf, waits=[tk], wdst=[Q.last["tensor"], tk])
            for t in range(T):
                for k in range(KD):
                    tp = pe(lambda e, t=t, k=k: e.matmul(PB[7][:, t * 64:t * 64 + 36], hf[:, k, t * P:(t + 1) * P],
                                                         wr[:, k, :], start=(k == 0), stop=(k == KD - 1)),
                            toks[k], tw, free[7])
            for t in range(T):
                L = lg[:, t, :]
                z = sm_[:, t, :]
                dve(lambda e, t=t, L=L: e.tensor_tensor(L, PB[7][:, t * 64:t * 64 + 36], rbias, ALU.add), tp)
                gl, el = L[:, 0:4], L[:, 4:36].rearrange("p (g e) -> p g e", e=8)
                gmx, ngm, oh, gs, gr = z[:, 0:1], z[:, 1:2], z[:, 4:8], z[:, 2:3], z[:, 3:4]
                dve(lambda e, gl=gl, gmx=gmx: e.tensor_reduce(gmx, gl, AX_X, ALU.max))
                tn = dve(lambda e, gmx=gmx, ngm=ngm: e.tensor_scalar(ngm, gmx, -1.0, None, ALU.mult))
                ta = act(lambda e, gl=gl, ngm=ngm, gs=gs, z=z: e.activation(z[:, 8:12], gl, ACT.Exp, bias=ngm, scale=1.0,
                                                                       accum_out=gs), tn)
                dve(lambda e, gr=gr, gs=gs: e.reciprocal(gr, gs), ta)

                def first_of(dst, v, mx, n, tmp):
                    dve(lambda e: e.scalar_tensor_tensor(dst, v, mx, tie[:, 8 - n:8], ALU.is_equal, ALU.mult), tw)
                    dve(lambda e: e.tensor_reduce(tmp, dst, AX_X, ALU.max))
                    return dve(lambda e: e.tensor_scalar(dst, dst, tmp, None, ALU.is_equal))

                first_of(oh, gl, gmx, 4, z[:, 12:13])
                ein = z[:, 16:24]
                pe_ = z[:, 32:64].rearrange("p (g e) -> p g e", e=8)
                dve(lambda e, pe_=pe_, el=el, oh=oh: e.tensor_tensor(pe_, el, oh.unsqueeze(2).to_broadcast([P, 4, 8]),
                                                                     ALU.mult))
                dve(lambda e, pe_=pe_, ein=ein: e.tensor_reduce(ein, pe_.rearrange("p g e -> p e g"), AX_X, ALU.add))
                v8 = z[:, 64:72]
                dve(lambda e, v8=v8, ein=ein: e.max(v8, ein))
                o1, o2, e2 = z[:, 72:80], z[:, 80:88], z[:, 88:96]
                first_of(o1, ein, v8[:, 0:1], 8, z[:, 12:13])
                dve(lambda e, e2=e2, o1=o1, ein=ein: e.scalar_tensor_tensor(e2, o1, MARK, ein, ALU.mult, ALU.add))
                first_of(o2, e2, v8[:, 1:2], 8, z[:, 12:13])
                dv, ez, w1, w2 = z[:, 96:97], z[:, 97:98], z[:, 98:99], z[:, 99:100]
                tn = dve(lambda e, dv=dv, v8=v8: e.tensor_tensor(dv, v8[:, 1:2], v8[:, 0:1], ALU.subtract))
                ta = act(lambda e, ez=ez, dv=dv: e.activation(ez, dv, ACT.Exp), tn)
                dve(lambda e, w1=w1, ez=ez: e.tensor_scalar(w1, ez, 1.0, None, ALU.add), ta)
                dve(lambda e, w1=w1: e.reciprocal(w1, w1))
                dve(lambda e, w1=w1, gr=gr: e.tensor_tensor(w1, w1, gr, ALU.mult))
                dve(lambda e, w2=w2, w1=w1, ez=ez: e.tensor_tensor(w2, w1, ez, ALU.mult))
                dve(lambda e, o1=o1, w1=w1: e.tensor_scalar(o1, o1, w1, None, ALU.mult))
                dve(lambda e, o1=o1, o2=o2, w2=w2: e.scalar_tensor_tensor(o1, o2, w2, o1, ALU.mult, ALU.add))
                cv = comb[:, t, :].rearrange("p (g e) -> p g e", e=8)
                tcb = dve(lambda e, cv=cv, o1=o1, oh=oh: e.tensor_tensor(
                    cv, o1.unsqueeze(1).to_broadcast([P, 4, 8]), oh.unsqueeze(2).to_broadcast([P, 4, 8]), ALU.mult))
            free[7] = [tcb]
            tok = ffn_like(32, lambda b: ("mu", b), lambda b: ("md", b), toks, lambda b: None, combine=tcb)
            outs = []
            for t in range(T):
                for h in range(2):
                    xs = x[:, t, h * 512:(h + 1) * 512]
                    tk = dve(lambda e, xs=xs, t=t, h=h: e.tensor_tensor(xs, xs, ypsum(t, h), ALU.add), tok)
                outs.append(load(out_ap[0, t * P:(t + 1) * P, :], x[:, t, :], tk, q="sync"))
            if Q.active in (None, "sync"):
                Q.wait(outs)
            assert cpos[0] == len(chunks), (cpos, len(chunks))

        flow()
        Q.counted()
        block = ctx.enter_context(nc.Block())

        def emit(name):
            def body(eng):
                Q.begin(name, eng)
                flow()
            return body

        block.tensor(emit("tensor"))
        block.vector(emit("vector"))
        block.scalar(emit("scalar"))
        block.gpsimd(emit("gpsimd"))
        block.sync(emit("sync"))


_INS = ["x", "c", "ada_w", "ada_b", "norm_g", "ffn_w_in", "ffn_w_out", "pool_w", "pool_b", "pool_scale",
        "mla_w_in", "mla_q_norm", "mla_kv_norm", "mla_w_uq", "mla_w_uk", "mla_w_uv", "mla_w_o", "mem_2",
        "g_mix_2", "w_in_2", "b_gate_2", "g_qa_2", "g_ka_2", "g_idx_k_2", "conv_w_2", "conv_b_2", "ln_g_2",
        "ln_b_2", "g_mem_2", "w_mem_kv_2", "g_qm_2", "g_km_2", "w_br_a_2", "w_br_b_2", "w_br_m_2", "w_o_2",
        "g_ffn_2", "w_rg_2", "b_rg_2", "w_re_2", "b_re_2", "w_up_2", "w_down_2"]


def _constants():
    f = np.float32
    out = {"ident_c": np.eye(P, dtype=f)}
    out["sum4_c"] = np.tile((np.arange(P) % 32 == 0).astype(f)[:, None], (1, P))
    t = np.arange(S)
    rc = []
    for w in (2, 4, 8, 16):
        n = np.clip(t + w // 2, 0, S) - np.clip(t - w // 2, 0, S)
        rc.append(1.0 / n)
    out["rc_c"] = np.asarray(rc, dtype=f)
    for half, name in ((16, "rope16_c"), (32, "rope32_c")):
        inv = (10000.0 ** (-(np.arange(half, dtype=f) / f(half)))).astype(f)
        ang = (t.astype(f)[:, None] * inv[None, :]).astype(f).astype(np.float64)
        cs = np.stack([np.cos(ang), np.sin(ang)])
        out[name] = np.ascontiguousarray(cs.reshape(2, T, P, half).transpose(2, 0, 1, 3).reshape(P, -1)).astype(f)
    ca = (t[None, :] <= t[:, None]).astype(f)
    ca = np.where(ca > 0, f(3e38), f(NEG))
    out["cap_c"] = np.ascontiguousarray(ca.reshape(T, P, S).transpose(1, 0, 2).reshape(P, -1))
    out["tie_c"] = np.arange(8, 0, -1).astype(f)[None, :]
    return out


def kernel(**inputs):
    import numpy as _np
    import concourse.bacc as _bacc
    from concourse import mybir as _mybir
    from concourse.bass_utils import run_bass_kernel_spmd as _run

    nc = _bacc.Bacc("TRN2", target_bir_lowering=False, num_devices=1)
    arrays, aps = {}, {}
    named = {n: _np.ascontiguousarray(inputs[n]) for n in _INS}
    named.update(_constants())
    for name, a in named.items():
        arrays[f"in_{name}"] = a
        aps[name] = nc.dram_tensor(f"in_{name}", a.shape, _mybir.dt.from_np(a.dtype), kind="ExternalInput").ap()
    out = nc.dram_tensor("out_0", (1, S, D), F32, kind="ExternalOutput").ap()
    build(nc, aps, out)
    r = _run(nc, [arrays], core_ids=[0])
    return r.results[0]["out_0"]
```

```python
from contextlib import ExitStack

import numpy as np

import concourse.bass as bass
from concourse import mybir

F32 = mybir.dt.float32
F32R = mybir.dt.float32r
I32 = mybir.dt.int32
ACT = mybir.ActivationFunctionType
ALU = mybir.AluOpType
AX_X = mybir.AxisListType.X

P = 128
T = 2
S = 256
D = 1024
KD = D // P
EPS = 1e-6
F2 = 2816
CHUNK = 2048
UNIT = 1024
NRAW = 6
NUNIT = 6
NFF = 11
ARENA = 11460
NEG = -1e30
MARK = -3e38
PROJ = [(1352, 512), (1864, 512), (1280, 72), (768, 512), (0, 512), (512, 256), (2376, 512)]
GATE0 = 2888
CONVW = 31


class Tok:

    def __init__(self, queue, index, sem, value):
        self.queue, self.index, self.sem, self.value = queue, index, sem, value


class Queues:

    NAMES = ("tensor", "vector", "scalar", "gpsimd", "sync")

    def __init__(self, sems):
        self.sems = sems
        self.wanted = {n: set() for n in self.NAMES}
        self.values = {}
        self.begin(None, None)

    def begin(self, name, eng):
        self.active, self.eng = name, eng
        self.at = {n: 0 for n in self.NAMES}
        self.last, self.seen = {}, {}

    def counted(self):
        for n in self.NAMES:
            self.values[n] = {index: k + 1 for k, index in enumerate(sorted(self.wanted[n]))}

    def wait(self, waits):
        if self.active is None:
            for w in waits:
                if w.queue is not None:
                    self.wanted[w.queue].add(w.index)
            return
        need = {}
        for w in waits:
            if w.value > self.seen.get(w.sem.name, 0):
                if w.sem.name not in need or w.value > need[w.sem.name].value:
                    need[w.sem.name] = w
        for key, w in need.items():
            self.eng.wait_ge(w.sem, w.value)
            self.seen[key] = w.value

    def put(self, name, fn, waits, own=True):
        index = self.at[name]
        self.at[name] += 1
        waits = flat(waits)
        if own and name in self.last and name != "tensor":
            waits.append(self.last[name])
        value = self.values[name].get(index) if self.values else None
        tok = Tok(name, index, self.sems[name], value)
        self.last[name] = tok
        if self.active in (None, name):
            self.wait(waits)
        if self.active == name:
            ins = fn(self.eng)
            if value is not None:
                ins.then_inc(tok.sem, 1)
        return tok

    def dma(self, name, fn, waits, sem, value):
        if self.active in (None, name):
            self.wait(flat(waits))
        if self.active == name:
            fn(self.eng).then_inc(sem, 16)
        return Tok(None, None, sem, value)


def flat(x):
    if x is None:
        return []
    if isinstance(x, Tok):
        return [x]
    return [t for y in x for t in flat(y)]


def build(nc, I, out_ap):
    ctx = ExitStack()
    with ctx:
        def sb(name, shape, dt=F32):
            return ctx.enter_context(nc.sbuf_tensor(name, shape, dt))

        named = {}

        def sem(name):
            if name not in named:
                named[name] = ctx.enter_context(nc.semaphore(name))
            return named[name]

        Q = Queues({n: sem(f"done_{n}") for n in Queues.NAMES})

        def pe(fn, *w):
            return Q.put("tensor", fn, w)

        def dve(fn, *w, own=True):
            return Q.put("vector", fn, w, own)

        def act(fn, *w, own=True):
            return Q.put("scalar", fn, w, own)

        def pool(fn, *w, own=True):
            return Q.put("gpsimd", fn, w, own)

        PS = ctx.enter_context(nc.psum_tensor("banks", [P, 8, 512], F32))
        PB = [PS[:, i, :] for i in range(8)]
        YB = [[0, 1], [2, 3]]
        AB = [4, 5]

        raw = [sb(f"raw{i}", [P, CHUNK]) for i in range(NRAW)]
        uh = [sb(f"uh{i}", [P, UNIT], F32R) for i in range(NUNIT)]
        ul = [sb(f"ul{i}", [P, UNIT], F32R) for i in range(NUNIT)]
        ident = sb("ident", [P, P])
        x = sb("x", [P, T, D])
        hh = sb("hh", [P, KD, S], F32R)
        hl = sb("hl", [P, KD, S], F32R)
        Gs = sb("Gs", [P, 3, D])
        G = [Gs[:, i, :] for i in range(3)]
        bh = sb("bh", [P, 4, S], F32R)
        bl = sb("bl", [P, 4, S], F32R)
        gT_h = [bh[:, 2 * i:2 * i + 2, :] for i in range(2)]
        gT_l = [bl[:, 2 * i:2 * i + 2, :] for i in range(2)]
        sg = sb("sg", [P, T, 256])
        ug = [sb(f"ug{i}", [P, T, 256]) for i in range(2)]
        full = sb("full", [P, 2, 512])
        ab = sb("ab", [P, 6, 2, KD])
        ngc = sb("ngc", [P, 96])
        cc = sb("cc", [P, 48])
        sc = sb("sc", [P, KD])
        st = sb("st", [P, 280])
        flag = st[:, 276:278].bitcast(I32)
        comb = Gs[:, 0, 0:64].rearrange("p (t n) -> p t n", t=T)
        AR = sb("arena", [P, ARENA])
        adab = sb("adab", [P, 512])
        kvm = sb("kvm", [P, 2, T, 512])
        sum4 = sb("sum4", [P, P])

        def flow():
            free = {i: [] for i in range(8)}
            at = [0]

            def arena(*shape):
                n = int(np.prod(shape))
                a = AR[:, at[0]:at[0] + n]
                at[0] += n
                assert at[0] <= ARENA, at[0]
                if len(shape) == 2:
                    a = a.rearrange("p (a b) -> p a b", b=shape[1])
                elif len(shape) == 3:
                    a = a.rearrange("p (a b c) -> p a b c", b=shape[1], c=shape[2])
                return a

            chunks = []

            def plan_rows(key, w, k0, kk, c0, n, conv=True):
                v = w.rearrange("(k p) n -> p k n", p=P)[:, k0:k0 + kk, c0:c0 + n]
                chunks.append((key, [(v, kk, n, 0)], kk, n, conv))

            def plan_block(key, w, c0, n, K=KD):
                for k0 in range(0, K, 4):
                    plan_rows(key, w, k0, 4, c0, n)

            def plan_wide(key, w, r0):
                v = w[r0:r0 + 256, :].rearrange("(k p) n -> p k n", p=P)
                chunks.append((key, [(v, 2, D, 0)], 2, D, True))

            def plan_ffn_block(key, i, s, b):
                w = I["ffn_w_in"][i, s].rearrange("(k p) (g n) -> p k g n", p=P, g=2)
                for k0 in (0, 4):
                    pcs = [(w[:, k0:k0 + 4, g, b * 256:(b + 1) * 256], 4, 512, g * 256) for g in (0, 1)]
                    chunks.append((key, pcs, 4, 512, True))

            def plan_ada(i, j):
                w = I["ada_w"][i]
                for k0 in (0, 4):
                    plan_rows(("ada", i, j), w, k0, 4, j * 512, 512, conv=False)

            ada_order = [(i, j) for i in range(2) for j in range(18)]
            ADA_AT, at_ = {}, 4
            for i_, s_, n_ in ((0, 0, 11), (0, 1, 11), (1, 0, 7)):
                for b_ in range(n_):
                    ADA_AT[(i_, s_, b_)] = ada_order[at_:at_ + 1]
                    at_ += 1
                if at_ == 15:
                    ada_pool = ada_order[15:18]
                    at_ = 18

            def plan_ffn(i, s):
                for b in range(NFF):
                    plan_ffn_block(("fi", i, s, b), i, s, b)
                    if b:
                        plan_wide(("fo", i, s, b - 1), I["ffn_w_out"][i, s], (b - 1) * 256)
                    for a in ADA_AT.get((i, s, b), []):
                        plan_ada(*a)
                plan_wide(("fo", i, s, NFF - 1), I["ffn_w_out"][i, s], (NFF - 1) * 256)

            for a in ada_order[:4]:
                plan_ada(*a)
            plan_ffn(0, 0)
            for b in range(2):
                plan_block(("kv",), I["w_mem_kv_2"][0], b * 512, 512)
            for a in ada_pool:
                plan_ada(*a)
            chunks.append((("pw",), [(I["pool_w"][0].rearrange("g (k p) n -> p (g k) n", p=P), 8, 256, 0)], 8, 256, False))
            plan_ffn(0, 1)
            plan_ffn(1, 0)
            plan_block(("mi",), I["mla_w_in"][0], 0, 416)
            for k in range(2):
                v = I["mla_w_uq"][0].rearrange("(k p) h d -> p k (h d)", p=P)[:, k:k + 1, :]
                chunks.append((("uq",), [(v, 1, 1536, 0)], 1, 1536, False))
            for nm in ("mla_w_uk", "mla_w_uv"):
                v = I[nm].rearrange("a c h d -> c a (h d)")
                chunks.append(((nm,), [(v, 1, 1024, 0)], 1, 1024, False))
            for k in range(4):
                plan_wide(("mo",), I["mla_w_o"][0], k * 256)
            plan_ffn(1, 1)
            for c0, n in PROJ:
                plan_block(("pj",), I["w_in_2"][0], c0, n)
            for g in (0, 2, 1):
                for c in range(2):
                    plan_block(("gt",), I["w_in_2"][0], GATE0 + g * 1024 + c * 512, 512)
            for nm in ("w_br_a_2", "w_br_m_2", "w_br_b_2"):
                for k in range(2):
                    plan_wide(("br",), I[nm][0], k * 256)
            for k in range(4):
                plan_wide(("wo",), I["w_o_2"][0], k * 256)
            limit = [0]
            for _ in range(2):
                for b in range(32):
                    plan_block(("mu", b), I["w_up_2"][0, b], 0, 512)
                    if b:
                        plan_wide(("md", b - 1), I["w_down_2"][0, b - 1], 0)
                plan_wide(("md", 31), I["w_down_2"][0, 31], 0)
                limit[0] = limit[0] or len(chunks)

            ring_sem = [sem(f"ring{i}") for i in range(NRAW)]
            dma_tok, chunk_rel = {}, {}
            nxt = [0]

            def pump():
                while nxt[0] < limit[0] and (nxt[0] < NRAW or nxt[0] - NRAW in chunk_rel):
                    m = nxt[0]
                    key, pcs, kk, n, conv = chunks[m]
                    waits = chunk_rel[m - NRAW] if m >= NRAW else []
                    slot = raw[m % NRAW][:, 0:kk * n].rearrange("p (k n) -> p k n", n=n)
                    base = fills[m % NRAW]
                    for v, k_, n_, c0 in pcs:
                        w = v.shape[-1]
                        base += 16
                        tok = Q.dma("sync", lambda e, d=slot[:, :, c0:c0 + w], v=v: e.dma_start(d, v), waits,
                                    ring_sem[m % NRAW], base)
                    fills[m % NRAW] = base
                    dma_tok[m] = tok
                    nxt[0] += 1

            fills = [0] * NRAW
            units = []
            for m, (key, pcs, kk, n, conv) in enumerate(chunks):
                if conv:
                    for h in range(2):
                        units.append((m, h, kk // 2, n))
            unit_rel, unit_tok = {}, {}
            cpos, upos, conv_pos = [0], [0], [0]
            pump()

            def convert(u):
                m, h, kk, n = units[u]
                w = kk * n
                src = raw[m % NRAW][:, h * w:(h + 1) * w]
                r = u % NUNIT
                th = act(lambda e: e.activation(uh[r][:, 0:w], src, ACT.Copy), dma_tok[m],
                         unit_rel[u - NUNIT] if u >= NUNIT else [], own=False)
                tl = dve(lambda e: e.tensor_tensor(ul[r][:, 0:w], src, uh[r][:, 0:w].bitcast(F32), ALU.subtract),
                         th, own=False)
                unit_tok[u] = tl
                if h == 1:
                    chunk_rel[m] = [tl]
                    pump()

            def ahead(u):
                while conv_pos[0] < len(units) and conv_pos[0] <= u + NUNIT - 1:
                    c = conv_pos[0]
                    if c >= NUNIT and c - NUNIT not in unit_rel:
                        break
                    if units[c][0] not in dma_tok:
                        break
                    convert(c)
                    conv_pos[0] += 1

            later, rate, spent, after_unit = [], [1.5], [0.0], [lambda: None]

            def step(budget):
                spent[0] = min(spent[0] + budget, budget)
                while later and spent[0] > 0:
                    w, fn = later.pop(0)
                    spent[0] -= w
                    fn()

            def flush(mark=None):
                while later and not (mark is not None and mark in done_marks):
                    later.pop(0)[1]()
                spent[0] = 0.0

            done_marks = set()

            def put_off(weight, fn):
                later.append((weight, fn))

            def put_mark(mark):
                later.append((0.0, lambda: done_marks.add(mark)))

            def take_unit(key):
                u = upos[0]
                while u not in unit_tok:
                    ahead(u)
                    if u not in unit_tok:
                        assert later, (u, units[u], chunks[units[u][0]][0])
                        later.pop(0)[1]()
                m, h, kk, n = units[u]
                assert m == cpos[0], (chunks[m][0], chunks[cpos[0]][0], key)
                assert chunks[m][0][:len(key)] == key, (chunks[m][0], key)
                upos[0] += 1
                if h == 1:
                    cpos[0] += 1
                ahead(u)
                r = u % NUNIT
                hi = uh[r][:, 0:kk * n].rearrange("p (k n) -> p k n", n=n)
                lo = ul[r][:, 0:kk * n].rearrange("p (k n) -> p k n", n=n)
                return u, hi, lo, kk, n, unit_tok[u]

            def take_raw(key):
                m = cpos[0]
                k, pcs, kk, n, conv = chunks[m]
                assert k[:len(key)] == key and not conv, (k, key)
                cpos[0] += 1
                return m, raw[m % NRAW][:, 0:kk * n].rearrange("p (k n) -> p k n", n=n), dma_tok[m]

            def give_raw(m, tok):
                chunk_rel[m] = [tok]
                pump()

            def linear(key, K, lhi, llo, lt, banks, first=True, last=True, mid=None, tiles=T):
                k = 0
                tok = None
                while k < K:
                    u, hi, lo, kk, n, ut = take_unit(key)
                    if mid is not None and k >= K // 2:
                        mid()
                        mid = None
                    for t in range(tiles):
                        for j in range(kk):
                            for c in range((n + 511) // 512):
                                w = min(512, n - c * 512)
                                o = PB[banks[t][c]][:, 0:w]
                                a, b = lhi(k + j, t), llo(k + j, t)
                                wh, wl = hi[:, j, c * 512:c * 512 + w], lo[:, j, c * 512:c * 512 + w]
                                s0 = first and k + j == 0
                                s1 = last and k + j == K - 1
                                pe(lambda e, o=o, a=a, wh=wh, s0=s0: e.matmul(o, a, wh, start=s0, stop=False),
                                   ut, lt[k + j] if isinstance(lt, list) and lt and isinstance(lt[0], list) else lt,
                                   free[banks[t][c]] if s0 else [])
                                pe(lambda e, o=o, a=a, wl=wl: e.matmul(o, a, wl, start=False, stop=False))
                                tok = pe(lambda e, o=o, b=b, wh=wh, s1=s1: e.matmul(o, b, wh, start=False, stop=s1))
                    unit_rel[u] = [tok]
                    k += kk
                    step(rate[0])
                    after_unit[0]()
                ahead(upos[0] - 1)
                return tok

            loads = [0]

            def load(dst, src, *w, q="gpsimd"):
                loads[0] += 1
                s = sem(f"load{loads[0]}")
                return Q.dma(q, lambda e: e.dma_start(dst, src), w, s, 16)

            t_s4 = load(sum4[:, :], I["sum4_c"], q="scalar")
            t_id = load(ident[:, :], I["ident_c"], q="scalar")
            stk1 = G[2][0:96, 0:128]
            stk2 = G[2][0:48, 128:256]
            l2 = []
            r0 = 0
            where = {}
            for nm, rows in (("c", 8), ("mla_q_norm", 2), ("mla_kv_norm", 1), ("g_mix_2", 8), ("conv_b_2", 4),
                             ("ln_g_2", 4), ("ln_b_2", 4), ("g_mem_2", 8), ("g_ffn_2", 8)):
                l2.append(load(stk2[r0:r0 + rows, :], I[nm].rearrange("a (k p) -> (a k) p", p=P), q="scalar"))
                where[nm] = r0
                r0 += rows
            t_n = load(stk1, I["norm_g"].rearrange("i m (k p) -> (i m k) p", p=P), q="scalar")
            t_x = [load(x[:, t, :], I["x"][0, t * P:(t + 1) * P, :], q="scalar") for t in range(T)]

            def col(nm, k):
                return cc[:, where[nm] + k:where[nm] + k + 1]

            tp = pe(lambda e: e.transpose(PB[7][:, 0:r0], stk2[0:r0, :], ident[0:r0, 0:r0]), t_id, l2)
            t_cc = dve(lambda e: e.tensor_copy(cc[:, 0:r0], PB[7][:, 0:r0]), tp)
            t_sc = act(lambda e: e.activation(sc[:, :], cc[:, 0:8], ACT.Silu), t_cc)
            tp = pe(lambda e: e.transpose(PB[6][:, 0:96], stk1, ident[0:96, 0:96]), t_n)
            t_ng = dve(lambda e: e.tensor_copy(ngc[:, :], PB[6][:, 0:96]), tp)
            free[7] = [t_cc]
            free[6] = [t_ng]

            def bcast_row(src, n):
                return src.to_broadcast([P, n])

            g_tok, g_done = {}, {}

            def load_G(s, *w):
                i, m = s // 3, s % 3
                src = I["norm_g"][i, 2 * m + 1:2 * m + 2, :]
                g_tok[s] = load(G[s % 3][:, :], src.to_broadcast([P, D]), *w)

            load_G(0)
            load_G(1)
            load_G(2, t_ng, t_cc)

            t_ab = load(adab[0:36, :], I["ada_b"].rearrange("i (j n) -> (i j) n", n=512), q="scalar")
            ab_tok = {s: [] for s in range(6)}

            xn = arena(T, D)
            XN_END = at[0]
            def ada_end(i, j, tok):
                s, kind, half = i * 3 + j // 6, (j // 2) % 3, j % 2
                if kind == 2:
                    g = G[s % 3][:, half * 512:half * 512 + 512]
                    tk = dve(lambda e: e.scalar_tensor_tensor(g, PB[7], 1.0, g, ALU.add, ALU.mult), tok, g_tok[s])
                    g_done.setdefault(s, []).append(tk)
                else:
                    d = full[:, 1, :].rearrange("p (a b) -> p a b", b=P)
                    dve(lambda e: e.tensor_tensor(d, PB[7].rearrange("p (a b) -> p a b", b=P),
                                                  ident[:, :].unsqueeze(1).to_broadcast([P, 4, P]), ALU.mult),
                        tok, Q.last["scalar"])
                    dst = ab[:, s, 1 - kind, half * 4:half * 4 + 4]
                    tk = dve(lambda e: e.tensor_reduce(dst, d, AX_X, ALU.add))
                    if kind == 1:
                        gc = ngc[:, i * 48 + (s % 3) * 16 + half * 4:i * 48 + (s % 3) * 16 + half * 4 + 4]
                        tk = dve(lambda e: e.scalar_tensor_tensor(dst, dst, 1.0, gc, ALU.add, ALU.mult), t_ng)
                    ab_tok[s].append(tk)
                free[7] = [tk]

            def ada(i, j):
                got = [take_raw(("ada", i, j)) for _ in range(2)]
                r = i * 18 + j

                def parts():
                    pe(lambda e: e.matmul(PB[7][0:32, :], ident[0:36, r:r + 1].to_broadcast([36, 32]),
                                          adab[0:36, :], start=True, stop=False), t_ab, t_id, free[7])
                    for k in range(KD):
                        m, w, dt = got[k // 4]
                        g = (k + 1) % 4
                        tok = pe(lambda e: e.matmul(
                            PB[7][32 * g:32 * g + 32, :], sc[:, k:k + 1].to_broadcast([P, 32]), w[:, k % 4, :],
                            start=(k < 3), stop=(k >= 4)), dt, t_sc)
                        if k % 4 == 3:
                            give_raw(m, tok)
                    ada_s[i, j] = act(lambda e: e.activation(full[:, 0, :], PB[7], ACT.Copy), tok,
                                      Q.last["vector"])

                def total():
                    tok = pe(lambda e: e.matmul(PB[7], sum4[:, :], full[:, 0, :], start=True, stop=True),
                             ada_s[i, j], t_s4)
                    ada_end(i, j, tok)
                    full_pe[:] = [tok, Q.last["vector"]]

                parts()
                put_off(1.3, total)

            ada_s, full_pe = {}, []

            def warm():
                act(lambda e: e.activation(st[:, 258:259], sum4[:, 0:1], ACT.Sqrt), t_s4)

            def rstd(dst, ss, n, *w, weight=1.0):
                c = ss.shape[-1]
                v, r, a = st[:, 128:128 + c], st[:, 160:160 + c], st[:, 192:192 + c]
                tv = dve(lambda e: e.tensor_scalar(v, ss, 1.0 / n, EPS, ALU.mult, ALU.add), w)
                ts = act(lambda e: e.activation(r, v, ACT.Sqrt), tv)
                dve(lambda e: e.reciprocal(r, r), ts)
                dve(lambda e: e.tensor_tensor(a, r, r, ALU.mult))
                dve(lambda e: e.tensor_tensor(a, a, v, ALU.mult))
                dve(lambda e: e.tensor_scalar(a, a, -0.5, 1.5, ALU.mult, ALU.add))
                return dve(lambda e: e.scalar_tensor_tensor(dst, r, weight, a, ALU.mult, ALU.mult))

            def row_squares(dst, src, *w):
                o = full[:, :, :].rearrange("p a b -> p (a b)")
                return act(lambda e: e.activation(o, src, ACT.Square, accum_out=dst), w, full_pe)

            RB = [6, 7, 4, 5]
            rb = [0]

            def to_T(src, K, dst_h, dst_l, scale=None, bias=None, func=None, keep=None, waits=(), wdst=()):
                toks = []
                for k0 in range(0, K, 2):
                    b = RB[rb[0] % 4]
                    rb[0] += 1
                    nk = min(2, K - k0)
                    for k in range(nk):
                        for t in range(T):
                            tp = pe(lambda e, k=k, t=t, b=b: e.transpose(
                                PB[b][:, k * S + t * P:k * S + (t + 1) * P], src(t, k0 + k), ident[:, :]),
                                waits, free[b], t_id)
                    ps = PB[b][:, 0:nk * S].rearrange("p (k n) -> p k n", n=S)
                    H, L = (dst_h[:, k0:k0 + nk, :], dst_l[:, k0:k0 + nk, :]) if dst_h is not None else (None, None)
                    fl = full[:, (k0 // 2) % 2, 0:nk * S].rearrange("p (k n) -> p k n", n=S)
                    if scale is None:
                        th = act(lambda e: e.activation(H, ps, ACT.Copy), tp, wdst)
                        tl = dve(lambda e: e.tensor_tensor(L, ps, H.bitcast(F32), ALU.subtract), th)
                        fr = [th, tl]
                    elif func is None:
                        if keep is not None:
                            fl = keep[:, k0:k0 + nk, :]
                        for k in range(nk):
                            sc_, bi_ = scale(k0 + k), (bias(k0 + k) if bias is not None else 0.0)
                            tf = dve(lambda e: e.tensor_scalar(fl[:, k, :], ps[:, k, :], sc_, bi_, ALU.mult, ALU.add),
                                     tp, wdst, full_pe)
                        fr = [tf]
                        if H is None:
                            toks += [[tf]] * nk
                            free[b] = fr
                            continue
                        th = act(lambda e: e.activation(H, fl, ACT.Copy), tf)
                        tl = dve(lambda e: e.tensor_tensor(L, fl, H.bitcast(F32), ALU.subtract), th)
                    else:
                        for k in range(nk):
                            sc_, bi_ = scale(k0 + k), bias(k0 + k)
                            tf = act(lambda e: e.activation(fl[:, k, :], ps[:, k, :], func, bias=bi_, scale=sc_),
                                     tp, wdst)
                        th = act(lambda e: e.activation(H, fl, ACT.Copy))
                        tl = dve(lambda e: e.tensor_tensor(L, fl, H.bitcast(F32), ALU.subtract), th)
                        fr = [tf]
                    toks += [[th, tl]] * nk
                    free[b] = fr
                return toks


            def prenorm(waits=(), src=None, dst=None, gain=None, tg=()):
                src = x if src is None else src
                dst = xn if dst is None else dst
                for t in range(T):
                    ta = row_squares(st[:, 4 + t:5 + t], src[:, t, :], waits[t:t + 1] if len(waits) == T else waits)
                rstd(st[:, 6:8], st[:, 4:6], D, ta)
                for t in range(T):
                    if gain is not None:
                        tk = dve(lambda e: e.scalar_tensor_tensor(dst[:, t, :], src[:, t, :], st[:, 6 + t:7 + t], gain,
                                                                  ALU.mult, ALU.mult), last_pe_xn, tg)
                    else:
                        tk = dve(lambda e: e.tensor_scalar(dst[:, t, :], src[:, t, :], st[:, 6 + t:7 + t], None,
                                                           ALU.mult), last_pe_xn)
                return tk

            last_pe_xn = []

            def rows_xn(t, k):
                return xn[:, t, k * P:(k + 1) * P]

            def pre(s, keep=None, split=True):
                wd = [Q.last["tensor"]]
                flush()
                tk = prenorm(x_tok)
                toks = to_T(rows_xn, KD, hh if split else None, hl, scale=lambda k: ab[:, s, 0, k:k + 1],
                            bias=lambda k: ab[:, s, 1, k:k + 1],
                            keep=keep, waits=[tk], wdst=wd + ab_tok[s])
                last_pe_xn[:] = [Q.last["tensor"]]
                return toks

            def post(s, src, weight, waits, psum=True):
                while len(g_done.get(s, [])) < 2:
                    later.pop(0)[1]()
                warm()
                g = G[s % 3]
                if psum:
                    t0 = row_squares(st[:, 4:5], src(0), waits)
                    d1 = dve(lambda e: e.tensor_tensor(xn[:, 1, :], src(1), g, ALU.mult), waits, g_done[s], last_pe_xn)
                    t1 = row_squares(st[:, 5:6], src(1), d1)
                    d0 = dve(lambda e: e.tensor_tensor(xn[:, 0, :], src(0), g, ALU.mult), t0)
                else:
                    for t in range(T):
                        t1 = row_squares(st[:, 4 + t:5 + t], src(t), waits)
                        dve(lambda e: e.tensor_tensor(xn[:, t, :], src(t), g, ALU.mult), t1, g_done[s])
                rstd(st[:, 6:8], st[:, 4:6], D, t1, weight=weight)
                x_tok[:] = [dve(lambda e: e.scalar_tensor_tensor(
                    x[:, t, :], xn[:, t, :], st[:, 6 + t:7 + t], x[:, t, :], ALU.mult, ALU.add)) for t in range(T)]
                if psum:
                    for t in range(T):
                        for b in YB[t]:
                            free[b] = [x_tok[0]]
                if s + 3 < 6:
                    load_G(s + 3, x_tok)

            def ypsum2(t):
                return PS[:, 2 * t:2 * t + 2, :].rearrange("p a b -> p (a b)")

            def ypsum(t, h):
                return PB[YB[t][h]][:, :]

            lh = lambda k, t: hh[:, k, t * P:(t + 1) * P]
            ll = lambda k, t: hl[:, k, t * P:(t + 1) * P]

            ff = {"n": 0, "ug": [[], []], "gt": [[], []], "sg": []}

            def ffn_like(nb, kin, kout, toks, between, combine=None):
                def spread(b):
                    i = b % 2
                    for f in range(2):
                        for t in range(T):
                            tp = pe(lambda e, f=f, t=t: e.transpose(
                                PB[6][:, f * S + t * P:f * S + (t + 1) * P], ug[i][:, t, f * P:(f + 1) * P], ident[:, :]),
                                ff["ug"][i], free[6])
                    th = act(lambda e: e.activation(gT_h[i][:, :, :], PB[6][:, :].rearrange("p (a b) -> p a b", b=S),
                                                    ACT.Copy), tp, ff["gt"][i])
                    tl = dve(lambda e: e.tensor_tensor(
                        gT_l[i][:, :, :], PB[6][:, :].rearrange("p (a b) -> p a b", b=S),
                        gT_h[i][:, :, :].bitcast(F32), ALU.subtract), th)
                    free[6] = [th, tl]
                    ff["ugfree"][i] = [tp]
                    ff["gtt"][i] = [th, tl]

                ff["ugfree"] = [[], []]
                ff["gtt"] = [[], []]

                def outp(b):
                    i = b % 2
                    tok = linear(kout(b), 2, lambda k, t: gT_h[i][:, k, t * P:(t + 1) * P],
                                 lambda k, t: gT_l[i][:, k, t * P:(t + 1) * P], ff["gtt"][i], YB,
                                 first=(b == 0), last=(b == nb - 1))
                    ff["gt"][i] = [tok]
                    return tok

                for b in range(nb):
                    i = b % 2
                    tok = linear(kin(b), KD, lh, ll, toks, [[AB[0]], [AB[1]]], mid=(lambda b=b: spread(b - 1)) if b else None)
                    for t in range(T):
                        ta = act(lambda e, t=t: e.activation(sg[:, t, :], PB[AB[t]][:, 0:256], ACT.Silu), tok, ff["sg"])
                        if combine is None:
                            td = dve(lambda e, t=t: e.tensor_tensor(ug[i][:, t, :], sg[:, t, :], PB[AB[t]][:, 256:512],
                                                                   ALU.mult), ta, ff["ugfree"][i])
                        else:
                            td = dve(lambda e, t=t: e.scalar_tensor_tensor(
                                ug[i][:, t, :], sg[:, t, :], comb[:, t, b:b + 1], PB[AB[t]][:, 256:512],
                                ALU.mult, ALU.mult), ta, ff["ugfree"][i], combine)
                        free[AB[t]] = [ta, td]
                    ff["sg"] = [td]
                    ff["ug"][i] = [td]
                    if b:
                        outp(b - 1)
                    between(b)
                spread(nb - 1)
                return outp(nb - 1)

            x_tok = list(t_x)
            for a in ada_order[:4]:
                ada(*a)
                flush()

            def ffn(i, s):
                sl = i * 3 + 2 * s
                toks = pre(sl)

                def between(b):
                    for a in ADA_AT.get((i, s, b), []):
                        ada(*a)
                tok = ffn_like(NFF, lambda b: ("fi", i, s, b), lambda b: ("fo", i, s, b), toks, between)
                flush()
                post(sl, ypsum2, 0.5, [tok])

            ffn(0, 0)

            at[0] = XN_END
            hp = arena(KD, 272)
            sA, sB = arena(2, 272), arena(2, 272)
            zT = arena(KD, S)
            rc = arena(4, S)
            pbb = arena(D)
            psb = arena(D)
            yp = xn
            t_rc = load(rc, I["rc_c"].rearrange("g n -> (g n)").unsqueeze(0).to_broadcast([P, 4 * S])
                        .rearrange("p (g n) -> p g n", n=S))
            t_pb = load(pbb, I["pool_b"].rearrange("a g n -> a (g n)").to_broadcast([P, D]))
            t_ps = load(psb, I["pool_scale"].to_broadcast([P, D]))
            tz = dve(lambda e: e.memset(hp[:, :, 0:8], 0.0))
            tz = dve(lambda e: e.memset(hp[:, :, 264:272], 0.0))
            KM, VM = kvm[:, 0, :, :], kvm[:, 1, :, :]
            mrow = zT.rearrange("p (a b) c -> p a (b c)", a=T)
            t_mem = load(mrow, I["mem_2"][0].rearrange("(t p) n -> p t n", p=P), x_tok)
            pre(1, keep=hp[:, :, 8:264], split=False)
            tk = prenorm([t_mem], mrow, mrow)
            mtoks = to_T(lambda t, k: mrow[:, t, k * P:(k + 1) * P], KD, hh, hl,
                         scale=lambda k: col("g_mem_2", k), waits=[tk], wdst=[Q.last["tensor"]])
            mtr = [Q.last["tensor"]]
            zt = []
            for g in range(4):
                src = hp[:, 2 * g:2 * g + 2, :]
                n = 272
                for m in range(g + 1):
                    sh = 1 << m
                    n -= sh
                    dst = (sA, sB)[m % 2]
                    dve(lambda e, dst=dst, src=src, n=n, sh=sh: e.tensor_tensor(
                        dst[:, :, 0:n], src[:, :, 0:n], src[:, :, sh:sh + n], ALU.add))
                    src = dst
                o = 8 - (1 << g)
                z = zT[:, 2 * g:2 * g + 2, :]
                dve(lambda e, z=z, src=src, o=o, g=g: e.tensor_tensor(
                    z, src[:, :, o:o + S], rc[:, g:g + 1, :].to_broadcast([P, 2, S]), ALU.mult), t_rc, mtr)
                zt.append(dve(lambda e, z=z, g=g: e.tensor_tensor(z, z, hp[:, 2 * g:2 * g + 2, 8:264], ALU.subtract)))
            tok = linear(("kv",), KD, lh, ll, mtoks, [[4], [5]])
            tok2 = linear(("kv",), KD, lh, ll, mtoks, [[0], [2]])
            for t in range(T):
                tk = act(lambda e: e.activation(KM[:, t, :], PB[4 + t], ACT.Copy), tok)
                free[4 + t] = [tk]
                tk = act(lambda e: e.activation(VM[:, t, :], PB[2 * t], ACT.Copy), tok2)
                free[2 * t] = [tk]
            for a in ada_pool:
                ada(*a)
                flush()
            m, w, dt = take_raw(("pw",))
            for g in range(4):
                for t in range(T):
                    b = YB[t][g // 2]
                    for k in range(2):
                        tp = pe(lambda e, g=g, t=t, k=k, b=b: e.matmul(
                            PB[b][:, (g % 2) * 256:(g % 2) * 256 + 256], zT[:, 2 * g + k, t * P:(t + 1) * P],
                            w[:, 2 * g + k, :], start=(k == 0), stop=(k == 1)), zt[g], dt, free[b])
            give_raw(m, tp)
            for t in range(T):
                for h in range(2):
                    b = YB[t][h]
                    o = yp[:, t, h * 512:(h + 1) * 512]
                    td = dve(lambda e, o=o, b=b, h=h: e.tensor_tensor(o, PB[b][:, :], pbb[:, h * 512:(h + 1) * 512],
                                                                     ALU.add), tp, t_pb)
                    free[b] = [td]
                    tk = dve(lambda e, o=o, h=h: e.tensor_tensor(o, o, psb[:, h * 512:(h + 1) * 512], ALU.mult), t_ps)
            post(1, lambda t: yp[:, t, :], 1.0, [tk], psum=False)

            ffn(0, 1)
            ffn(1, 0)

            def rope(v, n_t, nh, half, cos, sin, tmp, *w, dve=dve):
                x1, x2 = v[:, :, 0:half], v[:, :, half:2 * half]
                c = cos.unsqueeze(1).to_broadcast([P, nh, half])
                s = sin.unsqueeze(1).to_broadcast([P, nh, half])
                a, b = tmp[0], tmp[1]
                a = a[:, 0:nh * half].rearrange("p (h d) -> p h d", d=half)
                b = b[:, 0:nh * half].rearrange("p (h d) -> p h d", d=half)
                dve(lambda e: e.tensor_tensor(a, x2, s, ALU.mult), w)
                dve(lambda e: e.tensor_tensor(b, x1, s, ALU.mult))
                dve(lambda e: e.tensor_tensor(x1, x1, c, ALU.mult))
                dve(lambda e: e.tensor_tensor(x1, x1, a, ALU.subtract))
                dve(lambda e: e.tensor_tensor(x2, x2, c, ALU.mult))
                return dve(lambda e: e.tensor_tensor(x2, x2, b, ALU.add))

            def attention(nh, hd, vd, qrow, krow, kshare, vrow, orow, scale, tq, bufs, mask=None, extra=None):
                qk, pr, pT, sm, mx = bufs
                fq, fp, fpt = [[], []], [[], []], [[], []]
                ex, pt, tS = {}, {}, {}
                kt_of = {}
                sums = st[:, 64:64 + 2 * nh]
                result = []

                cp = {}

                def zero(h):
                    i = h % 2
                    for t in range(T):
                        pe(lambda e, t=t: e.transpose(PB[6][0:hd, t * P:(t + 1) * P], qrow(h, t), ident[:, :]),
                           tq, free[6])
                    for t in range(T):
                        tp = pe(lambda e, t=t: e.transpose(PB[6][0:hd, S + t * P:S + (t + 1) * P], krow(h // kshare, t),
                                                           ident[:, :]))
                    tc = act(lambda e: e.activation(qk[i][0:hd, :], PB[6][0:hd, :], ACT.Copy), tp, fq[i])
                    free[6] = [tc]
                    cp[h] = tc

                def one(h):
                    i = h % 2
                    b = AB[i]
                    tc = cp[h]
                    for t in range(T):
                        ts = pe(lambda e, t=t: e.matmul(PB[b][:, t * S:(t + 1) * S], qk[i][0:hd, t * P:(t + 1) * P],
                                                        qk[i][0:hd, S:2 * S], start=True, stop=True), tc, free[b])
                    fq[i] = [ts]
                    if mask is not None:
                        sv = sm[i].rearrange("p (t n) -> p t n", n=S)
                        tm = dve(lambda e: e.tensor_tensor(sv, PB[b][:, :].rearrange("p (t n) -> p t n", n=S), mask,
                                                           ALU.add), ts)
                        free[b] = [tm]
                    else:
                        sv = PB[b][:, :].rearrange("p (t n) -> p t n", n=S)
                    m2 = mx[:, 2 * i:2 * i + 2]
                    dve(lambda e: e.tensor_reduce(m2, sv, AX_X, ALU.max), ts)
                    tm = dve(lambda e: e.tensor_scalar(m2, m2, -scale, None, ALU.mult))
                    for t in range(T):
                        te = act(lambda e, t=t: e.activation(pr[i][:, t * S:(t + 1) * S], sv[:, t, :], ACT.Exp,
                                                             bias=m2[:, t:t + 1], scale=scale,
                                                             accum_out=sums[:, 2 * h + t:2 * h + t + 1]), tm, fp[i])
                    if mask is None:
                        free[b] = [te]
                    ex[h] = te

                def two(h):
                    i = h % 2
                    for c in range(2):
                        for t in range(T):
                            tp = pe(lambda e, c=c, t=t: e.transpose(
                                PB[7][:, c * S + t * P:c * S + (t + 1) * P], pr[i][:, t * S + c * P:t * S + (c + 1) * P],
                                ident[:, :]), ex[h], free[7])
                    fp[i] = [tp]
                    tc = dve(lambda e: e.tensor_copy(pT[i], PB[7][:, :]), tp, fpt[i])
                    free[7] = [tc]
                    pt[h] = tc

                tlast = [None]

                def three(h):
                    i = h % 2
                    for t in range(T):
                        b = YB[t][h * vd // 512]
                        c0 = h * vd % 512
                        for c in range(2):
                            tlast[0] = pe(lambda e, c=c, t=t, b=b, c0=c0: e.matmul(
                                PB[b][:, c0:c0 + vd], pT[i][:, c * S + t * P:c * S + (t + 1) * P],
                                vrow(c, h // kshare), start=(c == 0), stop=(c == 1)), pt[h], free[b])
                    fpt[i] = [tlast[0]]

                def at_step(h):
                    if extra is not None:
                        extra()
                    if h < nh:
                        zero(h)
                    if 1 <= h <= nh:
                        one(h - 1)
                    if 2 <= h <= nh + 1:
                        two(h - 2)
                    if h >= 3:
                        three(h - 3)

                def finish():
                    rs = st[:, 224:224 + 2 * nh]
                    dve(lambda e: e.reciprocal(rs, sums), ex[nh - 1])
                    rv = rs.rearrange("p (h t) -> p h t", t=2)
                    for t in range(T):
                        for hb in range((nh * vd + 511) // 512):
                            n0 = 512 // vd
                            b = YB[t][hb]
                            tk = dve(lambda e: e.tensor_tensor(
                                orow(t)[:, hb * n0:(hb + 1) * n0, :], PB[b].rearrange("p (h d) -> p h d", d=vd),
                                rv[:, hb * n0:(hb + 1) * n0, t:t + 1].to_broadcast([P, n0, vd]), ALU.mult), tlast[0])
                            free[b] = [tk]
                    result.append(tk)

                for h in range(nh + 3):
                    put_off(2.2 if mask is not None else 1.6, lambda h=h: at_step(h))
                put_off(1.2, finish)
                return result

            at[0] = XN_END
            xf = xn.rearrange("p a b -> p (a b)")
            lat = xf[:, 0:832].rearrange("p (a b) -> p a b", b=416)
            qr = arena(T, 1536)
            kr = arena(T, 1536)
            vr = arena(T, 1024)
            cqT = xf[:, 1024:1536].rearrange("p (a b) -> p a b", b=S)
            ckT = xf[:, 1536:1792]
            ropeC = arena(2, T, 16)
            flat2 = lambda a: a.rearrange("p a b -> p (a b)")
            qk = [flat2(ug[0][:, :, :]), flat2(ug[1][:, :, :])]
            pr = [flat2(sg[:, :, :]), arena(512)]
            pT = [G[0][:, 0:512], G[0][:, 512:1024]]
            orow_a = xn
            tmpA = [qk[0], pr[0]]
            t_rp = load(ropeC, I["rope16_c"].rearrange("p (a t d) -> p a t d", a=2, t=2), x_tok)
            toks = pre(4)
            tok = linear(("mi",), KD, lh, ll, toks, [[AB[0]], [AB[1]]])
            for t in range(T):
                td = dve(lambda e, t=t: e.tensor_copy(lat[:, t, :], PB[AB[t]][:, 0:416]), tok)
                free[AB[t]] = [td]
                for c, (a, n) in enumerate(((0, 256), (256, 128))):
                    ts = act(lambda e, t=t, c=c, a=a, n=n: e.activation(
                        full[:, 1, 0:n], lat[:, t, a:a + n], ACT.Square,
                        accum_out=st[:, 10 + 2 * c + t:11 + 2 * c + t]), td)
            rstd(st[:, 16:18], st[:, 10:12], 256, ts)
            tr = rstd(st[:, 18:20], st[:, 12:14], 128)
            for t in range(T):
                dve(lambda e, t=t: e.tensor_scalar(lat[:, t, 0:256], lat[:, t, 0:256], st[:, 16 + t:17 + t], None, ALU.mult))
                td = dve(lambda e, t=t: e.tensor_scalar(lat[:, t, 256:384], lat[:, t, 256:384], st[:, 18 + t:19 + t], None,
                                                        ALU.mult))
            for k in range(3):
                b = 6 if k < 2 else 7
                for t in range(T):
                    tp = pe(lambda e, k=k, t=t, b=b: e.transpose(
                        PB[b][:, (k % 2) * S + t * P:(k % 2) * S + (t + 1) * P], lat[:, t, k * P:(k + 1) * P],
                        ident[:, :]), td, free[b])
                dst = cqT[:, k, :] if k < 2 else ckT
                g = col("mla_q_norm", k) if k < 2 else col("mla_kv_norm", 0)
                tc = dve(lambda e, dst=dst, g=g, b=b, k=k: e.tensor_scalar(dst, PB[b][:, (k % 2) * S:(k % 2) * S + S], g,
                                                                          None, ALU.mult), tp)
                free[b] = [tc]
            QB = [[0, 1, 4], [2, 3, 5]]
            for k in range(2):
                m, w, dt = take_raw(("uq",))
                for t in range(T):
                    for c in range(3):
                        tp = pe(lambda e, k=k, t=t, c=c, w=w: e.matmul(
                            PB[QB[t][c]][:, :], cqT[:, k, t * P:(t + 1) * P], w[:, 0, c * 512:(c + 1) * 512],
                            start=(k == 0), stop=(k == 1)), dt, tc, free[QB[t][c]])
                give_raw(m, tp)
            for t in range(T):
                for c in range(3):
                    b = QB[t][c]
                    if c % 2:
                        tk = dve(lambda e, t=t, c=c, b=b: e.tensor_copy(qr[:, t, c * 512:(c + 1) * 512], PB[b][:, :]), tp)
                    else:
                        tk = act(lambda e, t=t, c=c, b=b: e.activation(qr[:, t, c * 512:(c + 1) * 512], PB[b][:, :],
                                                                      ACT.Copy), tp)
                    free[b] = [tk]
            ta = Q.last["scalar"]
            krv = kr.rearrange("p t (h d) -> p t h d", d=96)
            qrv = qr.rearrange("p t (h d) -> p t h d", d=96)
            for nm, tgt in (("mla_w_uk", 0), ("mla_w_uv", 1)):
                m, w, dt = take_raw((nm,))
                for t in range(T):
                    for c in range(2):
                        b = YB[t][c]
                        tp = pe(lambda e, t=t, c=c, w=w, b=b: e.matmul(
                            PB[b][:, :], ckT[:, t * P:(t + 1) * P], w[:, 0, c * 512:(c + 1) * 512],
                            start=True, stop=True), dt, tc, free[b])
                        if tgt == 0:
                            tk = act(lambda e, t=t, c=c, b=b: e.activation(
                                krv[:, t, 8 * c:8 * c + 8, 0:64], PB[b][:, :].rearrange("p (h d) -> p h d", d=64),
                                ACT.Copy), tp)
                        else:
                            tk = act(lambda e, t=t, c=c, b=b: e.activation(vr[:, t, c * 512:(c + 1) * 512], PB[b][:, :],
                                                                          ACT.Copy), tp)
                        free[b] = [tk]
                give_raw(m, tp)
            for t in range(T):
                rope(lat[:, t, 384:416].rearrange("p (h d) -> p h d", h=1), T, 1, 16, ropeC[:, 0, t, :], ropeC[:, 1, t, :],
                     tmpA, t_rp)
                dve(lambda e, t=t: e.tensor_copy(krv[:, t, :, 64:96],
                                                 lat[:, t, 384:416].unsqueeze(1).to_broadcast([P, 16, 32])))
                tk2 = rope(qrv[:, t, :, 64:96], T, 16, 16, ropeC[:, 0, t, :], ropeC[:, 1, t, :], tmpA, ta)
            att = attention(16, 96, 64, lambda h, t: qrv[:, t, h, :], lambda h, t: krv[:, t, h, :], 1,
                           lambda c, h: vr[:, c, h * 64:(h + 1) * 64],
                           lambda t: orow_a[:, t, :].rearrange("p (h d) -> p h d", d=64),
                           96 ** -0.5, [tk, tk2], (qk, pr, pT, None, st[:, 96:100]))
            flush()
            wd = [Q.last["tensor"]]
            toks = to_T(lambda t, k: orow_a[:, t, k * P:(k + 1) * P], KD, hh, hl,
                        waits=att, wdst=wd)
            tok = linear(("mo",), KD, lh, ll, toks, YB)
            post(4, ypsum2, 1.0, [tok])

            ffn(1, 1)

            at[0] = XN_END
            QK = arena(T, 19, 64)
            V = arena(T, 128)
            QM = arena(T, 4, 128)
            wi = arena(T, 8)
            gqk = arena(3, 64)
            gqm = arena(2, 128)
            rp32 = arena(2, T, 32)
            cw = arena(4, CONVW)
            uT = arena(4, 286)
            mask = arena(T, S)
            score = arena(T, S)
            pr = [flat2(sg[:, :, :]), arena(512)]
            ga = arena(2, T, 512)
            om = xf[:, 0:1024].rearrange("p (t n) -> p t n", t=T)
            ca = xf[:, 1024:2048].rearrange("p (t n) -> p t n", t=T)
            gm = [G[1].rearrange("p (t n) -> p t n", t=T), ca]
            yc = G[0].rearrange("p (k n) -> p k n", n=S)
            ht = G[2]
            qk = [flat2(ug[0][:, :, :]), flat2(ug[1][:, :, :])]
            pT = [ht[:, 0:512], ht[:, 512:1024]]
            KMv = KM.rearrange("p t (h d) -> p t h d", d=P)
            base = list(x_tok)
            tgn = [load(gqk[:, i:i + 1, :], I[nm].unsqueeze(0).to_broadcast([P, 1, 64]), base)
                   for i, nm in enumerate(("g_qa_2", "g_ka_2", "g_idx_k_2"))]
            tgn += [load(gqm[:, i, :], I[nm].to_broadcast([P, 128]), base) for i, nm in enumerate(("g_qm_2", "g_km_2"))]
            t_rp = load(rp32, I["rope32_c"].rearrange("p (a t d) -> p a t d", a=2, t=2), base)
            t_cm = load(mask, I["cap_c"].rearrange("p (t n) -> p t n", n=S), base)
            cwr = om[0:CONVW, 0, :]
            t_bg = load(adab[0:6, :], I["b_gate_2"].rearrange("a (j n) -> (a j) n", n=512), base)

            tk = prenorm(x_tok)
            toks = to_T(rows_xn, KD, hh, hl, scale=lambda k: col("g_mix_2", k), waits=[tk], wdst=[Q.last["tensor"]])
            t_cw = load(cwr, I["conv_w_2"][0].rearrange("j a n -> j (a n)"), Q.last["tensor"])
            tz = dve(lambda e: e.memset(uT[:, :, 0:30], 0.0), base)

            def norm_steps(v, nh, hd, gains, waits):
                ss, rr = st[:, 20:20 + 2 * nh], st[:, 42:42 + 2 * nh]

                def squares(t):
                    tmp = ht[:, 0:nh * hd].rearrange("p (h d) -> p h d", d=hd)
                    dve(lambda e: e.tensor_tensor(tmp, v(t), v(t), ALU.mult), waits)
                    dve(lambda e: e.tensor_reduce(ss[:, t * nh:(t + 1) * nh], tmp, AX_X, ALU.add))

                def scaled(t):
                    dve(lambda e: e.tensor_tensor(v(t), v(t), rr[:, t * nh:(t + 1) * nh].unsqueeze(2)
                                                  .to_broadcast([P, nh, hd]), ALU.mult))

                def gained(t, a, n, g):
                    dve(lambda e: e.tensor_tensor(v(t)[:, a:a + n, :], v(t)[:, a:a + n, :],
                                                  g.to_broadcast([P, n, hd]), ALU.mult), tgn)

                for t in range(T):
                    put_off(nh * hd * 2.1e-3, lambda t=t: squares(t))
                put_off(1.5, lambda: rstd(rr, ss, hd))
                for t in range(T):
                    put_off(nh * hd * 1.1e-3, lambda t=t: scaled(t))
                    for a, n, g in gains:
                        put_off(n * hd * 1.1e-3, lambda t=t, a=a, n=n, g=g: gained(t, a, n, g))

            rope_tok = {}

            def rope_steps(key, a, n, waits):
                for t in range(T):
                    def go(t=t):
                        rope_tok[key, t] = rope(QK[:, t, a:a + n, :], T, n, 32, rp32[:, 0, t, :], rp32[:, 1, t, :],
                                                [ht[:, 0:512], ht[:, 512:1024]], t_rp, waits)
                    put_off(n * 0.22, go)

            fqk = [[], []]
            ix = {}

            def ix_copy(h):
                i = h % 2
                src = (lambda t: QK[:, t, 10, :]) if h < 0 else (lambda t: QK[:, t, 11 + h, :])
                dst = pr[0][0:64, 0:S] if h < 0 else qk[i][0:64, 0:S]
                for t in range(T):
                    tp = pe(lambda e: e.transpose(PB[6][0:64, t * P:(t + 1) * P], src(t), ident[:, :]),
                            free[6], [rope_tok[k] for k in rope_tok])
                ix[h] = act(lambda e: e.activation(dst, PB[6][0:64, 0:S], ACT.Copy), tp, fqk[i] if h >= 0 else [])
                free[6] = [ix[h]]

            def ix_score(h):
                i, b = h % 2, AB[h % 2]
                for t in range(T):
                    ts = pe(lambda e: e.matmul(PB[b][:, t * S:(t + 1) * S], qk[i][0:64, t * P:(t + 1) * P],
                                               pr[0][0:64, 0:S], start=True, stop=True), ix[h], ix[-1], free[b])
                fqk[i] = [ts]
                rl = pT[h % 2].rearrange("p (t n) -> p t n", n=S)
                ta = act(lambda e: e.activation(pT[h % 2], PB[b], ACT.Relu, scale=0.125), ts, ix.get(("d", h - 2)),
                         Q.last["vector"] if h < 2 else [])
                free[b] = [ta]
                for t in range(T):
                    if h == 0:
                        td = dve(lambda e: e.tensor_scalar(score[:, t, :], rl[:, t, :], wi[:, t, 0:1], None,
                                                           ALU.mult), ta)
                    else:
                        td = dve(lambda e: e.scalar_tensor_tensor(
                            score[:, t, :], rl[:, t, :], wi[:, t, h:h + 1], score[:, t, :], ALU.mult, ALU.add), ta)
                ix["d", h] = td

            def index_steps():
                put_off(0.0, lambda: ix_copy(-1))
                for h in range(9):
                    def go(h=h):
                        if h < 8:
                            ix_copy(h)
                        if h >= 1:
                            ix_score(h - 1)
                    put_off(0.8, go)
                put_off(0.6, lambda: dve(lambda e: e.tensor_tensor(score, score, mask, ALU.min), t_cm))
                for r in range(8):
                    for t in range(T):
                        def mark(t=t):
                            m8 = st[:, 260 + 8 * t:268 + 8 * t]
                            dve(lambda e: e.max(m8, score[:, t, :]))
                            dve(lambda e: e.match_replace(score[:, t, :], m8, score[:, t, :], MARK))
                        put_off(0.8, mark)

                def to_mask():
                    dve(lambda e: e.tensor_scalar(score, score, MARK, None, ALU.is_equal))
                    dve(lambda e: e.scalar_tensor_tensor(mask, mask, 0.0, score, ALU.is_gt, ALU.mult))
                    ix["mask"] = dve(lambda e: e.tensor_scalar(mask, mask, -1.0, -NEG, ALU.add, ALU.mult))
                put_off(1.4, to_mask)

            def conv_taps(k, j):
                y, u, w = yc[:, k, :], uT[:, k, j:j + S], cw[:, k, j:j + 1]
                if j == 0:
                    return dve(lambda e: e.tensor_scalar(y, u, w, col("conv_b_2", k), ALU.mult, ALU.add), t_uT)
                return dve(lambda e: e.scalar_tensor_tensor(y, u, w, y, ALU.mult, ALU.add))

            fill = []

            def filler(n):
                for _ in range(n):
                    if fill:
                        conv_done[0] = conv_taps(*fill.pop(0))

            conv_done = [None]

            lbh = lambda k, t: bh[:, k, t * P:(t + 1) * P]
            lbl = lambda k, t: bl[:, k, t * P:(t + 1) * P]
            pairs = [(1, 3), (0, 2)]
            f64 = lambda a: a.rearrange("p (h d) -> p h d", d=64)
            conv_tr = []

            def conv_transposes():
                for k in range(4):
                    tp = pe(lambda e: e.transpose(PB[7][:, k * 32:k * 32 + CONVW], cwr[:, k * P:(k + 1) * P],
                                                  ident[0:CONVW, 0:CONVW]), t_cw, free[7])
                tc = dve(lambda e: e.tensor_copy(cw, PB[7][:, 0:128].rearrange("p (k j) -> p k j", j=32)[:, :, 0:CONVW]),
                         tp)
                free[7] = [tc]
                tcw = tc
                for k0 in (0, 2):
                    b = 6 if k0 else 5
                    for k in range(2):
                        for t in range(T):
                            tp = pe(lambda e: e.transpose(
                                PB[b][:, k * S + t * P:k * S + (t + 1) * P], ca[:, t, (k0 + k) * P:(k0 + k + 1) * P],
                                ident[:, :]), t_u, free[b])
                    tc = act(lambda e: e.activation(
                        uT[:, k0:k0 + 2, 30:286], PB[b].rearrange("p (k n) -> p k n", n=S), ACT.Copy), tp, tz)
                    free[b] = [tc]
                return [tc, tcw]

            t_uT, fill_rate = [], [0]
            for n_, (c0, n) in enumerate(PROJ):
                b0, b1 = pairs[n_ % 2]
                def go_conv():
                    t_uT.append(conv_transposes())
                    fill[:] = [(k, j) for j in range(CONVW) for k in range(4)]
                mid = go_conv if n_ == 3 else None
                tok = linear(("pj",), KD, lh, ll, toks, [[b0], [b1]], mid=mid)
                for t, b in ((0, b0), (1, b1)):
                    src = PB[b]
                    if n_ == 0:
                        tk = act(lambda e: e.activation(ca[:, t, :], src, ACT.Copy), tok)
                    elif n_ == 1:
                        tk = act(lambda e: e.activation(full[:, t, :], src, ACT.Sigmoid), tok)
                        t_u = dve(lambda e: e.tensor_tensor(ca[:, t, :], ca[:, t, :], full[:, t, :], ALU.mult), tk)
                    elif n_ == 2:
                        act(lambda e: e.activation(QK[:, t, 10, :], src[:, 0:64], ACT.Copy), tok, base)
                        tk = act(lambda e: e.activation(wi[:, t, :], src[:, 64:72], ACT.Copy, scale=8 ** -0.5), tok)
                    elif n_ == 3:
                        tk = act(lambda e: e.activation(QK[:, t, 11:19, :], f64(src), ACT.Copy), tok)
                    elif n_ == 4:
                        tk = act(lambda e: e.activation(QK[:, t, 0:8, :], f64(src), ACT.Copy), tok)
                    elif n_ == 5:
                        act(lambda e: e.activation(QK[:, t, 8:10, :], f64(src[:, 0:128]), ACT.Copy), tok)
                        tk = act(lambda e: e.activation(V[:, t, :], src[:, 128:256], ACT.Copy), tok)
                    else:
                        tk = act(lambda e: e.activation(QM[:, t, :, :], src.rearrange("p (h d) -> p h d", d=128),
                                                        ACT.Copy), tok)
                    free[b] = [tk]
                if n_ == 2:
                    norm_steps(lambda t: QK[:, t, 10:11, :], 1, 64, [(0, 1, gqk[:, 2:3, :])], tk)
                    rope_steps("ki", 10, 1, [])
                elif n_ == 3:
                    rope_steps("qi", 11, 8, tk)
                    index_steps()
                elif n_ == 5:
                    norm_steps(lambda t: QK[:, t, 0:10, :], 10, 64, [(0, 8, gqk[:, 0:1, :]), (8, 2, gqk[:, 1:2, :])], tk)
                    rope_steps("qa", 0, 10, [])

                    def go():
                        ix["att"] = attention(
                            8, 64, 64, lambda h, t: QK[:, t, h, :], lambda h, t: QK[:, t, 8 + h, :], 4,
                            lambda c, h: V[:, c, h * 64:(h + 1) * 64],
                            lambda t: om[:, t, :].rearrange("p (h d) -> p h d", d=64),
                            0.125, [ix["mask"], rope_tok["qa", 1]],
                            (qk, pr, pT, [full[:, 0, :], full[:, 1, :]], st[:, 96:100]), mask=mask, extra=lambda: filler(2))
                        put_mark("att")
                    put_off(0.0, go)
            tqm = tk

            def gates(j, bank, dst, tb=None):
                for b in bank:
                    pe(lambda e: e.matmul(PB[b], ident[0:6, j:j + 1].to_broadcast([6, P]), adab[0:6, :],
                                          start=True, stop=False), free[b], t_bg)
                tok = linear(("gt",), KD, lh, ll, toks, [[b] for b in bank], first=False)
                tks = []
                for t, b in enumerate(bank):
                    ta = act(lambda e: e.activation(dst(t), PB[b], ACT.Sigmoid), tok)
                    free[b] = [ta]
                    tks.append(ta)
                return tks

            tg = {}
            for c in range(2):
                tg[0, c] = gates(c, (1, 3), lambda t: ga[:, c, t, :])
            for c in range(2):
                tg[2, c] = gates(4 + c, (1, 3), lambda t: gm[c][:, t, :])
            flush("att")
            btoks = to_T(lambda t, k: om[:, t, k * P:(k + 1) * P], 4, bh, bl, waits=ix["att"],
                         wdst=[Q.last["tensor"]])
            norm_steps(lambda t: QM[:, t, :, :], 4, 128, [(0, 4, gqm[:, 0:1, :])], tqm)
            norm_steps(lambda t: KMv[:, t, :, :], 4, 128, [(0, 4, gqm[:, 1:2, :])], base)

            def go_m():
                ix["mem"] = attention(
                    4, 128, 128, lambda h, t: QM[:, t, h, :], lambda h, t: KMv[:, t, h, :], 1,
                    lambda c, h: VM[:, c, h * 128:(h + 1) * 128],
                    lambda t: om[:, t, :].rearrange("p (h d) -> p h d", d=128),
                    128 ** -0.5, [Q.last["vector"]], (qk, pr, pT, None, st[:, 96:100]), extra=lambda: filler(3))
                put_mark("mem")
            put_off(0.0, go_m)
            gc = QK.rearrange("p t a b -> p (t a b)")[:, 0:2048].rearrange("p (c t n) -> p c t n", c=2, t=T)
            for c in range(2):
                tg[1, c] = gates(2 + c, (1, 3), lambda t: gc[:, c, t, :])
            flush("mem")
            grow = ht
            t_gr = load(grow, I["g_ffn_2"].to_broadcast([P, D]), Q.last["tensor"], Q.last["vector"], Q.last["scalar"])

            def branch(btoks, g, gt):
                tb = linear(("br",), 4, lbh, lbl, btoks, YB)
                tks = []
                for c in range(2):
                    for t in range(T):
                        b = YB[t][c]
                        o = gt(c, t)
                        tk = dve(lambda e: e.tensor_tensor(o, o, PB[b], ALU.mult), tg[g, c], tb)
                        free[b] = [tk]
                        if g != 0:
                            tk = dve(lambda e: e.tensor_tensor(ga[:, c, t, :], ga[:, c, t, :], o, ALU.add))
                        filler(1)
                return tk

            fill_rate[0] = 3
            after_unit[0] = lambda: filler(fill_rate[0])
            branch(btoks, 0, lambda c, t: ga[:, c, t, :])
            btoks = to_T(lambda t, k: om[:, t, k * P:(k + 1) * P], 4, bh, bl, waits=ix["mem"],
                         wdst=[Q.last["tensor"]])
            branch(btoks, 2, lambda c, t: gm[c][:, t, :])
            filler(999)
            fill_rate[0] = 0
            tcv = [conv_done[0], Q.last["vector"]]

            for k0 in range(4):
                for t in range(T):
                    tp = pe(lambda e: e.transpose(PB[6 + t][:, k0 * P:(k0 + 1) * P], yc[:, k0, t * P:(t + 1) * P],
                                                  ident[:, :]), tcv, free[6 + t])
            for t in range(T):
                s6, s2 = st[:, 20 + 8 * t:26 + 8 * t], st[:, 40 + 2 * t:42 + 2 * t]
                dve(lambda e: e.bn_stats(s6, PB[6 + t]), tp)
                dve(lambda e: e.bn_aggr(s2, s6))
                dve(lambda e: e.tensor_copy(st[:, 50 + t:51 + t], s2[:, 1:2]))
            rstd(st[:, 52:54], st[:, 50:52], 1)
            for t in range(T):
                tk = dve(lambda e: e.tensor_scalar(om[:, t, :], PB[6 + t], st[:, 40 + 2 * t:41 + 2 * t],
                                                   st[:, 52 + t:53 + t], ALU.subtract, ALU.mult),
                         Q.last["tensor"])
                free[6 + t] = [tk]
            btoks = to_T(lambda t, k: om[:, t, k * P:(k + 1) * P], 4, bh, bl, scale=lambda k: col("ln_g_2", k),
                         bias=lambda k: col("ln_b_2", k), func=ACT.Silu, waits=[tk], wdst=[Q.last["tensor"], tk])
            tk = branch(btoks, 1, lambda c, t: gc[:, c, t, :])
            toks = to_T(lambda t, k: ga[:, k // 4, t, (k % 4) * P:(k % 4 + 1) * P], KD, hh, hl,
                        waits=[tk], wdst=[Q.last["tensor"]])
            tok = linear(("wo",), KD, lh, ll, toks, YB)
            for t in range(T):
                for h in range(2):
                    xs = x[:, t, h * 512:(h + 1) * 512]
                    tk = dve(lambda e, xs=xs, t=t, h=h: e.tensor_tensor(xs, xs, ypsum(t, h), ALU.add), tok)
                    free[YB[t][h]] = [tk]
            x_tok[:] = [tk]

            at[0] = XN_END
            hf = arena(KD, S)
            wr = arena(KD, 36)
            rbias = arena(36)
            tw = [load(wr[:, :, 0:4], I["w_rg_2"][0].rearrange("(k p) n -> p k n", p=P), x_tok),
                  load(wr[:, :, 4:36], I["w_re_2"][0].rearrange("(k p) n -> p k n", p=P), x_tok),
                  load(rbias[:, 0:4], I["b_rg_2"].to_broadcast([P, 4]), x_tok),
                  load(rbias[:, 4:36], I["b_re_2"].to_broadcast([P, 32]), x_tok)]
            tie = arena(8)
            tw.append(load(tie, I["tie_c"].to_broadcast([P, 8]), x_tok))
            lg = arena(T, 36)
            sm_ = arena(T, 128)
            tri = arena(2, P)
            iota = arena(P)
            tw += [load(tri, I["tri_c"].rearrange("p (a b) -> p a b", b=P), x_tok),
                   load(iota, I["iota_c"].to_broadcast([P, P]), x_tok)]
            sel = [arena(T, P) for _ in range(2)]
            selT = [arena(264) for _ in range(2)]
            ysb = arena(D)
            xo = arena(T, D)
            gx = xn
            tk = prenorm(x_tok, gain=grow, tg=t_gr)
            hft = []
            for k0 in range(0, KD, 2):
                b = RB[(k0 // 2) % 4]
                for k in range(2):
                    for t in range(T):
                        tp = pe(lambda e: e.transpose(PB[b][:, k * S + t * P:k * S + (t + 1) * P],
                                                      rows_xn(t, k0 + k), ident[:, :]), tk, free[b])
                dst, ps = hf[:, k0:k0 + 2, :], PB[b].rearrange("p (k n) -> p k n", n=S)
                if k0 % 4:
                    tf = dve(lambda e: e.tensor_copy(dst, ps), tp)
                else:
                    tf = act(lambda e: e.activation(dst, ps, ACT.Copy), tp)
                free[b] = [tf]
                hft += [tf, tf]
            for t in range(T):
                for k in range(KD):
                    tp = pe(lambda e: e.matmul(PB[2][:, t * 36:t * 36 + 36], hf[:, k, t * P:(t + 1) * P],
                                               wr[:, k, :], start=(k == 0), stop=(k == KD - 1)),
                            hft[k], tw, free[2])

            def wide(v, n):
                return v.unsqueeze(2).to_broadcast([P, T, n])

            def first_of(dst, v, mx, n, tmp):
                dve(lambda e: e.tensor_tensor(dst, v, wide(mx, n), ALU.is_equal))
                dve(lambda e: e.tensor_tensor(dst, dst, tie[:, 8 - n:8].unsqueeze(1).to_broadcast([P, T, n]), ALU.mult))
                dve(lambda e: e.tensor_reduce(tmp, dst, AX_X, ALU.max))
                return dve(lambda e: e.tensor_tensor(dst, dst, wide(tmp, n), ALU.is_equal))

            tk = dve(lambda e: e.tensor_tensor(lg, PB[2][:, 0:72].rearrange("p (t n) -> p t n", n=36),
                                               rbias.unsqueeze(1).to_broadcast([P, T, 36]), ALU.add), tp)
            free[2] = [tk]
            gl = lg[:, :, 0:4]
            one_ = lambda i: sm_[:, :, i]
            gmx, gs, tmp, dv, ez, w1, w2, rk = (one_(i) for i in (0, 1, 2, 3, 12, 13, 14, 15))
            oh, ge = sm_[:, :, 4:8], sm_[:, :, 8:12]
            ein, o1, o2, e2, v8 = (sm_[:, :, i:i + 8] for i in (16, 24, 32, 40, 48))
            pe_ = sm_[:, :, 64:96]
            dve(lambda e: e.tensor_reduce(gmx, gl, AX_X, ALU.max))
            t_oh = first_of(oh, gl, gmx, 4, tmp)
            cnt = PB[3][:, 0:12]
            for t in range(T):
                pe(lambda e: e.matmul(cnt[:, 4 * t:4 * t + 4], tri[:, 0, :], oh[:, t, :], start=True, stop=(t == 0)),
                   t_oh, tw, free[3])
            pe(lambda e: e.matmul(cnt[:, 4:8], tri[:, 1, :], oh[:, 0, :], start=False, stop=True))
            for t in range(T):
                tp = pe(lambda e: e.matmul(cnt[:, 8:12], tri[:, 1, :], oh[:, t, :], start=(t == 0), stop=(t == 1)))
            tn = dve(lambda e: e.tensor_tensor(ge, gl, wide(gmx, 4), ALU.subtract))
            t_ge = act(lambda e: e.activation(ge, ge, ACT.Exp), tn)
            p4 = pe_.rearrange("p t (g e) -> p t g e", e=8)
            for t in range(T):
                dve(lambda e: e.tensor_tensor(p4[:, t, :, :], lg[:, t, 4:36].rearrange("p (g e) -> p g e", e=8),
                                              oh[:, t, :].unsqueeze(2).to_broadcast([P, 4, 8]), ALU.mult))
            dve(lambda e: e.tensor_reduce(ein, pe_.rearrange("p t (g e) -> p t e g", e=8), AX_X, ALU.add))
            c3 = cnt[:, 0:8].rearrange("p (t g) -> p t g", g=4)
            c4 = sm_[:, :, 56:60]
            dve(lambda e: e.tensor_tensor(c4, c3, oh, ALU.mult), tp)
            dve(lambda e: e.tensor_reduce(rk, c4, AX_X, ALU.add))
            dve(lambda e: e.tensor_reduce(sm_[:, 0, 60:61], cnt[:, 8:12], AX_X, ALU.max))
            t_flag = dve(lambda e: e.tensor_scalar(flag[:, 0:1], sm_[:, 0, 60:61], 128.5, None, ALU.is_gt))
            free[3] = [t_flag]

            half = lambda a, i: a[:, :, :].rearrange("p k n -> p (k n)")[:, i * D:(i + 1) * D].rearrange(
                "p (k n) -> p k n", n=P)
            GH, GL = [half(hh, i) for i in range(2)], [half(hl, i) for i in range(2)]
            done_up, done_y, sel_tok, gtok, ct_tok, back = {}, {}, {}, {}, {}, {}

            def build_sel(g):
                for t in range(T):
                    tk = dve(lambda e: e.tensor_scalar(sel[g % 2][:, t, :], iota, sm_[:, t, 15:16],
                                                       sm_[:, t, 4 + g:5 + g], ALU.is_equal, ALU.mult),
                             tw, gtok.get(("pe", g - 2)))
                sel_tok[g] = tk

            def build_back(g, b=7):
                for t in range(T):
                    pe(lambda e: e.transpose(PB[b][:, t * P:(t + 1) * P], sel[g % 2][:, t, :], ident[:, :]),
                       sel_tok[g], free[b])
                for t in range(T):
                    tp = pe(lambda e: e.matmul(PB[b][:, 256:264], sel[g % 2][:, t, :], comb[:, t, g * 8:g * 8 + 8],
                                               start=(t == 0), stop=(t == 1)), t_comb)
                ct_tok[g] = act(lambda e: e.activation(selT[g % 2], PB[b][:, 0:264], ACT.Copy), tp, back.get(g - 2),
                                done_w.get(g - 2))
                free[b] = [ct_tok[g]]

            def gather(g, q, b=7):
                for k in range(4 * q, 4 * q + 4):
                    for t in range(T):
                        tp = pe(lambda e: e.matmul(PB[b][:, (k % 4) * P:(k % 4 + 1) * P], gx[:, t, k * P:(k + 1) * P],
                                                   sel[g % 2][:, t, :], start=(t == 0), stop=(t == 1)),
                                sel_tok[g], free[b])
                gtok["pe", g] = tp
                ps = PB[b].rearrange("p (k n) -> p k n", n=P)
                H, L = GH[g % 2][:, 4 * q:4 * q + 4, :], GL[g % 2][:, 4 * q:4 * q + 4, :]
                th = act(lambda e: e.activation(H, ps, ACT.Copy), tp, done_up.get(g - 2))
                tl = dve(lambda e: e.tensor_tensor(L, ps, H.bitcast(F32), ALU.subtract), th)
                free[b] = [th, tl]
                gtok[g, q] = [th, tl]

            def take_y(g):
                bk = 2 * (g % 2)
                done_y["sb", g] = act(lambda e: e.activation(
                    ysb, PS[:, bk:bk + 2, :].rearrange("p a b -> p (a b)"), ACT.Copy), done_y[g], back.get(g - 1))
                free[bk] = free[bk + 1] = [done_y["sb", g]]

            def scatter(g, t, h, b=7):
                tp = pe(lambda e: e.matmul(PB[b], selT[g % 2][:, t * P:(t + 1) * P], ysb[:, h * 512:(h + 1) * 512],
                                           start=True, stop=True), done_y["sb", g], ct_tok[g], free[b])
                back[g] = tp
                o, r = xo[:, t, h * 512:(h + 1) * 512], (x if g == 0 else xo)[:, t, h * 512:(h + 1) * 512]
                free[b] = [dve(lambda e: e.tensor_tensor(o, r, PB[b], ALU.add), tp)]

            done_w = {}
            build_sel(0)
            gather(0, 0, 4)
            gather(0, 1, 5)

            for t in range(T):
                dve(lambda e: e.max(v8[:, t, :], ein[:, t, :]))
            first_of(o1, ein, v8[:, :, 0], 8, tmp)
            dve(lambda e: e.scalar_tensor_tensor(e2, o1, MARK, ein, ALU.mult, ALU.add))
            first_of(o2, e2, v8[:, :, 1], 8, tmp)
            tn = dve(lambda e: e.tensor_tensor(dv, v8[:, :, 1], v8[:, :, 0], ALU.subtract))
            ta = act(lambda e: e.activation(ez, dv, ACT.Exp), tn)
            dve(lambda e: e.tensor_reduce(gs, ge, AX_X, ALU.add), t_ge)
            dve(lambda e: e.reciprocal(gs, gs))
            dve(lambda e: e.tensor_scalar(w1, ez, 1.0, None, ALU.add), ta)
            dve(lambda e: e.reciprocal(w1, w1))
            dve(lambda e: e.tensor_tensor(w1, w1, gs, ALU.mult))
            dve(lambda e: e.tensor_tensor(w2, w1, ez, ALU.mult))
            dve(lambda e: e.tensor_tensor(o1, o1, wide(w1, 8), ALU.mult))
            dve(lambda e: e.tensor_tensor(o2, o2, wide(w2, 8), ALU.mult))
            dve(lambda e: e.tensor_tensor(o1, o1, o2, ALU.add))
            for t in range(T):
                t_comb = dve(lambda e: e.tensor_tensor(
                    comb[:, t, :].rearrange("p (g e) -> p g e", e=8), o1[:, t, :].unsqueeze(1).to_broadcast([P, 4, 8]),
                    oh[:, t, :].unsqueeze(2).to_broadcast([P, 4, 8]), ALU.mult))
            build_back(0)

            ugf, gtf, gtt, sgf, ugt = [[], []], [[], []], [[], []], [[], []], [[], []]
            upart = [ug[i][:, 0, :] for i in range(2)]

            def spread(b):
                i = b % 2
                for f in range(2):
                    tp = pe(lambda e: e.transpose(PB[6][:, f * P:(f + 1) * P], upart[i][:, f * P:(f + 1) * P],
                                                  ident[:, :]), ugt[i], free[6])
                ps = PB[6][:, 0:256].rearrange("p (a b) -> p a b", b=P)
                H, L = gT_h[i][:, :, 0:P], gT_l[i][:, :, 0:P]
                th = act(lambda e: e.activation(H, ps, ACT.Copy), tp, gtf[i])
                tl = dve(lambda e: e.tensor_tensor(L, ps, H.bitcast(F32), ALU.subtract), th)
                free[6] = [th, tl]
                ugf[i] = [tp]
                gtt[i] = [th, tl]

            def outp(b):
                i, g = b % 2, b // 8
                bk = 2 * (g % 2)
                tok = linear(("md", b), 2, lambda k, t: gT_h[i][:, k, 0:P], lambda k, t: gT_l[i][:, k, 0:P], gtt[i],
                             [[bk, bk + 1]], first=(b % 8 == 0), last=(b % 8 == 7), tiles=1)
                gtf[i] = [tok]
                if b % 8 == 7:
                    done_y[g] = tok
                    if g < 3:
                        put_off(0.1, lambda: take_y(g))
                        for t in range(T):
                            for h in range(2):
                                put_off(0.7, lambda t=t, h=h: scatter(g, t, h))

            rate[0] = 0.3
            for b in range(32):
                i, g = b % 2, b // 8
                if b % 8 == 0:
                    flush()
                if b % 8 == 2 and g < 3:
                    put_off(0.4, lambda g=g: build_sel(g + 1))
                    put_off(0.1, lambda g=g: build_back(g + 1))
                    for q in range(2):
                        put_off(0.6, lambda g=g, q=q: gather(g + 1, q))
                gl_ = [gtok[g, k // 4] for k in range(KD)]
                tok = linear(("mu", b), KD, lambda k, t: GH[g % 2][:, k, :], lambda k, t: GL[g % 2][:, k, :], gl_,
                             [[AB[i]]], mid=(lambda: spread(b - 1)) if b else None, tiles=1)
                done_up[g] = tok
                ta = act(lambda e: e.activation(sg[:, i, :], PB[AB[i]][:, 0:256], ACT.Silu), tok, sgf[i])
                td = dve(lambda e: e.scalar_tensor_tensor(upart[i], sg[:, i, :], selT[g % 2][:, 256 + b % 8:257 + b % 8],
                                                          PB[AB[i]][:, 256:512], ALU.mult, ALU.mult),
                         ta, ugf[i], ct_tok[g])
                done_w[g] = td
                free[AB[i]] = [ta, td]
                sgf[i] = [td]
                ugt[i] = [td]
                if b:
                    outp(b - 1)
            spread(31)
            outp(31)
            flush()
            take_y(3)
            outs = []
            for t in range(T):
                for h in range(2):
                    scatter(3, t, h, (7, 4, 5, 6)[2 * t + h])
                outs.append(load(out_ap[0, t * P:(t + 1) * P, :], xo[:, t, :], Q.last["vector"], q="sync"))
            if Q.active in (None, "sync"):
                Q.wait(outs)

            def dense():
                barrier = [Q.last[n] for n in ("tensor", "vector", "scalar")]
                if Q.active != "gpsimd":
                    Q.wait(barrier)
                limit[0] = len(chunks)
                pump()
                rate[0] = 1.5
                for i in range(8):
                    free[i] = []
                ff.update(ug=[[], []], gt=[[], []], sg=[])
                th = act(lambda e: e.activation(hh[:, :, :], hf, ACT.Copy))
                tl = dve(lambda e: e.tensor_tensor(hl[:, :, :], hf, hh[:, :, :].bitcast(F32), ALU.subtract), th)
                tok = ffn_like(32, lambda b: ("mu", b), lambda b: ("md", b), [th, tl], lambda b: None, combine=t_comb)
                last_out = []
                for t in range(T):
                    for h in range(2):
                        xs = x[:, t, h * 512:(h + 1) * 512]
                        tk = dve(lambda e, xs=xs, t=t, h=h: e.tensor_tensor(xs, xs, ypsum(t, h), ALU.add), tok)
                    last_out.append(load(out_ap[0, t * P:(t + 1) * P, :], x[:, t, :], tk, q="sync"))
                if Q.active in (None, "sync"):
                    Q.wait(last_out)

            if Q.active is None:
                Q.wait([t_flag])
                dense()
            elif Q.active != "gpsimd":
                Q.wait([t_flag])
                over = Q.eng.value_load(flag[0:1, 0:1], min_val=0, max_val=1)
                with Q.eng.If(over == 1):
                    dense()
            else:
                dense()
            assert cpos[0] == len(chunks), (cpos, len(chunks))

        flow()
        Q.counted()
        block = ctx.enter_context(nc.Block())

        def emit(name):
            def body(eng):
                Q.begin(name, eng)
                flow()
            return body

        block.tensor(emit("tensor"))
        block.vector(emit("vector"))
        block.scalar(emit("scalar"))
        block.gpsimd(emit("gpsimd"))
        block.sync(emit("sync"))


_INS = ["x", "c", "ada_w", "ada_b", "norm_g", "ffn_w_in", "ffn_w_out", "pool_w", "pool_b", "pool_scale",
        "mla_w_in", "mla_q_norm", "mla_kv_norm", "mla_w_uq", "mla_w_uk", "mla_w_uv", "mla_w_o", "mem_2",
        "g_mix_2", "w_in_2", "b_gate_2", "g_qa_2", "g_ka_2", "g_idx_k_2", "conv_w_2", "conv_b_2", "ln_g_2",
        "ln_b_2", "g_mem_2", "w_mem_kv_2", "g_qm_2", "g_km_2", "w_br_a_2", "w_br_b_2", "w_br_m_2", "w_o_2",
        "g_ffn_2", "w_rg_2", "b_rg_2", "w_re_2", "b_re_2", "w_up_2", "w_down_2"]


def _constants():
    f = np.float32
    out = {"ident_c": np.eye(P, dtype=f)}
    out["tri_c"] = np.concatenate([np.triu(np.ones((P, P), f), 1), np.ones((P, P), f)], 1)
    out["iota_c"] = np.arange(P, dtype=f)[None, :]
    out["sum4_c"] = np.tile((np.arange(P) % 32 == 0).astype(f)[:, None], (1, P))
    t = np.arange(S)
    rc = []
    for w in (2, 4, 8, 16):
        n = np.clip(t + w // 2, 0, S) - np.clip(t - w // 2, 0, S)
        rc.append(1.0 / n)
    out["rc_c"] = np.asarray(rc, dtype=f)
    for half, name in ((16, "rope16_c"), (32, "rope32_c")):
        inv = (10000.0 ** (-(np.arange(half, dtype=f) / f(half)))).astype(f)
        ang = (t.astype(f)[:, None] * inv[None, :]).astype(f).astype(np.float64)
        cs = np.stack([np.cos(ang), np.sin(ang)])
        out[name] = np.ascontiguousarray(cs.reshape(2, T, P, half).transpose(2, 0, 1, 3).reshape(P, -1)).astype(f)
    ca = (t[None, :] <= t[:, None]).astype(f)
    ca = np.where(ca > 0, f(3e38), f(NEG))
    out["cap_c"] = np.ascontiguousarray(ca.reshape(T, P, S).transpose(1, 0, 2).reshape(P, -1))
    out["tie_c"] = np.arange(8, 0, -1).astype(f)[None, :]
    return out


def kernel(**inputs):
    import numpy as _np
    import concourse.bacc as _bacc
    from concourse import mybir as _mybir
    from concourse.bass_utils import run_bass_kernel_spmd as _run

    nc = _bacc.Bacc("TRN2", target_bir_lowering=False, num_devices=1)
    arrays, aps = {}, {}
    named = {n: _np.ascontiguousarray(inputs[n]) for n in _INS}
    named.update(_constants())
    for name, a in named.items():
        arrays[f"in_{name}"] = a
        aps[name] = nc.dram_tensor(f"in_{name}", a.shape, _mybir.dt.from_np(a.dtype), kind="ExternalInput").ap()
    out = nc.dram_tensor("out_0", (1, S, D), F32, kind="ExternalOutput").ap()
    build(nc, aps, out)
    r = _run(nc, [arrays], core_ids=[0])
    return r.results[0]["out_0"]
```

```python
from contextlib import ExitStack

import numpy as np

import concourse.bass as bass
from concourse import mybir

F32 = mybir.dt.float32
F32R = mybir.dt.float32r
I32 = mybir.dt.int32
ACT = mybir.ActivationFunctionType
ALU = mybir.AluOpType
AX_X = mybir.AxisListType.X

P = 128
T = 2
S = 256
D = 1024
KD = D // P
EPS = 1e-6
CHUNK = 2048
UNIT = 1024
NRAW = 6
NUNIT = 6
NFF = 11
PE_TAPS = 12
ARENA = 11460
NEG = -1e30
MARK = -3e38
PROJ = [(1352, 512), (1864, 512), (1280, 72), (768, 512), (0, 512), (512, 256), (2376, 512)]
GATE0 = 2888
CONVW = 31


class Tok:

    def __init__(self, queue, index, sem, value):
        self.queue, self.index, self.sem, self.value = queue, index, sem, value


class Queues:

    NAMES = ("tensor", "vector", "scalar", "gpsimd", "sync")

    def __init__(self, sems):
        self.sems = sems
        self.wanted = {n: set() for n in self.NAMES}
        self.values = {}
        self.begin(None, None)

    def begin(self, name, eng):
        self.active, self.eng = name, eng
        self.at = {n: 0 for n in self.NAMES}
        self.last, self.seen = {}, {}

    def counted(self):
        for n in self.NAMES:
            self.values[n] = {index: k + 1 for k, index in enumerate(sorted(self.wanted[n]))}

    def wait(self, waits):
        if self.active is None:
            for w in waits:
                if w.queue is not None:
                    self.wanted[w.queue].add(w.index)
            return
        need = {}
        for w in waits:
            if w.value > self.seen.get(w.sem.name, 0):
                if w.sem.name not in need or w.value > need[w.sem.name].value:
                    need[w.sem.name] = w
        for key, w in need.items():
            self.eng.wait_ge(w.sem, w.value)
            self.seen[key] = w.value

    def put(self, name, fn, waits, own=True):
        index = self.at[name]
        self.at[name] += 1
        waits = flat(waits)
        if own and name in self.last and name != "tensor":
            waits.append(self.last[name])
        value = self.values[name].get(index) if self.values else None
        tok = Tok(name, index, self.sems[name], value)
        self.last[name] = tok
        if self.active in (None, name):
            self.wait(waits)
        if self.active == name:
            ins = fn(self.eng)
            if value is not None:
                ins.then_inc(tok.sem, 1)
        return tok

    def dma(self, name, fn, waits, sem, value):
        if self.active in (None, name):
            self.wait(flat(waits))
        if self.active == name:
            fn(self.eng).then_inc(sem, 16)
        return Tok(None, None, sem, value)


def flat(x):
    if x is None:
        return []
    if isinstance(x, Tok):
        return [x]
    return [t for y in x for t in flat(y)]


def build(nc, I, out_ap):
    ctx = ExitStack()
    with ctx:
        def sb(name, shape, dt=F32):
            return ctx.enter_context(nc.sbuf_tensor(name, shape, dt))

        named = {}

        def sem(name):
            if name not in named:
                named[name] = ctx.enter_context(nc.semaphore(name))
            return named[name]

        Q = Queues({n: sem(f"done_{n}") for n in Queues.NAMES})

        def pe(fn, *w):
            return Q.put("tensor", fn, w)

        def dve(fn, *w, own=True):
            return Q.put("vector", fn, w, own)

        def act(fn, *w, own=True):
            return Q.put("scalar", fn, w, own)

        PS = ctx.enter_context(nc.psum_tensor("banks", [P, 8, 512], F32))
        PB = [PS[:, i, :] for i in range(8)]
        YB = [[0, 1], [2, 3]]
        AB = [4, 5]

        raw = [sb(f"raw{i}", [P, CHUNK]) for i in range(NRAW)]
        uh = [sb(f"uh{i}", [P, UNIT], F32R) for i in range(NUNIT)]
        ul = [sb(f"ul{i}", [P, UNIT], F32R) for i in range(NUNIT)]
        ident = sb("ident", [P, P])
        x = sb("x", [P, T, D])
        hh = sb("hh", [P, KD, S], F32R)
        hl = sb("hl", [P, KD, S], F32R)
        Gs = sb("Gs", [P, 3, D])
        G = [Gs[:, i, :] for i in range(3)]
        bh = sb("bh", [P, 4, S], F32R)
        bl = sb("bl", [P, 4, S], F32R)
        gT_h = [bh[:, 2 * i:2 * i + 2, :] for i in range(2)]
        gT_l = [bl[:, 2 * i:2 * i + 2, :] for i in range(2)]
        sg = sb("sg", [P, T, 256])
        ug = [sb(f"ug{i}", [P, T, 256]) for i in range(2)]
        full = sb("full", [P, 2, 512])
        ab = sb("ab", [P, 6, 2, KD])
        ngc = sb("ngc", [P, 96])
        cc = sb("cc", [P, 48])
        sc = sb("sc", [P, KD])
        st = sb("st", [P, 280])
        flag = st[:, 276:278].bitcast(I32)
        comb = Gs[:, 0, 0:64].rearrange("p (t n) -> p t n", t=T)
        AR = sb("arena", [P, ARENA])
        adab = sb("adab", [P, 512])
        kvm = sb("kvm", [P, 2, T, 512])
        sum4 = sb("sum4", [P, P])

        def flow():
            free = {i: [] for i in range(8)}
            at = [0]

            def arena(*shape):
                n = int(np.prod(shape))
                a = AR[:, at[0]:at[0] + n]
                at[0] += n
                assert at[0] <= ARENA, at[0]
                if len(shape) == 2:
                    a = a.rearrange("p (a b) -> p a b", b=shape[1])
                elif len(shape) == 3:
                    a = a.rearrange("p (a b c) -> p a b c", b=shape[1], c=shape[2])
                return a

            chunks = []

            def plan_rows(key, w, k0, kk, c0, n, conv=True):
                v = w.rearrange("(k p) n -> p k n", p=P)[:, k0:k0 + kk, c0:c0 + n]
                chunks.append((key, [(v, kk, n, 0)], kk, n, conv))

            def plan_block(key, w, c0, n, K=KD):
                for k0 in range(0, K, 4):
                    plan_rows(key, w, k0, 4, c0, n)

            def plan_wide(key, w, r0):
                v = w[r0:r0 + 256, :].rearrange("(k p) n -> p k n", p=P)
                chunks.append((key, [(v, 2, D, 0)], 2, D, True))

            def plan_ffn_block(key, i, s, b):
                w = I["ffn_w_in"][i, s].rearrange("(k p) (g n) -> p k g n", p=P, g=2)
                for k0 in (0, 4):
                    pcs = [(w[:, k0:k0 + 4, g, b * 256:(b + 1) * 256], 4, 512, g * 256) for g in (0, 1)]
                    chunks.append((key, pcs, 4, 512, True))

            def plan_ada(i, j):
                w = I["ada_w"][i]
                for k0 in (0, 4):
                    plan_rows(("ada", i, j), w, k0, 4, j * 512, 512, conv=False)

            ada_order = [(i, j) for i in range(2) for j in range(18)]
            ADA_AT, ada_gap = {}, {}
            left = ada_order[4:]
            for i_, s_, n_, g_ in ((0, 0, 11, 3), (0, 1, 6, 2), (1, 0, 2, 2)):
                for b_ in range(n_):
                    ADA_AT[(i_, s_, b_ if n_ > 6 else b_ + 2)] = [left.pop(0)]
                if g_ == 3:
                    ada_pool = [left.pop(0) for _ in range(3)]
                    ada_gap[(0, 0)] = [left.pop(0) for _ in range(2)]
                else:
                    ada_gap[(i_, s_)] = [left.pop(0) for _ in range(2)]
            ada_mla = [left.pop(0) for _ in range(4)]
            assert not left

            def plan_ffn(i, s):
                for b in range(NFF):
                    plan_ffn_block(("fi", i, s, b), i, s, b)
                    if b:
                        plan_wide(("fo", i, s, b - 1), I["ffn_w_out"][i, s], (b - 1) * 256)
                    for a in ADA_AT.get((i, s, b), []):
                        plan_ada(*a)
                plan_wide(("fo", i, s, NFF - 1), I["ffn_w_out"][i, s], (NFF - 1) * 256)

            for a in ada_order[:4]:
                plan_ada(*a)
            plan_ffn(0, 0)
            for b in range(2):
                plan_block(("kv",), I["w_mem_kv_2"][0], b * 512, 512)
            for a in ada_pool:
                plan_ada(*a)
            chunks.append((("pw",), [(I["pool_w"][0].rearrange("g (k p) n -> p (g k) n", p=P), 8, 256, 0)], 8, 256, False))
            for a in ada_gap[0, 0]:
                plan_ada(*a)
            plan_ffn(0, 1)
            for a in ada_gap[0, 1]:
                plan_ada(*a)
            plan_ffn(1, 0)
            for a in ada_gap[1, 0]:
                plan_ada(*a)
            plan_block(("mi",), I["mla_w_in"][0], 0, 416)
            plan_ada(*ada_mla[0])
            for nm in ("mla_w_uk", "mla_w_uv"):
                v = I[nm].rearrange("a c h d -> c a (h d)")
                chunks.append(((nm,), [(v, 1, 1024, 0)], 1, 1024, False))
            for k in range(2):
                v = I["mla_w_uq"][0].rearrange("(k p) h d -> p k (h d)", p=P)[:, k:k + 1, :]
                chunks.append((("uq",), [(v, 1, 1536, 0)], 1, 1536, False))
            plan_ada(*ada_mla[1])
            for k in range(4):
                plan_wide(("mo",), I["mla_w_o"][0], k * 256)
            for a in ada_mla[2:]:
                plan_ada(*a)
            plan_ffn(1, 1)
            for c0, n in PROJ:
                plan_block(("pj",), I["w_in_2"][0], c0, n)
            for g in (0, 2, 1):
                for c in range(2):
                    plan_block(("gt",), I["w_in_2"][0], GATE0 + g * 1024 + c * 512, 512)
            for nm in ("w_br_a_2", "w_br_m_2", "w_br_b_2"):
                for k in range(2):
                    plan_wide(("br",), I[nm][0], k * 256)
            for k in range(4):
                plan_wide(("wo",), I["w_o_2"][0], k * 256)
            limit = [0]
            for _ in range(2):
                for b in range(32):
                    plan_block(("mu", b), I["w_up_2"][0, b], 0, 512)
                    if b:
                        plan_wide(("md", b - 1), I["w_down_2"][0, b - 1], 0)
                plan_wide(("md", 31), I["w_down_2"][0, 31], 0)
                limit[0] = limit[0] or len(chunks)

            ring_sem = [sem(f"ring{i}") for i in range(NRAW)]
            dma_tok, chunk_rel = {}, {}
            nxt = [0]

            def pump():
                while nxt[0] < limit[0] and (nxt[0] < NRAW or nxt[0] - NRAW in chunk_rel):
                    m = nxt[0]
                    key, pcs, kk, n, conv = chunks[m]
                    waits = chunk_rel[m - NRAW] if m >= NRAW else []
                    slot = raw[m % NRAW][:, 0:kk * n].rearrange("p (k n) -> p k n", n=n)
                    base = fills[m % NRAW]
                    for v, k_, n_, c0 in pcs:
                        w = v.shape[-1]
                        base += 16
                        tok = Q.dma("sync", lambda e, d=slot[:, :, c0:c0 + w], v=v: e.dma_start(d, v), waits,
                                    ring_sem[m % NRAW], base)
                    fills[m % NRAW] = base
                    dma_tok[m] = tok
                    nxt[0] += 1

            fills = [0] * NRAW
            units = []
            for m, (key, pcs, kk, n, conv) in enumerate(chunks):
                if conv:
                    for h in range(2):
                        units.append((m, h, kk // 2, n))
            unit_rel, unit_tok = {}, {}
            cpos, upos, conv_pos = [0], [0], [0]

            def convert(u):
                m, h, kk, n = units[u]
                w = kk * n
                src = raw[m % NRAW][:, h * w:(h + 1) * w]
                r = u % NUNIT
                th = act(lambda e: e.activation(uh[r][:, 0:w], src, ACT.Copy), dma_tok[m],
                         unit_rel[u - NUNIT] if u >= NUNIT else [], own=False)
                tl = dve(lambda e: e.tensor_tensor(ul[r][:, 0:w], src, uh[r][:, 0:w].bitcast(F32), ALU.subtract),
                         th, own=False)
                unit_tok[u] = tl
                if h == 1:
                    chunk_rel[m] = [tl]
                    pump()

            def ahead(u):
                while conv_pos[0] < len(units) and conv_pos[0] <= u + NUNIT - 1:
                    c = conv_pos[0]
                    if c >= NUNIT and c - NUNIT not in unit_rel:
                        break
                    if units[c][0] not in dma_tok:
                        break
                    convert(c)
                    conv_pos[0] += 1

            later, rate, spent, after_unit = [], [1.5], [0.0], [lambda: None]

            def step(budget):
                spent[0] = min(spent[0] + budget, budget)
                while later and spent[0] > 0:
                    w, fn = later.pop(0)
                    spent[0] -= w
                    fn()

            def flush(mark=None):
                while later and not (mark is not None and mark in done_marks):
                    later.pop(0)[1]()
                spent[0] = 0.0

            done_marks = set()

            def put_off(weight, fn):
                later.append((weight, fn))

            def put_mark(mark):
                later.append((0.0, lambda: done_marks.add(mark)))

            def take_unit(key):
                u = upos[0]
                while u not in unit_tok:
                    ahead(u)
                    if u not in unit_tok:
                        assert later, (u, units[u], chunks[units[u][0]][0])
                        later.pop(0)[1]()
                m, h, kk, n = units[u]
                assert m == cpos[0], (chunks[m][0], chunks[cpos[0]][0], key)
                assert chunks[m][0][:len(key)] == key, (chunks[m][0], key)
                upos[0] += 1
                if h == 1:
                    cpos[0] += 1
                ahead(u)
                r = u % NUNIT
                hi = uh[r][:, 0:kk * n].rearrange("p (k n) -> p k n", n=n)
                lo = ul[r][:, 0:kk * n].rearrange("p (k n) -> p k n", n=n)
                return u, hi, lo, kk, n, unit_tok[u]

            def take_raw(key):
                m = cpos[0]
                k, pcs, kk, n, conv = chunks[m]
                assert k[:len(key)] == key and not conv, (k, key)
                cpos[0] += 1
                return m, raw[m % NRAW][:, 0:kk * n].rearrange("p (k n) -> p k n", n=n), dma_tok[m]

            def give_raw(m, tok):
                chunk_rel[m] = [tok]
                pump()

            def linear(key, K, lhi, llo, lt, banks, first=True, last=True, mid=None, tiles=T):
                k = 0
                tok = None
                while k < K:
                    u, hi, lo, kk, n, ut = take_unit(key)
                    if mid is not None and k >= K // 2:
                        mid()
                        mid = None
                    for t in range(tiles):
                        for j in range(kk):
                            for c in range((n + 511) // 512):
                                w = min(512, n - c * 512)
                                o = PB[banks[t][c]][:, 0:w]
                                a, b = lhi(k + j, t), llo(k + j, t)
                                wh, wl = hi[:, j, c * 512:c * 512 + w], lo[:, j, c * 512:c * 512 + w]
                                s0 = first and k + j == 0
                                s1 = last and k + j == K - 1
                                pe(lambda e, o=o, a=a, wh=wh, s0=s0: e.matmul(o, a, wh, start=s0, stop=False),
                                   ut, lt[k + j] if isinstance(lt, list) and lt and isinstance(lt[0], list) else lt,
                                   free[banks[t][c]] if s0 else [])
                                pe(lambda e, o=o, a=a, wl=wl: e.matmul(o, a, wl, start=False, stop=False))
                                tok = pe(lambda e, o=o, b=b, wh=wh, s1=s1: e.matmul(o, b, wh, start=False, stop=s1))
                    unit_rel[u] = [tok]
                    k += kk
                    step(rate[0])
                    after_unit[0]()
                ahead(upos[0] - 1)
                return tok

            loads = [0]

            def load(dst, src, *w, q="gpsimd"):
                loads[0] += 1
                s = sem(f"load{loads[0]}")
                return Q.dma(q, lambda e: e.dma_start(dst, src), w, s, 16)

            stk0 = G[2][0:8, 256:384]
            t_c = load(stk0, I["c"].rearrange("a (k p) -> (a k) p", p=P), q="sync")
            t_id = load(ident[:, :], I["ident_c"], q="sync")
            t_ab = load(adab[0:36, :], I["ada_b"].rearrange("i (j n) -> (i j) n", n=512), q="sync")
            t_s4 = load(sum4[:, :], I["sum4_c"], q="sync")
            pump()
            stk1 = G[2][0:96, 0:128]
            stk2 = G[2][0:48, 128:256]
            t_n = load(stk1, I["norm_g"].rearrange("i m (k p) -> (i m k) p", p=P), q="scalar")
            t_x = [load(x[:, t, :], I["x"][0, t * P:(t + 1) * P, :], q="scalar") for t in range(T)]
            l2 = []
            r0 = 0
            where = {}
            for nm, rows in (("mla_q_norm", 2), ("mla_kv_norm", 1), ("g_mix_2", 8), ("conv_b_2", 4),
                             ("ln_g_2", 4), ("ln_b_2", 4), ("g_mem_2", 8)):
                l2.append(load(stk2[r0:r0 + rows, :], I[nm].rearrange("a (k p) -> (a k) p", p=P)))
                where[nm] = r0
                r0 += rows

            def col(nm, k):
                return cc[:, where[nm] + k:where[nm] + k + 1]

            tp = pe(lambda e: e.transpose(PB[7][:, 0:8], stk0, ident[0:8, 0:8]), t_id, t_c)
            t_sc = act(lambda e: e.activation(sc[:, :], PB[7][:, 0:8], ACT.Silu), tp)
            free[7] = [t_sc]
            tp = pe(lambda e: e.transpose(PB[6][:, 0:96], stk1, ident[0:96, 0:96]), t_n)
            t_ng = dve(lambda e: e.tensor_copy(ngc[:, :], PB[6][:, 0:96]), tp)
            free[6] = [t_ng]

            def small_columns():
                tp = pe(lambda e: e.transpose(PB[7][:, 0:r0], stk2[0:r0, :], ident[0:r0, 0:r0]), l2, free[7])
                t_cc = dve(lambda e: e.tensor_copy(cc[:, 0:r0], PB[7][:, 0:r0]), tp)
                free[7] = [t_cc]
                return t_cc

            g_tok, g_done = {}, {}

            def load_G(s, *w):
                i, m = s // 3, s % 3
                src = I["norm_g"][i, 2 * m + 1:2 * m + 2, :]
                g_tok[s] = load(G[s % 3][:, :], src.to_broadcast([P, D]), *w)

            load_G(0)
            load_G(1)
            ab_tok = {s: [] for s in range(6)}

            xn = arena(T, D)
            XN_END = at[0]
            def ada_end(i, j, tok, b=7):
                s, kind, half = i * 3 + j // 6, (j // 2) % 3, j % 2
                if kind == 2:
                    g = G[s % 3][:, half * 512:half * 512 + 512]
                    tk = dve(lambda e: e.scalar_tensor_tensor(g, PB[b], 1.0, g, ALU.add, ALU.mult), tok, g_tok[s])
                    g_done.setdefault(s, []).append(tk)
                else:
                    d = full[:, 1, :].rearrange("p (a b) -> p a b", b=P)
                    dve(lambda e: e.tensor_tensor(d, PB[b].rearrange("p (a b) -> p a b", b=P),
                                                  ident[:, :].unsqueeze(1).to_broadcast([P, 4, P]), ALU.mult),
                        tok, full_act)
                    dst = ab[:, s, 1 - kind, half * 4:half * 4 + 4]
                    tk = dve(lambda e: e.tensor_reduce(dst, d, AX_X, ALU.add))
                    if kind == 1:
                        gc = ngc[:, i * 48 + (s % 3) * 16 + half * 4:i * 48 + (s % 3) * 16 + half * 4 + 4]
                        tk = dve(lambda e: e.scalar_tensor_tensor(dst, dst, 1.0, gc, ALU.add, ALU.mult), t_ng)
                    ab_tok[s].append(tk)
                free[b] = [tk]

            def ada_parts(i, j, b):
                got = [take_raw(("ada", i, j)) for _ in range(2)]
                r = i * 18 + j
                pe(lambda e: e.matmul(PB[b][0:32, :], ident[0:36, r:r + 1].to_broadcast([36, 32]),
                                      adab[0:36, :], start=True, stop=False), t_ab, t_id, free[b])
                for k in range(KD):
                    m, w, dt = got[k // 4]
                    g = (k + 1) % 4
                    tok = pe(lambda e: e.matmul(
                        PB[b][32 * g:32 * g + 32, :], sc[:, k:k + 1].to_broadcast([P, 32]), w[:, k % 4, :],
                        start=(k < 3), stop=(k >= 4)), dt, t_sc)
                    if k % 4 == 3:
                        give_raw(m, tok)
                return tok

            def ada_copy(i, j, b, buf, tok, *w):
                ada_s[i, j] = act(lambda e: e.activation(buf, PB[b], ACT.Copy), tok, full_pe, w)
                full_act[:] = [ada_s[i, j]]
                free[b] = [ada_s[i, j]]

            def ada_total(i, j, b, buf):
                tok = pe(lambda e: e.matmul(PB[b], sum4[:, :], buf, start=True, stop=True),
                         ada_s[i, j], t_s4, free[b])
                ada_end(i, j, tok, b)
                full_pe[:] = [[tok], Q.last["vector"]]

            def ada(i, j, b=7, buf=full[:, 0, :]):
                ada_copy(i, j, b, buf, ada_parts(i, j, b))
                put_off(1.3, lambda: ada_total(i, j, b, buf))

            gap = []

            def gap_parts(slots, bufs, *w):
                for a, b, buf in zip(slots, (6, 7), bufs):
                    gap.append((a, b, buf, ada_parts(*a, b), w))

            def gap_copies():
                for a, b, buf, tok, w in gap:
                    ada_copy(*a, b, buf, tok, w)
                    put_off(1.6, lambda: None)
                    put_off(1.6, lambda: None)
                    put_off(1.6, lambda a=a, buf=buf: ada_total(*a, 7, buf))
                gap[:] = []

            ada_s, full_pe, full_act = {}, [[]], []

            def warm():
                act(lambda e: e.activation(st[:, 258:259], sum4[:, 0:1], ACT.Sqrt), t_s4)

            def rstd(dst, ss, n, *w, weight=1.0):
                c = ss.shape[-1]
                v, r, a = st[:, 128:128 + c], st[:, 160:160 + c], st[:, 192:192 + c]
                q = 1.0 / (weight * weight)
                tv = dve(lambda e: e.tensor_scalar(v, ss, q / n, q * EPS, ALU.mult, ALU.add), w)
                ts = act(lambda e: e.activation(r, v, ACT.Sqrt), tv)
                dve(lambda e: e.reciprocal(r, r), ts)
                dve(lambda e: e.scalar_tensor_tensor(a, r, -0.5, r, ALU.mult, ALU.mult))
                dve(lambda e: e.tensor_tensor(a, a, v, ALU.mult))
                return dve(lambda e: e.scalar_tensor_tensor(dst, a, 1.5, r, ALU.add, ALU.mult))

            def row_squares(dst, src, *w, o=None):
                if o is None:
                    o = full[:, :, :].rearrange("p a b -> p (a b)")
                full_act[:] = [act(lambda e: e.activation(o, src, ACT.Square, accum_out=dst), w, full_pe)]
                return full_act[0]

            RB = [4, 5, 6, 7]

            def to_T(src, K, dst_h, dst_l, scale=None, bias=None, func=None, keep=None, waits=(), wdst=(), bk=(4, 5, 6, 7), diag=None):
                toks = []
                held = []

                def low(L, fl, H, th, nk):
                    tl = dve(lambda e: e.tensor_tensor(L, fl, H.bitcast(F32), ALU.subtract), th)
                    toks.extend([[th, tl]] * nk)
                    full_pe[:] = full_pe[:1] + [tl]

                for k0 in range(0, K, 2):
                    b = bk[(k0 // 2) % 4]
                    nk = min(2, K - k0)
                    for k in range(nk):
                        for t in range(T):
                            o = PB[b][:, k * S + t * P:k * S + (t + 1) * P]
                            if diag is None:
                                tp = pe(lambda e: e.transpose(o, src(t, k0 + k), ident[:, :]), waits, free[b], t_id)
                            else:
                                tp = pe(lambda e: e.matmul(o, src(t, k0 + k), diag(t), start=True, stop=True),
                                        waits, free[b])
                    ps = PB[b][:, 0:nk * S].rearrange("p (k n) -> p k n", n=S)
                    H, L = (dst_h[:, k0:k0 + nk, :], dst_l[:, k0:k0 + nk, :]) if dst_h is not None else (None, None)
                    fl = full[:, (k0 // 2) % 2, 0:nk * S].rearrange("p (k n) -> p k n", n=S)
                    if scale is None:
                        th = act(lambda e: e.activation(H, ps, ACT.Copy), tp, wdst)
                        tl = dve(lambda e: e.tensor_tensor(L, ps, H.bitcast(F32), ALU.subtract), th)
                        fr = [th, tl]
                    elif func is None:
                        if keep is not None:
                            fl = keep[:, k0:k0 + nk, :]
                        for k in range(nk):
                            sc_, bi_ = scale(k0 + k), (bias(k0 + k) if bias is not None else 0.0)
                            tf = dve(lambda e: e.tensor_scalar(fl[:, k, :], ps[:, k, :], sc_, bi_, ALU.mult, ALU.add),
                                     tp, wdst, full_pe)
                        fr = [tf]
                        if H is None:
                            toks += [[tf]] * nk
                            free[b] = fr
                            continue
                        free[b] = fr
                        th = act(lambda e: e.activation(H, fl, ACT.Copy), tf)
                        full_act[:] = [th]
                        if held:
                            low(*held.pop())
                        held.append((L, fl, H, th, nk))
                        ahead(upos[0] - 4 + k0 // 2)
                        if k0 + 2 >= K:
                            low(*held.pop())
                        continue
                    else:
                        for k in range(nk):
                            sc_, bi_ = scale(k0 + k), bias(k0 + k)
                            tf = act(lambda e: e.activation(fl[:, k, :], ps[:, k, :], func, bias=bi_, scale=sc_),
                                     tp, wdst)
                        th = act(lambda e: e.activation(H, fl, ACT.Copy))
                        tl = dve(lambda e: e.tensor_tensor(L, fl, H.bitcast(F32), ALU.subtract), th)
                        fr = [tf]
                    toks += [[th, tl]] * nk
                    free[b] = fr
                return toks


            def prenorm(waits=(), src=None, dst=None, gain=None, tg=(), sq=None):
                src = x if src is None else src
                dst = xn if dst is None else dst
                for t in range(T):
                    ta = row_squares(st[:, 4 + t:5 + t], src[:, t, :], waits[t:t + 1] if len(waits) == T else waits,
                                     o=sq)
                rstd(st[:, 6:8], st[:, 4:6], D, ta)
                for t in range(T):
                    if gain is not None:
                        tk = dve(lambda e: e.scalar_tensor_tensor(dst[:, t, :], src[:, t, :], st[:, 6 + t:7 + t], gain,
                                                                  ALU.mult, ALU.mult), last_pe_xn, tg)
                    else:
                        tk = dve(lambda e: e.tensor_scalar(dst[:, t, :], src[:, t, :], st[:, 6 + t:7 + t], None,
                                                           ALU.mult), last_pe_xn)
                return tk

            last_pe_xn = []

            dgx = [xn[:, 0, t * P:(t + 1) * P] for t in range(T)]

            def diag_rstd(waits, sq=None):
                for t in range(T):
                    ta = row_squares(st[:, 4 + t:5 + t], x[:, t, :], waits[t:t + 1] if len(waits) == T else waits, o=sq)
                rstd(st[:, 6:8], st[:, 4:6], D, ta)
                for t in range(T):
                    tk = dve(lambda e: e.tensor_scalar(dgx[t], ident[:, :], st[:, 6 + t:7 + t], None, ALU.mult),
                             last_pe_xn, t_id)
                return tk

            def rows_x(t, k):
                return x[:, t, k * P:(k + 1) * P]

            def rows_xn(t, k):
                return xn[:, t, k * P:(k + 1) * P]

            def pre(s, keep=None, split=True, xn_tok=None, bk=(4, 5, 6, 7)):
                wd = [Q.last["tensor"]]
                flush()
                tk = diag_rstd(x_tok) if xn_tok is None else xn_tok
                gap_copies()
                toks = to_T(rows_x, KD, hh if split else None, hl, scale=lambda k: ab[:, s, 0, k:k + 1],
                            bias=lambda k: ab[:, s, 1, k:k + 1],
                            keep=keep, waits=[tk], wdst=wd + ab_tok[s], bk=bk,
                            diag=lambda t: dgx[t])
                last_pe_xn[:] = [Q.last["tensor"]]
                return toks

            def post(s, src, weight, waits, psum=True):
                while len(g_done.get(s, [])) < 2:
                    later.pop(0)[1]()
                warm()
                g = G[s % 3]
                if psum:
                    t0 = row_squares(st[:, 4:5], src(0), waits)
                    d1 = dve(lambda e: e.tensor_tensor(xn[:, 1, :], src(1), g, ALU.mult), waits, g_done[s], last_pe_xn)
                    t1 = row_squares(st[:, 5:6], src(1), d1)
                    dve(lambda e: e.tensor_tensor(xn[:, 0, :], src(0), g, ALU.mult), t0)
                else:
                    for t in range(T):
                        t1 = row_squares(st[:, 4 + t:5 + t], src(t), waits[t])
                        dve(lambda e: e.tensor_tensor(xn[:, t, :], src(t), g, ALU.mult), t1, g_done[s])
                rstd(st[:, 6:8], st[:, 4:6], D, t1, weight=weight)
                x_tok[:] = [dve(lambda e: e.scalar_tensor_tensor(
                    x[:, t, :], xn[:, t, :], st[:, 6 + t:7 + t], x[:, t, :], ALU.mult, ALU.add)) for t in range(T)]
                if psum:
                    for t in range(T):
                        for b in YB[t]:
                            free[b] = [x_tok[0]]
                if s + 3 < 6:
                    load_G(s + 3, x_tok)

            def ypsum2(t):
                return PS[:, 2 * t:2 * t + 2, :].rearrange("p a b -> p (a b)")

            def ypsum(t, h):
                return PB[YB[t][h]][:, :]

            lh = lambda k, t: hh[:, k, t * P:(t + 1) * P]
            ll = lambda k, t: hl[:, k, t * P:(t + 1) * P]

            ff = {"n": 0, "ug": [[], []], "gt": [[], []], "sg": []}

            def ffn_like(nb, kin, kout, toks, between, combine=None):
                def spread(b):
                    i = b % 2
                    for f in range(2):
                        for t in range(T):
                            tp = pe(lambda e, f=f, t=t: e.transpose(
                                PB[6][:, f * S + t * P:f * S + (t + 1) * P], ug[i][:, t, f * P:(f + 1) * P], ident[:, :]),
                                ff["ug"][i], free[6])
                    th = act(lambda e: e.activation(gT_h[i][:, :, :], PB[6][:, :].rearrange("p (a b) -> p a b", b=S),
                                                    ACT.Copy), tp, ff["gt"][i])
                    tl = dve(lambda e: e.tensor_tensor(
                        gT_l[i][:, :, :], PB[6][:, :].rearrange("p (a b) -> p a b", b=S),
                        gT_h[i][:, :, :].bitcast(F32), ALU.subtract), th)
                    free[6] = [th, tl]
                    ff["ugfree"][i] = [tp]
                    ff["gtt"][i] = [th, tl]

                ff["ugfree"] = [[], []]
                ff["gtt"] = [[], []]

                def outp(b):
                    i = b % 2
                    tok = linear(kout(b), 2, lambda k, t: gT_h[i][:, k, t * P:(t + 1) * P],
                                 lambda k, t: gT_l[i][:, k, t * P:(t + 1) * P], ff["gtt"][i], YB,
                                 first=(b == 0), last=(b == nb - 1))
                    ff["gt"][i] = [tok]
                    return tok

                for b in range(nb):
                    i = b % 2
                    tok = linear(kin(b), KD, lh, ll, toks, [[AB[0]], [AB[1]]], mid=(lambda b=b: spread(b - 1)) if b else None)
                    for t in range(T):
                        ta = act(lambda e, t=t: e.activation(sg[:, t, :], PB[AB[t]][:, 0:256], ACT.Silu), tok, ff["sg"])
                        if combine is None:
                            td = dve(lambda e, t=t: e.tensor_tensor(ug[i][:, t, :], sg[:, t, :], PB[AB[t]][:, 256:512],
                                                                   ALU.mult), ta, ff["ugfree"][i])
                        else:
                            td = dve(lambda e, t=t: e.scalar_tensor_tensor(
                                ug[i][:, t, :], sg[:, t, :], comb[:, t, b:b + 1], PB[AB[t]][:, 256:512],
                                ALU.mult, ALU.mult), ta, ff["ugfree"][i], combine)
                        free[AB[t]] = [ta, td]
                    ff["sg"] = [td]
                    ff["ug"][i] = [td]
                    if b:
                        outp(b - 1)
                    between(b)
                spread(nb - 1)
                return outp(nb - 1)

            x_tok = list(t_x)
            tk0 = diag_rstd(x_tok, sq=AR[:, XN_END + 2 * D:XN_END + 3 * D])
            bufs = [full[:, 0, :]] + [v[:, :, :].rearrange("p a b -> p (a b)") for v in (ug[0], ug[1], sg)]
            for n_, a in enumerate(ada_order[:4]):
                ada(*a, b=n_, buf=bufs[n_])
            flush()
            ahead(2 - NUNIT)
            load_G(2, t_ng, small_columns())

            spare = [AR[:, XN_END + n_ * 512:XN_END + n_ * 512 + 512] for n_ in range(2)]

            def ffn(i, s, xn_tok=None, then=None):
                sl = i * 3 + 2 * s
                toks = pre(sl, xn_tok=xn_tok)

                def between(b):
                    for a in ADA_AT.get((i, s, b), []):
                        ada(*a)
                    if then is not None and b == 5:
                        mem_norm()
                tok = ffn_like(NFF, lambda b: ("fi", i, s, b), lambda b: ("fo", i, s, b), toks, between)
                flush()
                if then is not None:
                    then()
                elif (i, s) in ada_gap:
                    gap_parts(ada_gap[i, s], spare)
                post(sl, ypsum2, 0.5, [tok])

            at[0] = XN_END
            hp = arena(KD, 272)
            sA, sB = arena(2, 272), arena(2, 272)
            zT = arena(KD, S)
            rc = arena(4, S)
            pbb = arena(D)
            psb = arena(D)
            yp = xn
            t_rc = load(rc, I["rc_c"].rearrange("g n -> (g n)").unsqueeze(0).to_broadcast([P, 4 * S])
                        .rearrange("p (g n) -> p g n", n=S))
            t_pb = load(pbb[0:1, :], I["pool_b"].rearrange("a g n -> a (g n)"))
            t_ps = load(psb, I["pool_scale"].to_broadcast([P, D]))
            dve(lambda e: e.memset(hp[:, :, 0:8], 0.0))
            dve(lambda e: e.memset(hp[:, :, 264:272], 0.0))
            mrow = zT.rearrange("p (a b) c -> p a (b c)", a=T)
            t_mem = load(mrow, I["mem_2"][0].rearrange("(t p) n -> p t n", p=P))
            mem_tok = []

            def mem_norm():
                o = hp[:, 0:4, 8:264]
                for t in range(T):
                    put_off(0.5, lambda t=t: row_squares(st[:, 8 + t:9 + t], mrow[:, t, :], t_mem, o=o))
                put_off(1.0, lambda: rstd(st[:, 10:12], st[:, 8:10], D, Q.last["scalar"]))
                for t in range(T):
                    put_off(0.7, lambda t=t: mem_tok.append(dve(lambda e: e.tensor_scalar(
                        mrow[:, t, :], mrow[:, t, :], st[:, 10 + t:11 + t], None, ALU.mult))))

            def mem_T():
                mtoks[:] = to_T(lambda t, k: mrow[:, t, k * P:(k + 1) * P], KD, hh, hl,
                                scale=lambda k: col("g_mem_2", k), waits=mem_tok, wdst=[Q.last["tensor"]])

            mtoks = []
            ffn(0, 0, tk0, then=mem_T)

            KM, VM = kvm[:, 0, :, :], kvm[:, 1, :, :]
            ptok = diag_rstd(x_tok)
            tok = linear(("kv",), KD, lh, ll, mtoks, [[4], [5]])
            for t in range(T):
                tk = act(lambda e: e.activation(KM[:, t, :], PB[4 + t], ACT.Copy), tok)
                free[4 + t] = [tk]
            tok2 = linear(("kv",), KD, lh, ll, mtoks, [[6], [7]])
            pre(1, keep=hp[:, :, 8:264], split=False, xn_tok=ptok, bk=(0, 1, 2, 3))
            for t in range(T):
                tk = act(lambda e: e.activation(VM[:, t, :], PB[6 + t], ACT.Copy), tok2)
                free[6 + t] = [tk]
            mtr = [Q.last["tensor"]]
            bufs = [v[:, :, :].rearrange("p a b -> p (a b)") for v in (ug[0], ug[1], sg)]
            for n_, a in enumerate(ada_pool):
                ada(*a, b=(4, 5, 7)[n_], buf=bufs[n_])
            m, w, dt = take_raw(("pw",))
            for g in range(4):
                src = hp[:, 2 * g:2 * g + 2, :]
                n = 272
                for i in range(g + 1):
                    sh = 1 << i
                    n -= sh
                    dst = (sA, sB)[i % 2]
                    dve(lambda e: e.tensor_tensor(dst[:, :, 0:n], src[:, :, 0:n], src[:, :, sh:sh + n], ALU.add))
                    src = dst
                o = 8 - (1 << g)
                z = zT[:, 2 * g:2 * g + 2, :]
                dve(lambda e: e.tensor_tensor(z, src[:, :, o:o + S], rc[:, g:g + 1, :].to_broadcast([P, 2, S]),
                                              ALU.mult), t_rc, mtr)
                zt = dve(lambda e: e.tensor_tensor(z, z, hp[:, 2 * g:2 * g + 2, 8:264], ALU.subtract))
                if g == 2:
                    flush()
                for t in range(T):
                    b, c0 = YB[t][g // 2], (g % 2) * 256
                    pe(lambda e: e.matmul(PB[b][:, c0:c0 + 256], sum4[0:1, :], pbb[0:1, g * 256:g * 256 + 256],
                                          start=True, stop=False), t_s4, t_pb, free[b])
                    for k in range(2):
                        tp = pe(lambda e: e.matmul(PB[b][:, c0:c0 + 256], zT[:, 2 * g + k, t * P:(t + 1) * P],
                                                   w[:, 2 * g + k, :], start=False, stop=(k == 1)), zt, dt)
            give_raw(m, tp)
            gap_parts(ada_gap[0, 0], spare, Q.last["vector"])
            ptk = []
            for t in range(T):
                for h in range(2):
                    b = YB[t][h]
                    o = yp[:, t, h * 512:(h + 1) * 512]
                    tk = dve(lambda e: e.tensor_tensor(o, PB[b], psb[:, h * 512:(h + 1) * 512], ALU.mult), tp, t_ps)
                    free[b] = [tk]
                ptk.append(tk)
            post(1, lambda t: yp[:, t, :], 1.0, ptk, psum=False)

            ffn(0, 1)
            ffn(1, 0)

            def rope(v, n_t, nh, half, cos, sin, tmp, *w, dve=dve):
                x1, x2 = v[:, :, 0:half], v[:, :, half:2 * half]
                c = cos.unsqueeze(1).to_broadcast([P, nh, half])
                s = sin.unsqueeze(1).to_broadcast([P, nh, half])
                a, b = tmp[0], tmp[1]
                a = a[:, 0:nh * half].rearrange("p (h d) -> p h d", d=half)
                b = b[:, 0:nh * half].rearrange("p (h d) -> p h d", d=half)
                dve(lambda e: e.tensor_tensor(a, x2, s, ALU.mult), w)
                dve(lambda e: e.tensor_tensor(b, x1, s, ALU.mult))
                dve(lambda e: e.tensor_tensor(x1, x1, c, ALU.mult))
                dve(lambda e: e.tensor_tensor(x1, x1, a, ALU.subtract))
                dve(lambda e: e.tensor_tensor(x2, x2, c, ALU.mult))
                return dve(lambda e: e.tensor_tensor(x2, x2, b, ALU.add))

            def attention(nh, hd, vd, qrow, krow, kshare, vrow, orow, scale, tq, bufs, mask=None, extra=None):
                qk, pr, pT, sm, mx = bufs
                fq, fp, fpt = [[], []], [[], []], [[], []]
                ex, pt = {}, {}
                sums = st[:, 64:64 + 2 * nh]
                result = []

                cp = {}

                def zero(h):
                    i = h % 2
                    for t in range(T):
                        pe(lambda e, t=t: e.transpose(PB[6][0:hd, t * P:(t + 1) * P], qrow(h, t), ident[:, :]),
                           tq, free[6])
                    for t in range(T):
                        tp = pe(lambda e, t=t: e.transpose(PB[6][0:hd, S + t * P:S + (t + 1) * P], krow(h // kshare, t),
                                                           ident[:, :]))
                    tc = act(lambda e: e.activation(qk[i][0:hd, :], PB[6][0:hd, :], ACT.Copy), tp, fq[i])
                    free[6] = [tc]
                    cp[h] = tc

                def one(h):
                    i = h % 2
                    b = AB[i]
                    tc = cp[h]
                    for t in range(T):
                        ts = pe(lambda e, t=t: e.matmul(PB[b][:, t * S:(t + 1) * S], qk[i][0:hd, t * P:(t + 1) * P],
                                                        qk[i][0:hd, S:2 * S], start=True, stop=True), tc, free[b])
                    fq[i] = [ts]
                    if mask is not None:
                        sv = sm[i].rearrange("p (t n) -> p t n", n=S)
                        tm = dve(lambda e: e.tensor_tensor(sv, PB[b][:, :].rearrange("p (t n) -> p t n", n=S), mask,
                                                           ALU.add), ts)
                        free[b] = [tm]
                    else:
                        sv = PB[b][:, :].rearrange("p (t n) -> p t n", n=S)
                    m2 = mx[:, 2 * i:2 * i + 2]
                    dve(lambda e: e.tensor_reduce(m2, sv, AX_X, ALU.max), ts)
                    tm = dve(lambda e: e.tensor_scalar(m2, m2, -scale, None, ALU.mult))
                    for t in range(T):
                        te = act(lambda e, t=t: e.activation(pr[i][:, t * S:(t + 1) * S], sv[:, t, :], ACT.Exp,
                                                             bias=m2[:, t:t + 1], scale=scale,
                                                             accum_out=sums[:, 2 * h + t:2 * h + t + 1]), tm, fp[i])
                    if mask is None:
                        free[b] = [te]
                    ex[h] = te

                def two(h):
                    i = h % 2
                    for c in range(2):
                        for t in range(T):
                            tp = pe(lambda e, c=c, t=t: e.transpose(
                                PB[7][:, c * S + t * P:c * S + (t + 1) * P], pr[i][:, t * S + c * P:t * S + (c + 1) * P],
                                ident[:, :]), ex[h], free[7])
                    fp[i] = [tp]
                    tc = act(lambda e: e.activation(pT[i], PB[7][:, :], ACT.Copy), tp, fpt[i])
                    free[7] = [tc]
                    pt[h] = tc

                tlast = [None]

                def three(h):
                    i = h % 2
                    for t in range(T):
                        b = YB[t][h * vd // 512]
                        c0 = h * vd % 512
                        for c in range(2):
                            tlast[0] = pe(lambda e, c=c, t=t, b=b, c0=c0: e.matmul(
                                PB[b][:, c0:c0 + vd], pT[i][:, c * S + t * P:c * S + (t + 1) * P],
                                vrow(c, h // kshare), start=(c == 0), stop=(c == 1)), pt[h], free[b])
                    fpt[i] = [tlast[0]]

                def at_step(h):
                    if extra is not None:
                        extra()
                    if h < nh:
                        zero(h)
                    if 1 <= h <= nh:
                        one(h - 1)
                    if 2 <= h <= nh + 1:
                        two(h - 2)
                    if h >= 3:
                        three(h - 3)

                def finish():
                    rs = st[:, 224:224 + 2 * nh]
                    dve(lambda e: e.reciprocal(rs, sums), ex[nh - 1])
                    rv = rs.rearrange("p (h t) -> p h t", t=2)
                    for t in range(T):
                        for hb in range((nh * vd + 511) // 512):
                            n0 = 512 // vd
                            b = YB[t][hb]
                            tk = dve(lambda e: e.tensor_tensor(
                                orow(t)[:, hb * n0:(hb + 1) * n0, :], PB[b].rearrange("p (h d) -> p h d", d=vd),
                                rv[:, hb * n0:(hb + 1) * n0, t:t + 1].to_broadcast([P, n0, vd]), ALU.mult), tlast[0])
                            free[b] = [tk]
                    result.append(tk)

                for h in range(nh + 3):
                    put_off(2.2 if mask is not None else 1.6, lambda h=h: at_step(h))
                put_off(1.2, finish)
                return result

            at[0] = XN_END
            xf = xn.rearrange("p a b -> p (a b)")
            lat = xf[:, 0:832].rearrange("p (a b) -> p a b", b=416)
            qr = arena(T, 1536)
            kr = arena(T, 1536)
            vr = arena(T, 1024)
            cqT = xf[:, 1024:1536].rearrange("p (a b) -> p a b", b=S)
            ckT = xf[:, 1536:1792]
            ropeC = arena(2, T, 16)
            flat2 = lambda a: a.rearrange("p a b -> p (a b)")
            qk = [flat2(ug[0][:, :, :]), flat2(ug[1][:, :, :])]
            pr = [flat2(sg[:, :, :]), arena(512)]
            pT = [G[0][:, 0:512], G[0][:, 512:1024]]
            orow_a = xn
            tmpA = [qk[0], pr[0]]
            t_rp = load(ropeC, I["rope16_c"].rearrange("p (a t d) -> p a t d", a=2, t=2), x_tok)
            toks = pre(4)
            tok = linear(("mi",), KD, lh, ll, toks, [[AB[0]], [AB[1]]])
            bufA = full[:, 0, :]
            bufB = arena(512)
            tpA = ada_parts(*ada_mla[0], 1)
            for t in range(T):
                td = dve(lambda e, t=t: e.tensor_copy(lat[:, t, :], PB[AB[t]][:, 0:416]), tok)
                free[AB[t]] = [td]
                for c, (a, n) in enumerate(((0, 256), (256, 128))):
                    ts = act(lambda e, t=t, c=c, a=a, n=n: e.activation(
                        full[:, 1, 0:n], lat[:, t, a:a + n], ACT.Square,
                        accum_out=st[:, 10 + 2 * c + t:11 + 2 * c + t]), td)
            rstd(st[:, 16:18], st[:, 10:12], 256, ts)
            rstd(st[:, 18:20], st[:, 12:14], 128)
            ada_copy(*ada_mla[0], 1, bufA, tpA)
            for t in range(T):
                dve(lambda e, t=t: e.tensor_scalar(lat[:, t, 0:256], lat[:, t, 0:256], st[:, 16 + t:17 + t], None, ALU.mult))
                td = dve(lambda e, t=t: e.tensor_scalar(lat[:, t, 256:384], lat[:, t, 256:384], st[:, 18 + t:19 + t], None,
                                                        ALU.mult))
            for k in range(3):
                b = 6 if k < 2 else 7
                for t in range(T):
                    tp = pe(lambda e, k=k, t=t, b=b: e.transpose(
                        PB[b][:, (k % 2) * S + t * P:(k % 2) * S + (t + 1) * P], lat[:, t, k * P:(k + 1) * P],
                        ident[:, :]), td, free[b])
                dst = cqT[:, k, :] if k < 2 else ckT
                g = col("mla_q_norm", k) if k < 2 else col("mla_kv_norm", 0)
                tc = dve(lambda e, dst=dst, g=g, b=b, k=k: e.tensor_scalar(dst, PB[b][:, (k % 2) * S:(k % 2) * S + S], g,
                                                                          None, ALU.mult), tp)
                free[b] = [tc]
            krv = kr.rearrange("p t (h d) -> p t h d", d=96)
            qrv = qr.rearrange("p t (h d) -> p t h d", d=96)
            for nm, tgt in (("mla_w_uk", 0), ("mla_w_uv", 1)):
                m, w, dt = take_raw((nm,))
                for t in range(T):
                    for c in range(2):
                        b = YB[t][c]
                        tp = pe(lambda e: e.matmul(
                            PB[b][:, :], ckT[:, t * P:(t + 1) * P], w[:, 0, c * 512:(c + 1) * 512],
                            start=True, stop=True), dt, tc, free[b])
                        if tgt == 0:
                            tk = act(lambda e: e.activation(
                                krv[:, t, 8 * c:8 * c + 8, 0:64], PB[b][:, :].rearrange("p (h d) -> p h d", d=64),
                                ACT.Copy), tp)
                        else:
                            tk = act(lambda e: e.activation(vr[:, t, c * 512:(c + 1) * 512], PB[b][:, :],
                                                            ACT.Copy), tp)
                        free[b] = [tk]
                give_raw(m, tp)
            for t in range(T):
                rope(lat[:, t, 384:416].rearrange("p (h d) -> p h d", h=1), T, 1, 16, ropeC[:, 0, t, :], ropeC[:, 1, t, :],
                     tmpA, t_rp)
                tk = dve(lambda e: e.tensor_copy(krv[:, t, :, 64:96],
                                                 lat[:, t, 384:416].unsqueeze(1).to_broadcast([P, 16, 32])))
            flush()
            QB = [[4, 5, 7], [0, 1, 2]]
            wq = [take_raw(("uq",)) for k in range(2)]
            for t in range(T):
                for c in range(3):
                    b = QB[t][c]
                    for k in range(2):
                        tp = pe(lambda e: e.matmul(
                            PB[b][:, :], cqT[:, k, t * P:(t + 1) * P], wq[k][1][:, 0, c * 512:(c + 1) * 512],
                            start=(k == 0), stop=(k == 1)), wq[k][2], tc, free[b])
                    if c == 1:
                        ta = dve(lambda e: e.tensor_copy(qr[:, t, c * 512:(c + 1) * 512], PB[b][:, :]), tp)
                    else:
                        ta = act(lambda e: e.activation(qr[:, t, c * 512:(c + 1) * 512], PB[b][:, :], ACT.Copy), tp)
                    free[b] = [ta]
                tk2 = rope(qrv[:, t, :, 64:96], T, 16, 16, ropeC[:, 0, t, :], ropeC[:, 1, t, :], tmpA, ta)
            for m, w, dt in wq:
                give_raw(m, tp)
            ada_copy(*ada_mla[1], 3, bufB, ada_parts(*ada_mla[1], 3))
            att = attention(16, 96, 64, lambda h, t: qrv[:, t, h, :], lambda h, t: krv[:, t, h, :], 1,
                           lambda c, h: vr[:, c, h * 64:(h + 1) * 64],
                           lambda t: orow_a[:, t, :].rearrange("p (h d) -> p h d", d=64),
                           96 ** -0.5, [tk, tk2], (qk, pr, pT, None, st[:, 96:100]))
            flush()
            wd = [Q.last["tensor"]]
            toks = to_T(lambda t, k: orow_a[:, t, k * P:(k + 1) * P], KD, hh, hl,
                        waits=att, wdst=wd)
            put_off(1.3, lambda: ada_total(*ada_mla[0], 7, bufA))
            put_off(1.3, lambda: ada_total(*ada_mla[1], 7, bufB))
            tok = linear(("mo",), KD, lh, ll, toks, YB)
            gap_parts(ada_mla[2:], spare, Q.last["tensor"])
            post(4, ypsum2, 1.0, [tok])

            ffn(1, 1)

            at[0] = XN_END
            QK = arena(T, 19, 64)
            V = arena(T, 128)
            QM = arena(T, 4, 128)
            wi = arena(T, 8)
            gqk = arena(3, 64)
            gqm = arena(2, 128)
            rp32 = arena(2, T, 32)
            cw = arena(4, CONVW)
            uT = arena(4, 286)
            mask = arena(T, S)
            score = arena(T, S)
            pr = [flat2(sg[:, :, :]), arena(512)]
            ga = arena(2, T, 512)
            om = xf[:, 0:1024].rearrange("p (t n) -> p t n", t=T)
            ca = xf[:, 1024:2048].rearrange("p (t n) -> p t n", t=T)
            gm = [G[1].rearrange("p (t n) -> p t n", t=T), ca]
            yc = G[0].rearrange("p (k n) -> p k n", n=S)
            ht = G[2]
            qk = [flat2(ug[0][:, :, :]), flat2(ug[1][:, :, :])]
            pT = [ht[:, 0:512], ht[:, 512:1024]]
            KMv = KM.rearrange("p t (h d) -> p t h d", d=P)
            base = list(x_tok)
            tgn = [load(gqk[:, i:i + 1, :], I[nm].unsqueeze(0).to_broadcast([P, 1, 64]), base)
                   for i, nm in enumerate(("g_qa_2", "g_ka_2", "g_idx_k_2"))]
            tgn += [load(gqm[:, i, :], I[nm].to_broadcast([P, 128]), base) for i, nm in enumerate(("g_qm_2", "g_km_2"))]
            t_rp = load(rp32, I["rope32_c"].rearrange("p (a t d) -> p a t d", a=2, t=2), base)
            t_cm = load(mask, I["cap_c"].rearrange("p (t n) -> p t n", n=S), base)
            cwr = om[0:CONVW, 0, :]
            t_bg = load(adab[0:6, :], I["b_gate_2"].rearrange("a (j n) -> (a j) n", n=512), base)

            tk = diag_rstd(x_tok)
            toks = to_T(rows_x, KD, hh, hl, scale=lambda k: col("g_mix_2", k), waits=[tk], wdst=[Q.last["tensor"]],
                        diag=lambda t: dgx[t])
            t_cw = load(cwr, I["conv_w_2"][0].rearrange("j a n -> j (a n)"), Q.last["tensor"])
            tz = dve(lambda e: e.memset(uT[:, :, 0:30], 0.0), base)

            def norm_steps(v, nh, hd, gains, waits):
                ss, rr = st[:, 20:20 + 2 * nh], st[:, 42:42 + 2 * nh]

                def squares(t):
                    tmp = ht[:, 0:nh * hd].rearrange("p (h d) -> p h d", d=hd)
                    dve(lambda e: e.tensor_tensor(tmp, v(t), v(t), ALU.mult), waits)
                    dve(lambda e: e.tensor_reduce(ss[:, t * nh:(t + 1) * nh], tmp, AX_X, ALU.add))

                def scaled(t):
                    dve(lambda e: e.tensor_tensor(v(t), v(t), rr[:, t * nh:(t + 1) * nh].unsqueeze(2)
                                                  .to_broadcast([P, nh, hd]), ALU.mult))

                def gained(t, a, n, g):
                    dve(lambda e: e.tensor_tensor(v(t)[:, a:a + n, :], v(t)[:, a:a + n, :],
                                                  g.to_broadcast([P, n, hd]), ALU.mult), tgn)

                for t in range(T):
                    put_off(nh * hd * 2.1e-3, lambda t=t: squares(t))
                put_off(1.5, lambda: rstd(rr, ss, hd))
                for t in range(T):
                    put_off(nh * hd * 1.1e-3, lambda t=t: scaled(t))
                    for a, n, g in gains:
                        put_off(n * hd * 1.1e-3, lambda t=t, a=a, n=n, g=g: gained(t, a, n, g))

            rope_tok = {}

            def rope_steps(key, a, n, waits):
                for t in range(T):
                    def go(t=t):
                        rope_tok[key, t] = rope(QK[:, t, a:a + n, :], T, n, 32, rp32[:, 0, t, :], rp32[:, 1, t, :],
                                                [ht[:, 0:512], ht[:, 512:1024]], t_rp, waits)
                    put_off(n * 0.22, go)

            fqk = [[], []]
            ix = {}

            def ix_copy(h):
                i = h % 2
                src = (lambda t: QK[:, t, 10, :]) if h < 0 else (lambda t: QK[:, t, 11 + h, :])
                dst = pr[0][0:64, 0:S] if h < 0 else qk[i][0:64, 0:S]
                for t in range(T):
                    tp = pe(lambda e: e.transpose(PB[6][0:64, t * P:(t + 1) * P], src(t), ident[:, :]),
                            free[6], [rope_tok[k] for k in rope_tok])
                ix[h] = act(lambda e: e.activation(dst, PB[6][0:64, 0:S], ACT.Copy), tp, fqk[i] if h >= 0 else [])
                free[6] = [ix[h]]

            def ix_score(h):
                i, b = h % 2, AB[h % 2]
                for t in range(T):
                    ts = pe(lambda e: e.matmul(PB[b][:, t * S:(t + 1) * S], qk[i][0:64, t * P:(t + 1) * P],
                                               pr[0][0:64, 0:S], start=True, stop=True), ix[h], ix[-1], free[b])
                fqk[i] = [ts]
                rl = pT[h % 2].rearrange("p (t n) -> p t n", n=S)
                ta = act(lambda e: e.activation(pT[h % 2], PB[b], ACT.Relu, scale=0.125), ts, ix.get(("d", h - 2)),
                         Q.last["vector"] if h < 2 else [])
                free[b] = [ta]
                for t in range(T):
                    if h == 0:
                        td = dve(lambda e: e.tensor_scalar(score[:, t, :], rl[:, t, :], wi[:, t, 0:1], None,
                                                           ALU.mult), ta)
                    else:
                        td = dve(lambda e: e.scalar_tensor_tensor(
                            score[:, t, :], rl[:, t, :], wi[:, t, h:h + 1], score[:, t, :], ALU.mult, ALU.add), ta)
                ix["d", h] = td

            def index_steps():
                put_off(0.0, lambda: ix_copy(-1))
                for h in range(9):
                    def go(h=h):
                        if h < 8:
                            ix_copy(h)
                        if h >= 1:
                            ix_score(h - 1)
                    put_off(0.8, go)
                put_off(0.6, lambda: dve(lambda e: e.tensor_tensor(score, score, mask, ALU.min), t_cm))
                for r in range(8):
                    for t in range(T):
                        def mark(t=t):
                            m8 = st[:, 260 + 8 * t:268 + 8 * t]
                            dve(lambda e: e.max(m8, score[:, t, :]))
                            dve(lambda e: e.match_replace(score[:, t, :], m8, score[:, t, :], MARK))
                        put_off(0.8, mark)

                def to_mask():
                    dve(lambda e: e.tensor_scalar(score, score, MARK, None, ALU.is_equal))
                    dve(lambda e: e.scalar_tensor_tensor(mask, mask, 0.0, score, ALU.is_gt, ALU.mult))
                    ix["mask"] = dve(lambda e: e.tensor_scalar(mask, mask, -1.0, -NEG, ALU.add, ALU.mult))
                put_off(1.4, to_mask)

            def conv_taps(k, j):
                y, u, w = yc[:, k, :], uT[:, k, j:j + S], cw[:, k, j:j + 1]
                if j == 0:
                    return dve(lambda e: e.tensor_scalar(y, u, w, col("conv_b_2", k), ALU.mult, ALU.add), t_uT)
                return dve(lambda e: e.scalar_tensor_tensor(y, u, w, y, ALU.mult, ALU.add))

            fill = []

            def filler(n):
                for _ in range(n):
                    if fill:
                        conv_done[0] = conv_taps(*fill.pop(0))

            conv_done = [None]

            pe_fill = [(k, j) for j in range(CONVW - PE_TAPS, CONVW) for k in range(4)]
            dg = [v[:, t, h * P:(h + 1) * P] for v in (mask, score) for t in range(T) for h in range(2)]
            dg_free = {}

            def pe_taps(n):
                for _ in range(n):
                    if pe_fill:
                        k, j = pe_fill.pop(0)
                        i = len(pe_fill) % 8
                        td = act(lambda e: e.activation(dg[i], ident[:, :], ACT.Copy, scale=cw[:, k, j:j + 1]),
                                 t_uT, dg_free.get(i), ix["att"])
                        for t in range(T):
                            dg_free[i] = pe(lambda e: e.matmul(
                                PB[6 + t][:, k * P:(k + 1) * P], uT[:, k, j + t * P:j + (t + 1) * P], dg[i],
                                start=(j == CONVW - PE_TAPS and k == 0), stop=False), td, free[6 + t])

            lbh = lambda k, t: bh[:, k, t * P:(t + 1) * P]
            lbl = lambda k, t: bl[:, k, t * P:(t + 1) * P]
            pairs = [(1, 3), (0, 2)]
            f64 = lambda a: a.rearrange("p (h d) -> p h d", d=64)

            def conv_transposes():
                for k in range(4):
                    tp = pe(lambda e: e.transpose(PB[7][:, k * 32:k * 32 + CONVW], cwr[:, k * P:(k + 1) * P],
                                                  ident[0:CONVW, 0:CONVW]), t_cw, free[7])
                tc = dve(lambda e: e.tensor_copy(cw, PB[7][:, 0:128].rearrange("p (k j) -> p k j", j=32)[:, :, 0:CONVW]),
                         tp)
                free[7] = [tc]
                tcw = tc
                for k0 in (0, 2):
                    b = 6 if k0 else 5
                    for k in range(2):
                        for t in range(T):
                            tp = pe(lambda e: e.transpose(
                                PB[b][:, k * S + t * P:k * S + (t + 1) * P], ca[:, t, (k0 + k) * P:(k0 + k + 1) * P],
                                ident[:, :]), t_u, free[b])
                    tc = act(lambda e: e.activation(
                        uT[:, k0:k0 + 2, 30:286], PB[b].rearrange("p (k n) -> p k n", n=S), ACT.Copy), tp, tz)
                    free[b] = [tc]
                return [tc, tcw]

            t_uT = []
            for n_, (c0, n) in enumerate(PROJ):
                b0, b1 = pairs[n_ % 2]
                def go_conv():
                    t_uT.append(conv_transposes())
                    fill[:] = [(k, j) for j in range(CONVW - PE_TAPS) for k in range(4)]
                mid = go_conv if n_ == 3 else None
                tok = linear(("pj",), KD, lh, ll, toks, [[b0], [b1]], mid=mid)
                for t, b in ((0, b0), (1, b1)):
                    src = PB[b]
                    if n_ == 0:
                        tk = act(lambda e: e.activation(ca[:, t, :], src, ACT.Copy), tok)
                    elif n_ == 1:
                        tk = act(lambda e: e.activation(full[:, t, :], src, ACT.Sigmoid), tok)
                        t_u = dve(lambda e: e.tensor_tensor(ca[:, t, :], ca[:, t, :], full[:, t, :], ALU.mult), tk)
                    elif n_ == 2:
                        act(lambda e: e.activation(QK[:, t, 10, :], src[:, 0:64], ACT.Copy), tok, base)
                        tk = act(lambda e: e.activation(wi[:, t, :], src[:, 64:72], ACT.Copy, scale=8 ** -0.5), tok)
                    elif n_ == 3:
                        tk = act(lambda e: e.activation(QK[:, t, 11:19, :], f64(src), ACT.Copy), tok)
                    elif n_ == 4:
                        tk = act(lambda e: e.activation(QK[:, t, 0:8, :], f64(src), ACT.Copy), tok)
                    elif n_ == 5:
                        act(lambda e: e.activation(QK[:, t, 8:10, :], f64(src[:, 0:128]), ACT.Copy), tok)
                        tk = act(lambda e: e.activation(V[:, t, :], src[:, 128:256], ACT.Copy), tok)
                    else:
                        tk = act(lambda e: e.activation(QM[:, t, :, :], src.rearrange("p (h d) -> p h d", d=128),
                                                        ACT.Copy), tok)
                    free[b] = [tk]
                if n_ == 2:
                    norm_steps(lambda t: QK[:, t, 10:11, :], 1, 64, [(0, 1, gqk[:, 2:3, :])], tk)
                    rope_steps("ki", 10, 1, [])
                elif n_ == 3:
                    rope_steps("qi", 11, 8, tk)
                    index_steps()
                elif n_ == 5:
                    norm_steps(lambda t: QK[:, t, 0:10, :], 10, 64, [(0, 8, gqk[:, 0:1, :]), (8, 2, gqk[:, 1:2, :])], tk)
                    rope_steps("qa", 0, 10, [])

                    def go():
                        ix["att"] = attention(
                            8, 64, 64, lambda h, t: QK[:, t, h, :], lambda h, t: QK[:, t, 8 + h, :], 4,
                            lambda c, h: V[:, c, h * 64:(h + 1) * 64],
                            lambda t: om[:, t, :].rearrange("p (h d) -> p h d", d=64),
                            0.125, [ix["mask"], rope_tok["qa", 1]],
                            (qk, pr, pT, [full[:, 0, :], full[:, 1, :]], st[:, 96:100]), mask=mask, extra=lambda: filler(2))
                        put_mark("att")
                    put_off(0.0, go)
            tqm = tk

            def gates(j, bank, dst, tb=None):
                for b in bank:
                    pe(lambda e: e.matmul(PB[b], ident[0:6, j:j + 1].to_broadcast([6, P]), adab[0:6, :],
                                          start=True, stop=False), free[b], t_bg)
                tok = linear(("gt",), KD, lh, ll, toks, [[b] for b in bank], first=False)
                tks = []
                for t, b in enumerate(bank):
                    ta = act(lambda e: e.activation(dst(t), PB[b], ACT.Sigmoid), tok)
                    free[b] = [ta]
                    tks.append(ta)
                return tks

            tg = {}
            for c in range(2):
                tg[0, c] = gates(c, (1, 3), lambda t: ga[:, c, t, :])
            for c in range(2):
                tg[2, c] = gates(4 + c, (1, 3), lambda t: gm[c][:, t, :])
            flush("att")
            btoks = to_T(lambda t, k: om[:, t, k * P:(k + 1) * P], 4, bh, bl, waits=ix["att"],
                         wdst=[Q.last["tensor"]])
            norm_steps(lambda t: QM[:, t, :, :], 4, 128, [(0, 4, gqm[:, 0:1, :])], tqm)
            norm_steps(lambda t: KMv[:, t, :, :], 4, 128, [(0, 4, gqm[:, 1:2, :])], base)

            def go_m():
                ix["mem"] = attention(
                    4, 128, 128, lambda h, t: QM[:, t, h, :], lambda h, t: KMv[:, t, h, :], 1,
                    lambda c, h: VM[:, c, h * 128:(h + 1) * 128],
                    lambda t: om[:, t, :].rearrange("p (h d) -> p h d", d=128),
                    128 ** -0.5, [Q.last["vector"]], (qk, pr, pT, None, st[:, 96:100]), extra=lambda: filler(3))
                put_mark("mem")
            put_off(0.0, go_m)
            gc = QK.rearrange("p t a b -> p (t a b)")[:, 0:2048].rearrange("p (c t n) -> p c t n", c=2, t=T)
            for c in range(2):
                tg[1, c] = gates(2 + c, (1, 3), lambda t: gc[:, c, t, :])
            flush("mem")
            grow = ht
            t_gr = load(grow, I["g_ffn_2"].to_broadcast([P, D]), Q.last["tensor"], Q.last["vector"], Q.last["scalar"])

            def branch(btoks, g, gt):
                tb = linear(("br",), 4, lbh, lbl, btoks, YB)
                tks = []
                for c in range(2):
                    for t in range(T):
                        b = YB[t][c]
                        o = gt(c, t)
                        tk = dve(lambda e: e.tensor_tensor(o, o, PB[b], ALU.mult), tg[g, c], tb)
                        free[b] = [tk]
                        if g != 0:
                            tk = dve(lambda e: e.tensor_tensor(ga[:, c, t, :], ga[:, c, t, :], o, ALU.add))
                        filler(1)
                return tk

            def taps():
                filler(2)
                pe_taps(3)
            after_unit[0] = taps
            branch(btoks, 0, lambda c, t: ga[:, c, t, :])
            btoks = to_T(lambda t, k: om[:, t, k * P:(k + 1) * P], 4, bh, bl, waits=ix["mem"],
                         wdst=[Q.last["tensor"]])
            branch(btoks, 2, lambda c, t: gm[c][:, t, :])
            filler(999)
            pe_taps(999)
            after_unit[0] = lambda: None
            tcv = [conv_done[0], Q.last["vector"]]

            for k0 in range(4):
                for t in range(T):
                    tp = pe(lambda e: e.matmul(PB[6 + t][:, k0 * P:(k0 + 1) * P], yc[:, k0, t * P:(t + 1) * P],
                                               ident[:, :], start=False, stop=(k0 == 3)), tcv)
            for t in range(T):
                s6, s2 = st[:, 20 + 8 * t:26 + 8 * t], st[:, 40 + 2 * t:42 + 2 * t]
                dve(lambda e: e.bn_stats(s6, PB[6 + t]), tp)
                dve(lambda e: e.bn_aggr(s2, s6))
                dve(lambda e: e.tensor_copy(st[:, 50 + t:51 + t], s2[:, 1:2]))
            rstd(st[:, 52:54], st[:, 50:52], 1)
            for t in range(T):
                tk = dve(lambda e: e.tensor_scalar(om[:, t, :], PB[6 + t], st[:, 40 + 2 * t:41 + 2 * t],
                                                   st[:, 52 + t:53 + t], ALU.subtract, ALU.mult),
                         Q.last["tensor"])
                free[6 + t] = [tk]
            btoks = to_T(lambda t, k: om[:, t, k * P:(k + 1) * P], 4, bh, bl, scale=lambda k: col("ln_g_2", k),
                         bias=lambda k: col("ln_b_2", k), func=ACT.Silu, waits=[tk], wdst=[Q.last["tensor"], tk])
            tk = branch(btoks, 1, lambda c, t: gc[:, c, t, :])
            toks = to_T(lambda t, k: ga[:, k // 4, t, (k % 4) * P:(k % 4 + 1) * P], KD, hh, hl,
                        waits=[tk], wdst=[Q.last["tensor"]])
            tok = linear(("wo",), KD, lh, ll, toks, YB)
            x_tok[:] = []
            for t in range(T):
                tk = dve(lambda e: e.tensor_tensor(x[:, t, :], x[:, t, :], ypsum2(t), ALU.add), tok)
                free[YB[t][0]] = free[YB[t][1]] = [tk]
                x_tok.append(tk)

            at[0] = XN_END
            hf = arena(KD, S)
            wr = arena(KD, 36)
            rbias = arena(36)
            tw = [load(wr[:, :, 0:4], I["w_rg_2"][0].rearrange("(k p) n -> p k n", p=P), x_tok),
                  load(wr[:, :, 4:36], I["w_re_2"][0].rearrange("(k p) n -> p k n", p=P), x_tok),
                  load(rbias[:, 0:4], I["b_rg_2"].to_broadcast([P, 4]), x_tok),
                  load(rbias[:, 4:36], I["b_re_2"].to_broadcast([P, 32]), x_tok)]
            tie = arena(8)
            tw.append(load(tie, I["tie_c"].to_broadcast([P, 8]), x_tok))
            lg = arena(T, 36)
            sm_ = arena(T, 128)
            tri = arena(2, P)
            iota = arena(P)
            tw += [load(tri, I["tri_c"].rearrange("p (a b) -> p a b", b=P), x_tok),
                   load(iota, I["iota_c"].to_broadcast([P, P]), x_tok)]
            sel = [arena(T, P) for _ in range(2)]
            selT = [arena(264) for _ in range(2)]
            ysb = arena(D)
            xo = arena(T, D)
            gx = xn
            tk = prenorm(x_tok, gain=grow, tg=t_gr)
            hft = []
            for k0 in range(0, KD, 2):
                b = RB[(k0 // 2) % 4]
                for k in range(2):
                    for t in range(T):
                        tp = pe(lambda e: e.transpose(PB[b][:, k * S + t * P:k * S + (t + 1) * P],
                                                      rows_xn(t, k0 + k), ident[:, :]), tk, free[b])
                dst, ps = hf[:, k0:k0 + 2, :], PB[b].rearrange("p (k n) -> p k n", n=S)
                if k0 % 4:
                    tf = dve(lambda e: e.tensor_copy(dst, ps), tp)
                else:
                    tf = act(lambda e: e.activation(dst, ps, ACT.Copy), tp)
                free[b] = [tf]
                hft += [tf, tf]
            for t in range(T):
                for k in range(KD):
                    tp = pe(lambda e: e.matmul(PB[2][:, t * 36:t * 36 + 36], hf[:, k, t * P:(t + 1) * P],
                                               wr[:, k, :], start=(k == 0), stop=(k == KD - 1)),
                            hft[k], tw, free[2])

            def wide(v, n):
                return v.unsqueeze(2).to_broadcast([P, T, n])

            def first_of(dst, v, mx, n, tmp):
                dve(lambda e: e.tensor_tensor(dst, v, wide(mx, n), ALU.is_equal))
                dve(lambda e: e.tensor_tensor(dst, dst, tie[:, 8 - n:8].unsqueeze(1).to_broadcast([P, T, n]), ALU.mult))
                dve(lambda e: e.tensor_reduce(tmp, dst, AX_X, ALU.max))
                return dve(lambda e: e.tensor_tensor(dst, dst, wide(tmp, n), ALU.is_equal))

            tk = dve(lambda e: e.tensor_tensor(lg, PB[2][:, 0:72].rearrange("p (t n) -> p t n", n=36),
                                               rbias.unsqueeze(1).to_broadcast([P, T, 36]), ALU.add), tp)
            free[2] = [tk]
            gl = lg[:, :, 0:4]
            one_ = lambda i: sm_[:, :, i]
            gmx, gs, tmp, dv, ez, w1, w2, rk = (one_(i) for i in (0, 1, 2, 3, 12, 13, 14, 15))
            oh, ge = sm_[:, :, 4:8], sm_[:, :, 8:12]
            ein, o1, o2, e2, v8 = (sm_[:, :, i:i + 8] for i in (16, 24, 32, 40, 48))
            pe_ = sm_[:, :, 64:96]
            dve(lambda e: e.tensor_reduce(gmx, gl, AX_X, ALU.max))
            t_oh = first_of(oh, gl, gmx, 4, tmp)
            cnt = PB[3][:, 0:12]
            for t in range(T):
                pe(lambda e: e.matmul(cnt[:, 4 * t:4 * t + 4], tri[:, 0, :], oh[:, t, :], start=True, stop=(t == 0)),
                   t_oh, tw, free[3])
            pe(lambda e: e.matmul(cnt[:, 4:8], tri[:, 1, :], oh[:, 0, :], start=False, stop=True))
            for t in range(T):
                tp = pe(lambda e: e.matmul(cnt[:, 8:12], tri[:, 1, :], oh[:, t, :], start=(t == 0), stop=(t == 1)))
            tn = dve(lambda e: e.tensor_tensor(ge, gl, wide(gmx, 4), ALU.subtract))
            t_ge = act(lambda e: e.activation(ge, ge, ACT.Exp), tn)
            p4 = pe_.rearrange("p t (g e) -> p t g e", e=8)
            for t in range(T):
                dve(lambda e: e.tensor_tensor(p4[:, t, :, :], lg[:, t, 4:36].rearrange("p (g e) -> p g e", e=8),
                                              oh[:, t, :].unsqueeze(2).to_broadcast([P, 4, 8]), ALU.mult))
            dve(lambda e: e.tensor_reduce(ein, pe_.rearrange("p t (g e) -> p t e g", e=8), AX_X, ALU.add))
            c3 = cnt[:, 0:8].rearrange("p (t g) -> p t g", g=4)
            c4 = sm_[:, :, 56:60]
            dve(lambda e: e.tensor_tensor(c4, c3, oh, ALU.mult), tp)
            dve(lambda e: e.tensor_reduce(rk, c4, AX_X, ALU.add))
            dve(lambda e: e.tensor_reduce(sm_[:, 0, 60:61], cnt[:, 8:12], AX_X, ALU.max))
            t_flag = dve(lambda e: e.tensor_scalar(flag[:, 0:1], sm_[:, 0, 60:61], 128.5, None, ALU.is_gt))
            free[3] = [t_flag]

            half = lambda a, i: a[:, :, :].rearrange("p k n -> p (k n)")[:, i * D:(i + 1) * D].rearrange(
                "p (k n) -> p k n", n=P)
            GH, GL = [half(hh, i) for i in range(2)], [half(hl, i) for i in range(2)]
            done_up, done_y, sel_tok, gtok, ct_tok, back = {}, {}, {}, {}, {}, {}

            def build_sel(g):
                for t in range(T):
                    tk = dve(lambda e: e.tensor_scalar(sel[g % 2][:, t, :], iota, sm_[:, t, 15:16],
                                                       sm_[:, t, 4 + g:5 + g], ALU.is_equal, ALU.mult),
                             tw, gtok.get(("pe", g - 2)))
                sel_tok[g] = tk

            def build_back(g, b=7):
                for t in range(T):
                    pe(lambda e: e.transpose(PB[b][:, t * P:(t + 1) * P], sel[g % 2][:, t, :], ident[:, :]),
                       sel_tok[g], free[b])
                for t in range(T):
                    tp = pe(lambda e: e.matmul(PB[b][:, 256:264], sel[g % 2][:, t, :], comb[:, t, g * 8:g * 8 + 8],
                                               start=(t == 0), stop=(t == 1)), t_comb)
                ct_tok[g] = act(lambda e: e.activation(selT[g % 2], PB[b][:, 0:264], ACT.Copy), tp, back.get(g - 2),
                                done_w.get(g - 2))
                free[b] = [ct_tok[g]]

            def gather(g, q, b=7):
                for k in range(4 * q, 4 * q + 4):
                    for t in range(T):
                        tp = pe(lambda e: e.matmul(PB[b][:, (k % 4) * P:(k % 4 + 1) * P], gx[:, t, k * P:(k + 1) * P],
                                                   sel[g % 2][:, t, :], start=(t == 0), stop=(t == 1)),
                                sel_tok[g], free[b])
                gtok["pe", g] = tp
                ps = PB[b].rearrange("p (k n) -> p k n", n=P)
                H, L = GH[g % 2][:, 4 * q:4 * q + 4, :], GL[g % 2][:, 4 * q:4 * q + 4, :]
                th = act(lambda e: e.activation(H, ps, ACT.Copy), tp, done_up.get(g - 2))
                tl = dve(lambda e: e.tensor_tensor(L, ps, H.bitcast(F32), ALU.subtract), th)
                free[b] = [th, tl]
                gtok[g, q] = [th, tl]

            def take_y(g):
                bk = 2 * (g % 2)
                done_y["sb", g] = act(lambda e: e.activation(
                    ysb, PS[:, bk:bk + 2, :].rearrange("p a b -> p (a b)"), ACT.Copy), done_y[g], back.get(g - 1))
                free[bk] = free[bk + 1] = [done_y["sb", g]]

            def scatter(g, t, h, b=7):
                tp = pe(lambda e: e.matmul(PB[b], selT[g % 2][:, t * P:(t + 1) * P], ysb[:, h * 512:(h + 1) * 512],
                                           start=True, stop=True), done_y["sb", g], ct_tok[g], free[b])
                back[g] = tp
                o, r = xo[:, t, h * 512:(h + 1) * 512], (x if g == 0 else xo)[:, t, h * 512:(h + 1) * 512]
                free[b] = [dve(lambda e: e.tensor_tensor(o, r, PB[b], ALU.add), tp)]

            done_w = {}
            build_sel(0)
            gather(0, 0, 4)
            gather(0, 1, 5)

            for t in range(T):
                dve(lambda e: e.max(v8[:, t, :], ein[:, t, :]))
            first_of(o1, ein, v8[:, :, 0], 8, tmp)
            dve(lambda e: e.scalar_tensor_tensor(e2, o1, MARK, ein, ALU.mult, ALU.add))
            first_of(o2, e2, v8[:, :, 1], 8, tmp)
            tn = dve(lambda e: e.tensor_tensor(dv, v8[:, :, 1], v8[:, :, 0], ALU.subtract))
            ta = act(lambda e: e.activation(ez, dv, ACT.Exp), tn)
            dve(lambda e: e.tensor_reduce(gs, ge, AX_X, ALU.add), t_ge)
            dve(lambda e: e.reciprocal(gs, gs))
            dve(lambda e: e.tensor_scalar(w1, ez, 1.0, None, ALU.add), ta)
            dve(lambda e: e.reciprocal(w1, w1))
            dve(lambda e: e.tensor_tensor(w1, w1, gs, ALU.mult))
            dve(lambda e: e.tensor_tensor(w2, w1, ez, ALU.mult))
            dve(lambda e: e.tensor_tensor(o1, o1, wide(w1, 8), ALU.mult))
            dve(lambda e: e.tensor_tensor(o2, o2, wide(w2, 8), ALU.mult))
            dve(lambda e: e.tensor_tensor(o1, o1, o2, ALU.add))
            for t in range(T):
                t_comb = dve(lambda e: e.tensor_tensor(
                    comb[:, t, :].rearrange("p (g e) -> p g e", e=8), o1[:, t, :].unsqueeze(1).to_broadcast([P, 4, 8]),
                    oh[:, t, :].unsqueeze(2).to_broadcast([P, 4, 8]), ALU.mult))
            build_back(0)

            ugf, gtf, gtt, sgf, ugt = [[], []], [[], []], [[], []], [[], []], [[], []]
            upart = [ug[i][:, 0, :] for i in range(2)]

            def spread(b):
                i = b % 2
                for f in range(2):
                    tp = pe(lambda e: e.transpose(PB[6][:, f * P:(f + 1) * P], upart[i][:, f * P:(f + 1) * P],
                                                  ident[:, :]), ugt[i], free[6])
                ps = PB[6][:, 0:256].rearrange("p (a b) -> p a b", b=P)
                H, L = gT_h[i][:, :, 0:P], gT_l[i][:, :, 0:P]
                th = act(lambda e: e.activation(H, ps, ACT.Copy), tp, gtf[i])
                tl = dve(lambda e: e.tensor_tensor(L, ps, H.bitcast(F32), ALU.subtract), th)
                free[6] = [th, tl]
                ugf[i] = [tp]
                gtt[i] = [th, tl]

            def outp(b):
                i, g = b % 2, b // 8
                bk = 2 * (g % 2)
                tok = linear(("md", b), 2, lambda k, t: gT_h[i][:, k, 0:P], lambda k, t: gT_l[i][:, k, 0:P], gtt[i],
                             [[bk, bk + 1]], first=(b % 8 == 0), last=(b % 8 == 7), tiles=1)
                gtf[i] = [tok]
                if b % 8 == 7:
                    done_y[g] = tok
                    if g < 3:
                        put_off(0.1, lambda: take_y(g))
                        for t in range(T):
                            for h in range(2):
                                put_off(0.7, lambda t=t, h=h: scatter(g, t, h))

            rate[0] = 0.3
            for b in range(32):
                i, g = b % 2, b // 8
                if b % 8 == 0:
                    flush()
                if b % 8 == 2 and g < 3:
                    put_off(0.4, lambda g=g: build_sel(g + 1))
                    put_off(0.1, lambda g=g: build_back(g + 1))
                    for q in range(2):
                        put_off(0.6, lambda g=g, q=q: gather(g + 1, q))
                gl_ = [gtok[g, k // 4] for k in range(KD)]
                tok = linear(("mu", b), KD, lambda k, t: GH[g % 2][:, k, :], lambda k, t: GL[g % 2][:, k, :], gl_,
                             [[AB[i]]], mid=(lambda: spread(b - 1)) if b else None, tiles=1)
                done_up[g] = tok
                ta = act(lambda e: e.activation(sg[:, i, :], PB[AB[i]][:, 0:256], ACT.Silu), tok, sgf[i])
                td = dve(lambda e: e.scalar_tensor_tensor(upart[i], sg[:, i, :], selT[g % 2][:, 256 + b % 8:257 + b % 8],
                                                          PB[AB[i]][:, 256:512], ALU.mult, ALU.mult),
                         ta, ugf[i], ct_tok[g])
                done_w[g] = td
                free[AB[i]] = [ta, td]
                sgf[i] = [td]
                ugt[i] = [td]
                if b:
                    outp(b - 1)
            spread(31)
            outp(31)
            flush()
            take_y(3)
            outs = []
            for t in range(T):
                for h in range(2):
                    scatter(3, t, h, (7, 4, 5, 6)[2 * t + h])
                outs.append(load(out_ap[0, t * P:(t + 1) * P, :], xo[:, t, :], Q.last["vector"], q="sync"))
            if Q.active in (None, "sync"):
                Q.wait(outs)

            def dense():
                barrier = [Q.last[n] for n in ("tensor", "vector", "scalar")]
                if Q.active != "gpsimd":
                    Q.wait(barrier)
                limit[0] = len(chunks)
                pump()
                rate[0] = 1.5
                for i in range(8):
                    free[i] = []
                ff.update(ug=[[], []], gt=[[], []], sg=[])
                th = act(lambda e: e.activation(hh[:, :, :], hf, ACT.Copy))
                tl = dve(lambda e: e.tensor_tensor(hl[:, :, :], hf, hh[:, :, :].bitcast(F32), ALU.subtract), th)
                tok = ffn_like(32, lambda b: ("mu", b), lambda b: ("md", b), [th, tl], lambda b: None, combine=t_comb)
                last_out = []
                for t in range(T):
                    for h in range(2):
                        xs = x[:, t, h * 512:(h + 1) * 512]
                        tk = dve(lambda e, xs=xs, t=t, h=h: e.tensor_tensor(xs, xs, ypsum(t, h), ALU.add), tok)
                    last_out.append(load(out_ap[0, t * P:(t + 1) * P, :], x[:, t, :], tk, q="sync"))
                if Q.active in (None, "sync"):
                    Q.wait(last_out)

            if Q.active is None:
                Q.wait([t_flag])
                dense()
            elif Q.active != "gpsimd":
                Q.wait([t_flag])
                over = Q.eng.value_load(flag[0:1, 0:1], min_val=0, max_val=1)
                with Q.eng.If(over == 1):
                    dense()
            else:
                dense()
            assert cpos[0] == len(chunks), (cpos, len(chunks))

        flow()
        Q.counted()
        block = ctx.enter_context(nc.Block())

        def emit(name):
            def body(eng):
                Q.begin(name, eng)
                flow()
            return body

        block.tensor(emit("tensor"))
        block.vector(emit("vector"))
        block.scalar(emit("scalar"))
        block.gpsimd(emit("gpsimd"))
        block.sync(emit("sync"))


_INS = ["x", "c", "ada_w", "ada_b", "norm_g", "ffn_w_in", "ffn_w_out", "pool_w", "pool_b", "pool_scale",
        "mla_w_in", "mla_q_norm", "mla_kv_norm", "mla_w_uq", "mla_w_uk", "mla_w_uv", "mla_w_o", "mem_2",
        "g_mix_2", "w_in_2", "b_gate_2", "g_qa_2", "g_ka_2", "g_idx_k_2", "conv_w_2", "conv_b_2", "ln_g_2",
        "ln_b_2", "g_mem_2", "w_mem_kv_2", "g_qm_2", "g_km_2", "w_br_a_2", "w_br_b_2", "w_br_m_2", "w_o_2",
        "g_ffn_2", "w_rg_2", "b_rg_2", "w_re_2", "b_re_2", "w_up_2", "w_down_2"]


def _constants():
    f = np.float32
    out = {"ident_c": np.eye(P, dtype=f)}
    out["tri_c"] = np.concatenate([np.triu(np.ones((P, P), f), 1), np.ones((P, P), f)], 1)
    out["iota_c"] = np.arange(P, dtype=f)[None, :]
    out["sum4_c"] = np.tile((np.arange(P) % 32 == 0).astype(f)[:, None], (1, P))
    t = np.arange(S)
    rc = []
    for w in (2, 4, 8, 16):
        n = np.clip(t + w // 2, 0, S) - np.clip(t - w // 2, 0, S)
        rc.append(1.0 / n)
    out["rc_c"] = np.asarray(rc, dtype=f)
    for half, name in ((16, "rope16_c"), (32, "rope32_c")):
        inv = (10000.0 ** (-(np.arange(half, dtype=f) / f(half)))).astype(f)
        ang = (t.astype(f)[:, None] * inv[None, :]).astype(f).astype(np.float64)
        cs = np.stack([np.cos(ang), np.sin(ang)])
        out[name] = np.ascontiguousarray(cs.reshape(2, T, P, half).transpose(2, 0, 1, 3).reshape(P, -1)).astype(f)
    ca = (t[None, :] <= t[:, None]).astype(f)
    ca = np.where(ca > 0, f(3e38), f(NEG))
    out["cap_c"] = np.ascontiguousarray(ca.reshape(T, P, S).transpose(1, 0, 2).reshape(P, -1))
    out["tie_c"] = np.arange(8, 0, -1).astype(f)[None, :]
    return out


def kernel(**inputs):
    import numpy as _np
    import concourse.bacc as _bacc
    from concourse import mybir as _mybir
    from concourse.bass_utils import run_bass_kernel_spmd as _run

    nc = _bacc.Bacc("TRN2", target_bir_lowering=False, num_devices=1)
    arrays, aps = {}, {}
    named = {n: _np.ascontiguousarray(inputs[n]) for n in _INS}
    named.update(_constants())
    for name, a in named.items():
        arrays[f"in_{name}"] = a
        aps[name] = nc.dram_tensor(f"in_{name}", a.shape, _mybir.dt.from_np(a.dtype), kind="ExternalInput").ap()
    out = nc.dram_tensor("out_0", (1, S, D), F32, kind="ExternalOutput").ap()
    build(nc, aps, out)
    r = _run(nc, [arrays], core_ids=[0])
    return r.results[0]["out_0"]
```
